# Optimizing a Trainium2 kernel written in Bass

```python
import math
import jax, jax.numpy as jnp
from jax import lax
import numpy as np

D_MODEL = 1024
BATCH = 1
SEQ = 256
DEPTH = 1

CHUNK = 64
Q_BLOCK = 128
SSM_WIDTH = D_MODEL // 2
SSM_GROUP = 16
SSM_GROUPS = SSM_WIDTH // SSM_GROUP
SSM_STATE = 64
ATT_HEADS = 4
ATT_SUB_DIM = 64
ATT_V_DIM = 2 * ATT_SUB_DIM
ATT_QK_WIDTH = ATT_HEADS * 2 * ATT_SUB_DIM
ATT_V_WIDTH = ATT_HEADS * ATT_V_DIM
IN_WIDTH = SSM_WIDTH + 2 * ATT_QK_WIDTH + ATT_V_WIDTH + 2 * D_MODEL
N_EXPERTS = 32
TOP_K = 4
D_EXPERT = D_MODEL
SWIGLU_ALPHA = 1.702
SWIGLU_LIMIT = 7.0
MOE_BLOCK = 256
RMS_EPS = 1e-6

kernel_name = "hybrid_s5_diffattn_moe_block"

def rms_norm(x, g):
    xf = x.astype(jnp.float32)
    y = xf * lax.rsqrt(jnp.mean(xf * xf, axis=-1, keepdims=True) + RMS_EPS)
    return (y * g.astype(jnp.float32)).astype(x.dtype)

def _complex_linear_combine(left, right):
    a1r, a1i, b1r, b1i = left
    a2r, a2i, b2r, b2i = right
    ar = a2r * a1r - a2i * a1i
    ai = a2r * a1i + a2i * a1r
    br = a2r * b1r - a2i * b1i + b2r
    bi = a2r * b1i + a2i * b1r + b2i
    return (ar, ai, br, bi)

def s5_branch(u, a_re, a_im, log_dt, b_re, b_im, c_re, c_im, d_skip, w_glu, b_glu):
    f32 = jnp.float32
    bsz, seq, _ = u.shape
    ug = u.astype(f32).reshape(bsz, seq, SSM_GROUPS, SSM_GROUP)
    dt = jnp.exp(log_dt.astype(f32))[:, None]
    lr = a_re.astype(f32)
    li = a_im.astype(f32)
    mag = jnp.exp(lr * dt)
    abar_r = mag * jnp.cos(li * dt)
    abar_i = mag * jnp.sin(li * dt)
    den = lr * lr + li * li
    nr = abar_r - 1.0
    ni = abar_i
    coef_r = (nr * lr + ni * li) / den
    coef_i = (ni * lr - nr * li) / den
    br_ = b_re.astype(f32)
    bi_ = b_im.astype(f32)
    bbar_r = coef_r[..., None] * br_ - coef_i[..., None] * bi_
    bbar_i = coef_r[..., None] * bi_ + coef_i[..., None] * br_
    inp_r = jnp.einsum('blgh,gph->blgp', ug, bbar_r)
    inp_i = jnp.einsum('blgh,gph->blgp', ug, bbar_i)
    a_r = jnp.broadcast_to(abar_r, inp_r.shape)
    a_i = jnp.broadcast_to(abar_i, inp_i.shape)
    _, _, st_r, st_i = lax.associative_scan(
        _complex_linear_combine, (a_r, a_i, inp_r, inp_i), axis=1)
    y = (jnp.einsum('blgp,ghp->blgh', st_r, c_re.astype(f32))
         - jnp.einsum('blgp,ghp->blgh', st_i, c_im.astype(f32))
         + d_skip.astype(f32).reshape(SSM_GROUPS, SSM_GROUP) * ug)
    y = jax.nn.gelu(y.reshape(bsz, seq, SSM_WIDTH))
    y = y * jax.nn.sigmoid(y @ w_glu.astype(f32) + b_glu.astype(f32))
    return y.astype(u.dtype)

def diff_attention(q, k, v, q_g, k_g, lq1, lk1, lq2, lk2, subln_g, lambda_init):
    f32 = jnp.float32
    bsz, seq, _ = q.shape
    q = rms_norm(q.reshape(bsz, seq, ATT_HEADS, 2, ATT_SUB_DIM), q_g)
    k = rms_norm(k.reshape(bsz, seq, ATT_HEADS, 2, ATT_SUB_DIM), k_g)
    v = v.reshape(bsz, seq, ATT_HEADS, ATT_V_DIM)
    lam = (jnp.exp(jnp.sum(lq1.astype(f32) * lk1.astype(f32)))
           - jnp.exp(jnp.sum(lq2.astype(f32) * lk2.astype(f32))) + lambda_init)
    n_blocks = seq // Q_BLOCK
    q_blocks = q.reshape(bsz, n_blocks, Q_BLOCK, ATT_HEADS, 2, ATT_SUB_DIM).transpose(1, 0, 2, 3, 4, 5)
    key_chunk = jnp.arange(seq) // CHUNK
    scale = ATT_SUB_DIM ** -0.5

    def one_block(args):
        qblk, bi = args
        qpos = bi * Q_BLOCK + jnp.arange(Q_BLOCK)
        allowed = key_chunk[None, :] <= (qpos // CHUNK)[:, None]
        s = jnp.einsum('bqhtd,bkhtd->bhtqk', qblk, k).astype(f32) * scale
        p = jax.nn.softmax(jnp.where(allowed, s, -jnp.inf), axis=-1)
        w = p[:, :, 0] - lam * p[:, :, 1]
        return jnp.einsum('bhqk,bkhe->bqhe', w.astype(v.dtype), v)

    o = lax.map(one_block, (q_blocks, jnp.arange(n_blocks)))
    o = o.transpose(1, 0, 2, 3, 4).reshape(bsz, seq, ATT_HEADS, ATT_V_DIM)
    o = rms_norm(o, subln_g) * (1.0 - lambda_init)
    return o.reshape(bsz, seq, ATT_V_WIDTH)

def moe_ffn(hn, w_router, b_router, w_up, b_up, w_down, b_down):
    bsz, seq, dm = hn.shape
    xf = hn.reshape(-1, dm)
    n_tok = xf.shape[0]
    logits = (xf @ w_router + b_router).astype(jnp.float32)
    top_v, top_i = lax.top_k(logits, TOP_K)
    top_w = jax.nn.softmax(top_v, axis=-1)
    m = n_tok * TOP_K
    flat_e = top_i.reshape(-1)
    flat_tok = jnp.repeat(jnp.arange(n_tok, dtype=jnp.int32), TOP_K)
    flat_w = top_w.reshape(-1)
    order = jnp.argsort(flat_e)
    sorted_e = flat_e[order]
    counts = jnp.bincount(flat_e, length=N_EXPERTS)
    padded = ((counts + MOE_BLOCK - 1) // MOE_BLOCK) * MOE_BLOCK
    pad_end = jnp.cumsum(padded)
    pad_start = pad_end - padded
    start = jnp.cumsum(counts) - counts
    dest = pad_start[sorted_e] + jnp.arange(m) - start[sorted_e]
    n_rows = ((m + MOE_BLOCK - 1) // MOE_BLOCK) * MOE_BLOCK + N_EXPERTS * MOE_BLOCK
    n_blocks = n_rows // MOE_BLOCK
    row_tok = jnp.zeros((n_rows,), jnp.int32).at[dest].set(flat_tok[order])
    row_w = jnp.zeros((n_rows,), jnp.float32).at[dest].set(flat_w[order])
    block_e = jnp.minimum(
        jnp.searchsorted(pad_end, jnp.arange(n_blocks) * MOE_BLOCK, side='right'), N_EXPERTS - 1)
    xs = xf[row_tok].reshape(n_blocks, MOE_BLOCK, dm)

    def expert_block(args):
        xb, e = args
        hup = xb @ w_up[e] + b_up[e]
        glu = jnp.minimum(hup[:, 0::2], SWIGLU_LIMIT)
        lin = jnp.clip(hup[:, 1::2], -SWIGLU_LIMIT, SWIGLU_LIMIT)
        act = glu * jax.nn.sigmoid(SWIGLU_ALPHA * glu) * (lin + 1.0)
        return act @ w_down[e] + b_down[e]

    ys = lax.map(expert_block, (xs, block_e)).reshape(n_rows, dm)
    out = jnp.zeros_like(xf).at[row_tok].add(ys * row_w[:, None].astype(ys.dtype))
    return out.reshape(bsz, seq, dm)

def setup_inputs(seed: int = 0) -> dict:
    key = jax.random.key(seed)
    ks = jax.random.split(key, 32)
    f32 = jnp.float32

    def nrm(k, shape, scale):
        return jax.random.normal(k, shape, f32) * scale

    G, P, H, S = SSM_GROUPS, SSM_STATE, SSM_GROUP, SSM_WIDTH
    a_im_init = jnp.pi * jnp.arange(P, dtype=f32)
    return {
        "x": nrm(ks[0], (BATCH, SEQ, D_MODEL), 1.0),
        "norm1_g": 1.0 + nrm(ks[1], (DEPTH, D_MODEL), 0.02),
        "w_in": nrm(ks[2], (DEPTH, D_MODEL, IN_WIDTH), D_MODEL ** -0.5),
        "b_gate": nrm(ks[3], (DEPTH, 2 * D_MODEL), 0.01),
        "ssm_a_re": -0.5 + nrm(ks[4], (DEPTH, G, P), 0.01),
        "ssm_a_im": a_im_init + nrm(ks[5], (DEPTH, G, P), 0.01),
        "ssm_log_dt": jax.random.uniform(ks[6], (DEPTH, G), f32, math.log(1e-3), math.log(1e-1)),
        "ssm_b_re": nrm(ks[7], (DEPTH, G, P, H), (2 * H) ** -0.5),
        "ssm_b_im": nrm(ks[8], (DEPTH, G, P, H), (2 * H) ** -0.5),
        "ssm_c_re": nrm(ks[9], (DEPTH, G, H, P), (2 * P) ** -0.5),
        "ssm_c_im": nrm(ks[10], (DEPTH, G, H, P), (2 * P) ** -0.5),
        "ssm_d": nrm(ks[11], (DEPTH, S), 1.0),
        "ssm_w_glu": nrm(ks[12], (DEPTH, S, S), S ** -0.5),
        "ssm_b_glu": nrm(ks[13], (DEPTH, S), 0.01),
        "q_norm_g": 1.0 + nrm(ks[14], (DEPTH, ATT_SUB_DIM), 0.02),
        "k_norm_g": 1.0 + nrm(ks[15], (DEPTH, ATT_SUB_DIM), 0.02),
        "lambda_q1": nrm(ks[16], (DEPTH, ATT_SUB_DIM), 0.1),
        "lambda_k1": nrm(ks[17], (DEPTH, ATT_SUB_DIM), 0.1),
        "lambda_q2": nrm(ks[18], (DEPTH, ATT_SUB_DIM), 0.1),
        "lambda_k2": nrm(ks[19], (DEPTH, ATT_SUB_DIM), 0.1),
        "subln_g": 1.0 + nrm(ks[20], (DEPTH, ATT_V_DIM), 0.02),
        "w_proj_ssm": nrm(ks[21], (DEPTH, S, D_MODEL), S ** -0.5),
        "w_proj_att": nrm(ks[22], (DEPTH, ATT_V_WIDTH, D_MODEL), ATT_V_WIDTH ** -0.5),
        "w_out": nrm(ks[23], (DEPTH, D_MODEL, D_MODEL), D_MODEL ** -0.5),
        "norm2_g": 1.0 + nrm(ks[24], (DEPTH, D_MODEL), 0.02),
        "w_router": nrm(ks[25], (DEPTH, D_MODEL, N_EXPERTS), D_MODEL ** -0.5),
        "b_router": nrm(ks[26], (DEPTH, N_EXPERTS), 0.01),
        "w_up": nrm(ks[27], (DEPTH, N_EXPERTS, D_MODEL, 2 * D_EXPERT), D_MODEL ** -0.5),
        "b_up": nrm(ks[28], (DEPTH, N_EXPERTS, 2 * D_EXPERT), 0.01),
        "w_down": nrm(ks[29], (DEPTH, N_EXPERTS, D_EXPERT, D_MODEL), D_EXPERT ** -0.5),
        "b_down": nrm(ks[30], (DEPTH, N_EXPERTS, D_MODEL), 0.01),
    }

def reference(x, norm1_g, w_in, b_gate, ssm_a_re, ssm_a_im, ssm_log_dt, ssm_b_re, ssm_b_im,
              ssm_c_re, ssm_c_im, ssm_d, ssm_w_glu, ssm_b_glu, q_norm_g, k_norm_g,
              lambda_q1, lambda_k1, lambda_q2, lambda_k2, subln_g, w_proj_ssm, w_proj_att,
              w_out, norm2_g, w_router, b_router, w_up, b_up, w_down, b_down):
    split_at = [SSM_WIDTH,
                SSM_WIDTH + ATT_QK_WIDTH,
                SSM_WIDTH + 2 * ATT_QK_WIDTH,
                SSM_WIDTH + 2 * ATT_QK_WIDTH + ATT_V_WIDTH,
                SSM_WIDTH + 2 * ATT_QK_WIDTH + ATT_V_WIDTH + D_MODEL]
    h = x
    for l in range(DEPTH):
        lambda_init = 0.8 - 0.6 * math.exp(-0.3 * l)
        xn = rms_norm(h, norm1_g[l])
        z = xn @ w_in[l]
        u, q, k, v, g_ssm, g_att = jnp.split(z, split_at, axis=-1)
        y_ssm = s5_branch(u, ssm_a_re[l], ssm_a_im[l], ssm_log_dt[l], ssm_b_re[l], ssm_b_im[l],
                          ssm_c_re[l], ssm_c_im[l], ssm_d[l], ssm_w_glu[l], ssm_b_glu[l])
        y_att = diff_attention(q, k, v, q_norm_g[l], k_norm_g[l], lambda_q1[l], lambda_k1[l],
                               lambda_q2[l], lambda_k2[l], subln_g[l], lambda_init)
        gate_ssm = jax.nn.sigmoid(g_ssm + b_gate[l, :D_MODEL])
        gate_att = jax.nn.sigmoid(g_att + b_gate[l, D_MODEL:])
        mixed = gate_ssm * (y_ssm @ w_proj_ssm[l]) + gate_att * (y_att @ w_proj_att[l])
        h = h + mixed @ w_out[l]
        hn = rms_norm(h, norm2_g[l])
        h = h + moe_ffn(hn, w_router[l], b_router[l], w_up[l], b_up[l], w_down[l], b_down[l])
    return h


_drawn_inputs = setup_inputs


def setup_inputs(seed=0):
    import zlib

    import numpy as np

    out = dict(_drawn_inputs(seed))
    spreads = {}
    factors = {'b_gate': 8.0,
     'ssm_a_re': 64.0,
     'ssm_c_re': 3.117,
     'ssm_b_glu': 23.535,
     'k_norm_g': 3.022,
     'b_up': 8.0,
     'b_down': 8.0,
     'ssm_b_re': 2.988,
     'ssm_b_im': 3.91,
     'ssm_c_im': 8.0}
    for name, (base, spread) in spreads.items():
        noise = np.random.default_rng([zlib.crc32(name.encode()), seed]).standard_normal(out[name].shape)
        drawn = base * np.exp(spread * noise) if base else spread * noise
        out[name] = __import__('jax').numpy.asarray(drawn.astype(out[name].dtype))
    for name, factor in factors.items():
        out[name] = (out[name] * factor).astype(out[name].dtype)
    return out
```

```python
import math
from contextlib import ExitStack

import concourse.bass as bass
from concourse import mybir

ALU = mybir.AluOpType
ACT = mybir.ActivationFunctionType
F32 = mybir.dt.float32
I32 = mybir.dt.int32
U32 = mybir.dt.uint32
AX = mybir.AxisListType.X

P = 128
D = 1024
TOK = 256
TT = TOK // P
KT = D // P
G, PS, H = 32, 64, 16
GG = G // 2
S = G * H
L = P // H
NC = TOK // L
HEADS, SUB = 4, 64
AW = HEADS * 2 * SUB
WIN = S + 3 * AW + 2 * D
CHUNK = 64
E, TOPK = 32, 4
SLOTS = 64
EXTRA = TOK * TOPK // (SLOTS + 1)
TABLE = E + EXTRA + 1
ALPHA, LIMIT, EPS = 1.702, 7.0, 1e-6
LAMBDA_INIT = 0.8 - 0.6 * math.exp(0.0)
BIG = 1e30
ROUND = 1.5 * 2.0 ** 23
TWO_PI_1 = 6.28125
TWO_PI_2 = 0.0019350051879882812
TWO_PI_3 = 2 * math.pi - TWO_PI_1 - TWO_PI_2
PIECE = 256
RING = 3

SEMS = """ident x_in a_in c_in b_in vec_in d_in lam_in dve_step pool_step x_sq x_var x_rs xn xT_ps xT dt
 aT_in aT_ps cT_ps trig sincos win_t cp_ready u_sb u_out u_back q_sq v_sb qk_var qk_rs qk_tm
 wT_ps wT_sb kk_ps kk_sb kk_d m_zero m_in cp_zero U_ps U_sb st_ps st_sb sT_ps s_prev y_ps y_sb
 yT_ps gelu_sq gelu_w gelu_s yT glu_ps glu_s yg  gate_sb qkT_ps qkT kz_fill score smax
 prob lam_e lam_n wt w_ps w_sb oT_ps o_sq o_ms o_var o_rs oT ps_ssm ps_att mixed h h_sq
 h_var h_rs hn hT_ps hT lg_ps lg_sb lgt_ps top_e top_x gw rk_ps gT_ps gT bd_in bias_ps table_out
 table_in table bup_z sel xg_ps xg swt_ps swT glu_sb sig act aT2_ps aT2 ysb scat up_used dn_used
 bup_used dsel fin fin_out wr_in g2_in loop_z u_turn wg bb_rep gated""".split()


def mixer_and_experts(nc, a, out):
    ctx = ExitStack()
    with ctx:
        KB = 256
        arena = ctx.enter_context(nc.sbuf_tensor("arena", [P, 207 * KB], F32))
        u_dram = nc.dram_tensor("u_scratch", (TOK, S), F32, kind="Internal").ap()
        table_dram = nc.dram_tensor("table_scratch", (P, 3), I32, kind="Internal").ap()

        def at(kb, *dims):
            n = 1
            for d in dims:
                n *= d
            o = int(kb * KB)
            v = arena[:, o:o + n]
            names = "abcd"[:len(dims)]
            if len(dims) > 1:
                v = v.rearrange(f"p ({' '.join(names)}) -> p {' '.join(names)}",
                                **{k: d for k, d in zip(names, dims)})
            return v

        up_w = at(0, KT, 2 * D)
        dn_w = at(64, KT, D)
        CW = 9 * H
        CR = at(0, GG, 2, CW)
        CI = at(18, GG, 2, CW)
        WR = at(36, GG, P)
        WI = at(44, GG, P)
        KK = at(36, G, P)
        WIN_M = at(52, GG, 2, P)
        MM = at(68, G, P)
        tA = at(68, GG, 9, H)
        tB = at(172, GG, 9, H)
        U = at(84, 8, 4, NC)
        uc = at(88, L, P)
        uc2 = at(92, 8, L, H)
        Y_sb = at(88, L, 4, 2, H)
        bbR, bbI = at(144, GG, L, H), at(172, GG, L, H)
        wg = at(112, 4, 4, P)
        u_tm = at(92, TT, S)
        S_sb = at(92, 4, 2, P)
        hx = at(96, TT, D)
        hn = at(104, TT, D)
        Rr, Ri = at(104, GG, NC), at(106, GG, NC)
        magz = at(108, GG, NC)
        bbr, bbi = at(110, GG, H), at(111, GG, H)
        oT = at(104, HEADS, TOK)
        o2 = at(108, HEADS, TOK)
        xnT = at(112, KT, TOK)
        stream = [at(120 + 8 * i, 8, PIECE) for i in range(RING)]
        gates = at(144, 16, TOK)
        xn = at(144, TT, D)
        c_sb = at(152, 2, 4, 2, PS)
        br_raw, bi_raw = at(156, GG, H), at(157, GG, H)
        q_tm, k_tm = at(160, TT, AW), at(164, TT, AW)
        ge1, ge2 = at(160, L, 4, NC), at(164, L, 4, NC)
        o_rs = at(164, HEADS, TOK)
        v_tm = at(168, TT, AW)
        qz = at(172, 2, HEADS, TOK)
        kz = at(180, 2, HEADS, TOK)
        mixT = at(172, KT, TOK)
        mtmp = at(180, 2, 2 * TOK)
        prob = at(188, 2, 2 * TOK)
        wmix = at(192, 2, TOK)
        wTs = at(194, 2, 2, P)
        cTr, cTi = at(188, GG, H), at(189, GG, H)
        Pr, Pi = at(190, GG, 9), at(190.75, GG, 9)
        Vr, Vi = at(191.5, GG, L), at(192, GG, L)
        sc1, sc2, sc3, sc4 = [at(184 + i, GG, H) for i in range(4)]
        It = at(180, 4, GG, NC)
        Spr, Spi = at(196, GG, NC), at(198, GG, NC)
        dB, dd = at(196, G, H), at(198, G, H)
        yT = at(196, 4, TOK)
        ident = at(200, P)
        ones = at(200.5, P)
        ltri = at(201, P)
        iota = at(201.5, 5 * SLOTS)
        tq = at(202.75, TOK)
        tk = at(203.75, TOK)
        e0 = at(204.75, SLOTS)
        hsel = at(205, H)
        small = at(205.0625, 496)

        def sm(o, *dims):
            n = 1
            for d in dims:
                n *= d
            v = small[:, o:o + n]
            names = "abc"[:len(dims)]
            if len(dims) > 1:
                v = v.rearrange(f"p ({' '.join(names)}) -> p {' '.join(names)}",
                                **{k: d for k, d in zip(names, dims)})
            return v

        g1 = sm(0, KT)
        bgate = sm(8, 16)
        bglu = sm(24, 4)
        xs = sm(28, TT)
        xr = sm(30, TT)
        iop = sm(32, 1)
        lamv = sm(33, 8)
        subg = sm(41, 1)
        qg = sm(42, 1)
        kg = sm(43, 1)
        dts = sm(44, 2)
        pa = sm(48, 4, GG)
        tr = sm(112, 6, GG)
        mg = sm(208, 2, GG)
        qv = sm(240, 2, TT, 8)
        smx = sm(272, 2, 2)
        nmx = sm(276, 2, 2)
        rsum = sm(280, 2, 2)
        rinv = sm(284, 2, 2)
        br_col = sm(288, 1)
        e8r, e8i = sm(290, GG), sm(306, GG)
        cfr, cfi = sm(322, GG), sm(338, GG)
        t16 = [sm(354 + 16 * i, GG) for i in range(6)]
        natA = at(158, 4, P)
        lamrow = at(198, 4, SUB)
        hT = at(112, KT, TOK)
        bup = at(120, 2 * D)
        bdn = at(128, D)
        xg = at(132, KT, SLOTS)
        act_s = at(134, 4 * P)
        glu_t = at(136, 4 * P)
        lin_t = at(138, 4 * P)
        sig_t = at(140, 4 * P)
        actT = at(142, 4, 2, SLOTS)
        y_s = at(144, 4 * P)
        selw = at(146, TT, P)
        swT0, swT1 = at(147, TT, P), at(148, TT, P)
        selg = at(149, TT, P)
        wr = at(150, KT, E)
        lgT = at(151, TOK)
        lg = at(152, TT, E)
        top_v = at(152.25, TT, 8)
        top_f = at(152.375, TT, 8)
        top_w = at(152.5, TT, 8)
        gw = at(153, TT, E)
        routed = at(153.25, TT, E)
        rank = at(153.5, TT, E)
        cnt = at(153.75, E)
        ovf = at(153.875, E)
        ovt = at(154, E)
        cum = at(154.125, E)
        before = at(154.25, E)
        tabf = at(154.375, 16)
        gwT = at(155, TOK)
        g2b = at(156, D)
        table_row = at(150, 3 * P).bitcast(I32)
        top_i = at(152.625, TT * 8).bitcast(U32).rearrange("p (t n) -> p t n", t=TT)
        table_i = at(152.75, 4).bitcast(I32)

        B = [ctx.enter_context(nc.psum_tensor(f"bank{i}", [P, 512], F32)) for i in range(8)]
        s = {n: ctx.enter_context(nc.semaphore(n)) for n in SEMS}
        slot_in = [ctx.enter_context(nc.semaphore(f"slot{i}_in")) for i in range(RING)]
        up_in = [ctx.enter_context(nc.semaphore(f"up{i}_in")) for i in range(KT)]
        dn_in = [ctx.enter_context(nc.semaphore(f"dn{i}_in")) for i in range(KT // 2)]
        piece_used = ctx.enter_context(nc.semaphore("piece_used"))
        bup_in = ctx.enter_context(nc.semaphore("bup_in"))

        def piece(i):
            slot = stream[i % RING]
            if i < 16:
                w = a["w_in"][0].rearrange("(k p) n -> p k n", p=P)
                return [(slot, w[:, :, i * PIECE:(i + 1) * PIECE])]
            if i == 16:
                v = slot.rearrange("p a b -> p (a b)").rearrange("p (q n) -> p q n", q=4)
                w = a["ssm_w_glu"][0]
                return [(v[32 * t:32 * t + 32], w[P * t:P * t + P].rearrange("(q r) n -> r q n", q=4))
                        for t in range(4)]
            if i < 19:
                v = slot.rearrange("p a b -> p (a b)").rearrange("p (q n) -> p q n", q=4)
                w = a["w_proj_ssm"][0][:, (i - 17) * 512:(i - 16) * 512]
                return [(v[32 * t:32 * t + 32], w[P * t:P * t + P].rearrange("(q r) n -> r q n", q=4))
                        for t in range(4)]
            if i < 21:
                v = slot.rearrange("p a b -> p (a b)").rearrange("p (q n) -> p q n", q=4)
                w = a["w_proj_att"][0].rearrange("(k p) n -> p k n", p=P)
                return [(v, w[:, :, (i - 19) * 512:(i - 18) * 512])]
            w = a["w_out"][0].rearrange("(k p) n -> p k n", p=P)
            return [(slot, w[:, :, (i - 21) * PIECE:(i - 20) * PIECE])]

        def pv(i):
            return stream[i % RING].rearrange("p a b -> p (a b)").rearrange("p (q n) -> p q n", q=4)

        w_up, w_dn, b_up = a["w_up"][0], a["w_down"][0], a["b_up"][0]
        pairs = [(gg, g2) for gg in range(GG) for g2 in range(2)]

        def probs(u, sub):
            return prob[:, u % 2, :].rearrange("p (s k) -> p s k", s=2)[:, sub, 0:P * (u % 2 + 1)]

        block = ctx.enter_context(nc.Block())


        @block.sync
        def _(sp):
            sp.dma_start(hx, a["x"][0].rearrange("(t p) n -> p t n", p=P)).then_inc(s["x_in"], 16)
            for src, o in ((a["ssm_a_re"], 0), (a["ssm_a_im"], 1)):
                sp.dma_start(natA[0:GG, o, :], src[0].rearrange("(g t) p -> g (t p)", t=2))\
                  .then_inc(s["a_in"], 16)
            sp.dma_start(dts[0:GG], a["ssm_log_dt"][0].rearrange("(g t) -> g t", t=2))\
              .then_inc(s["a_in"], 16)
            for i in range(25):
                if i >= RING:
                    sp.wait_ge(piece_used, i - RING + 1)
                for dst, src in piece(i):
                    sp.dma_start(dst, src).then_inc(slot_in[i % RING], 16)
                if i == 16:
                    sp.wait_ge(s["y_ps"], 1)
                    sp.wait_ge(s["yT_ps"], 2)
                if i >= 16:
                    k = i - 16
                    if k < KT:
                        sp.dma_start(up_w[:, k, :], w_up[0, P * k:P * k + P, :]).then_inc(up_in[k], 16)
                    if k >= 5:
                        j = k - 5
                        sp.dma_start(dn_w[:, 2 * j:2 * j + 2, :],
                                     w_dn[0, 2 * P * j:2 * P * (j + 1), :].rearrange("(k p) n -> p k n", p=P))\
                          .then_inc(dn_in[j], 16)
            sp.wait_ge(s["bup_z"], 1)
            sp.dma_start(bup[0:1, :], b_up[0:1, :]).then_inc(bup_in, 16)
            sp.wait_ge(s["table_in"], 16)
            blocks = sp.value_load(table_row[0:1, 2:3], min_val=E, max_val=E + EXTRA)
            with sp.Fori(1, blocks) as b:
                e = sp.value_load(table_row[0:1, bass.ds(3 * b, 1)], min_val=0, max_val=E - 1)
                sp.wait_ge(s["bup_used"], b)
                sp.dma_start(bup[0:1, :], b_up[bass.ds(e, 1), :]).then_inc(bup_in, 16)
                for k in range(KT):
                    sp.wait_ge(s["up_used"], KT * b - KT + k + 1)
                    sp.dma_start(up_w[:, k, :],
                                 w_up[bass.ds(e, 1), P * k:P * k + P, :].rearrange("o p n -> p (o n)"))\
                      .then_inc(up_in[k], 16)
                for j in range(KT // 2):
                    sp.wait_ge(s["dn_used"], 4 * b - 4 + j + 1)
                    sp.dma_start(dn_w[:, 2 * j:2 * j + 2, :],
                                 w_dn[bass.ds(e, 1), 2 * P * j:2 * P * (j + 1), :]
                                 .rearrange("o (k p) n -> p (o k) n", p=P)).then_inc(dn_in[j], 16)
            for t in range(TT):
                for n in range(2):
                    sp.wait_ge(s["fin"], 2 * t + n + 1)
                    sp.dma_start(out[0, P * t:P * t + P, 512 * n:512 * n + 512],
                                 hx[:, t, 512 * n:512 * n + 512]).then_inc(s["fin_out"], 16)
            sp.wait_ge(s["fin_out"], 64)

        @block.gpsimd
        def _(pool):
            for n, half in enumerate((a["ssm_c_re"], a["ssm_c_im"])):
                for dup in range(2):
                    pool.dma_start(c_sb[:, n, :, dup, :],
                                   half[0].rearrange("g h p -> (g h) p").rearrange("(i q) p -> q i p", q=P))\
                        .then_inc(s["c_in"], 16)
            for dst, src in ((br_raw, a["ssm_b_re"]), (bi_raw, a["ssm_b_im"])):
                pool.dma_start(dst, src[0].rearrange("(g t) p h -> (t p) g h", t=2)).then_inc(s["b_in"], 16)
            steps = [0]

            def link(ins):
                steps[0] += 1
                ins.then_inc(s["pool_step"], 1)
                pool.wait_ge(s["pool_step"], steps[0])

            pool.memset(ident, 0.0)
            pool.memset(ltri, 1.0)
            pool.memset(tq, 0.0)
            pool.memset(tk, 0.0)
            pool.memset(e0, 0.0)
            link(pool.memset(ones, 1.0))
            pool.affine_select(out=ident, in_=ident, compare_op=ALU.not_equal, fill=1.0, base=0,
                               pattern=[[-1, P]], channel_multiplier=1).then_inc(s["ident"], 1)
            link(pool.affine_select(out=ltri, in_=ltri, compare_op=ALU.is_gt, fill=0.0, base=0,
                                    pattern=[[1, P]], channel_multiplier=-1))
            for half in range(2):
                lo = 64 * half
                for row in range(2):
                    q0, k0 = P * row, P * row + CHUNK
                    pool.affine_select(out=tq[lo:lo + 64, q0:q0 + CHUNK], in_=tq[lo:lo + 64, q0:q0 + CHUNK],
                                       compare_op=ALU.not_equal, fill=1.0, base=-row,
                                       pattern=[[0, CHUNK]], channel_multiplier=1)
                    last = pool.affine_select(out=tk[lo:lo + 64, k0:k0 + CHUNK],
                                              in_=tk[lo:lo + 64, k0:k0 + CHUNK],
                                              compare_op=ALU.not_equal, fill=-BIG, base=-row,
                                              pattern=[[0, CHUNK]], channel_multiplier=1)
                link(last)
            link(pool.memset(e0[0:1, :], 1.0))
            pool.iota(iota, pattern=[[1, 5 * SLOTS]], base=0, channel_multiplier=0,
                      allow_small_or_imprecise_dtypes=True)
            link(pool.iota(iop, pattern=[[0, 1]], base=-E, channel_multiplier=1,
                           allow_small_or_imprecise_dtypes=True))
            pool.memset(CR[0:64, :, 1, :], 0.0)
            link(pool.memset(CI[0:64, :, 1, :], 0.0))
            pool.memset(CR[64:P, :, 0, :], 0.0)
            pool.memset(CI[64:P, :, 0, :], 0.0).then_inc(s["cp_zero"], 1)
            for dst, src in ((bgate, a["b_gate"][0].rearrange("(n p) -> p n", p=P)),
                             (g1, a["norm1_g"][0].rearrange("(k p) -> p k", p=P)),
                             (subg, a["subln_g"][0].rearrange("(p o) -> p o", o=1)),
                             (br_col[0:E], a["b_router"][0].rearrange("(p o) -> p o", o=1))):
                pool.dma_start(dst, src, allow_slow_non_contiguous=True).then_inc(s["vec_in"], 16)
            for t in range(4):
                pool.dma_start(bglu[32 * t:32 * t + 32],
                               a["ssm_b_glu"][0][P * t:P * t + P].rearrange("(q r) -> r q", q=4),
                               allow_slow_non_contiguous=True)\
                    .then_inc(s["vec_in"], 16)
            for t in range(2):
                pool.dma_start(qg[64 * t:64 * t + 64], a["q_norm_g"][0].rearrange("(p o) -> p o", o=1))\
                    .then_inc(s["vec_in"], 16)
                pool.dma_start(kg[64 * t:64 * t + 64], a["k_norm_g"][0].rearrange("(p o) -> p o", o=1))\
                    .then_inc(s["vec_in"], 16)
            for i, n in enumerate(("lambda_q1", "lambda_k1", "lambda_q2", "lambda_k2")):
                pool.dma_start(lamrow[:, i, :], a[n][0:1, :].to_broadcast([P, SUB])).then_inc(s["lam_in"], 16)
            pool.dma_start(dB.rearrange("p g h -> p (g h)"), a["ssm_d"][0:1, :].to_broadcast([P, S]))\
                .then_inc(s["d_in"], 16)
            pool.wait_ge(s["u_sb"], 2)
            pool.dma_start(u_dram.rearrange("(t p) n -> p t n", p=P), u_tm).then_inc(s["u_out"], 16)
            pool.wait_ge(s["u_out"], 16)
            for j in range(4):
                pool.dma_start(uc[32 * j:32 * j + 32],
                               u_dram[:, P * j:P * j + P].rearrange("(c s) n -> c s n", s=L))\
                    .then_inc(s["u_back"], 16)
            pool.wait_ge(s["win_t"], 1)
            pool.wait_ge(s["xT_ps"], 4)
            for dst, src in ((bbR, bbr), (bbI, bbi)):
                pool.tensor_copy(dst, src.unsqueeze(2).to_broadcast([P, GG, L, H])).then_inc(s["bb_rep"], 1)
            pool.memset(MM, 0.0).then_inc(s["m_zero"], 1)
            pool.wait_ge(s["m_zero"], 1)
            pool.wait_ge(s["kk_d"], 1)
            for t in range(L):
                pool.dma_start(MM[H * t:H * t + H, :, H * t:P], KK[H * t:H * t + H, :, 0:P - H * t])\
                    .then_inc(s["m_in"], 16)
            pool.wait_ge(s["s_prev"], 1)
            for t, lo in ((0, 64), (1, 0)):
                pool.tensor_copy(qz[lo:lo + 64, t], tq[lo:lo + 64].unsqueeze(1).to_broadcast([64, HEADS, TOK]))
                pool.tensor_copy(kz[lo:lo + 64, t], tk[lo:lo + 64].unsqueeze(1).to_broadcast([64, HEADS, TOK]))\
                    .then_inc(s["kz_fill"], 1)
                pool.wait_ge(s["kz_fill"], t + 1)
            pool.wait_ge(s["mixed"], 4)
            pool.dma_start(wr, a["w_router"][0].rearrange("(k p) n -> p k n", p=P)).then_inc(s["wr_in"], 16)
            pool.dma_start(g2b, a["norm2_g"][0:1, :].to_broadcast([P, D])).then_inc(s["g2_in"], 16)
            pool.wait_ge(piece_used, 25)
            pool.memset(bup, 0.0).then_inc(s["bup_z"], 1)
            pool.memset(bdn, 0.0)
            pool.memset(gwT, 0.0)
            pool.memset(y_s, 0.0).then_inc(s["ysb"], 1)
            pool.memset(swT0, 0.0)
            link(pool.memset(swT1, 0.0))
            pool.dma_start(bdn[0:E, :], a["b_down"][0]).then_inc(s["bd_in"], 16)
            pool.memset(iota[:, 4 * SLOTS:], 4.0 * TOK).then_inc(s["loop_z"], 1)
            pool.wait_ge(s["table"], 1)
            pool.dma_start(table_dram, table_i[:, 0:3]).then_inc(s["table_out"], 16)
            pool.wait_ge(s["table_out"], 16)
            pool.dma_start(table_row[0:1, :], table_dram.rearrange("(o q) c -> o (q c)", o=1))\
                .then_inc(s["table_in"], 16)

        @block.tensor
        def _(pe):
            def piece_arrived(i):
                pe.wait_ge(slot_in[i % RING], 16 * sum(len(piece(j)) for j in range(i % RING, i + 1, RING)))

            def transposes(jobs):
                for dst, src in jobs:
                    last = pe.transpose(dst, src, ident[0:src.shape[0], 0:src.shape[0]])
                return last

            pe.wait_ge(s["ident"], 1)
            pe.wait_ge(s["aT_in"], 1)
            transposes([(B[4][:, GG * i:GG * i + GG], natA[0:GG, i, :]) for i in range(4)])\
                .then_inc(s["aT_ps"], 1)
            pe.wait_ge(s["c_in"], 64)
            for ri in range(2):
                transposes([(B[5 + ri][:, P * i:P * i + P], c_sb[:, ri, i].rearrange("p d n -> p (d n)"))
                            for i in range(4)]).then_inc(s["cT_ps"], 1)
            pe.wait_ge(s["xn"], 2)
            for t in range(TT):
                for half in range(2):
                    transposes([(B[2 * t + half][:, P * k:P * k + P],
                                 xn[:, t, P * (4 * half + k):P * (4 * half + k) + P]) for k in range(4)])\
                        .then_inc(s["xT_ps"], 1)
            pe.wait_ge(s["xT"], 4)

            def z_columns(first, banks):
                for i in (first, first + 1):
                    piece_arrived(i)
                    w, c = stream[i % RING], PIECE * (i - first)
                    for t in range(TT):
                        for k in range(KT):
                            last = pe.matmul(B[banks[t]][:, c:c + PIECE], xnT[:, k, P * t:P * t + P],
                                             w[:, k, :], start=(k == 0), stop=(k == KT - 1))
                    last.then_inc(piece_used, 1)

            z_columns(0, (0, 1))
            z_columns(2, (2, 3))
            pe.wait_ge(s["cp_ready"], 1)
            z_columns(4, (4, 5))
            z_columns(6, (6, 7))

            pe.wait_ge(s["win_t"], 1)
            pe.wait_ge(s["qk_tm"], 4)
            pe.wait_ge(s["v_sb"], 2)
            for f in range(8):
                if f >= 4:
                    pe.wait_ge(s["wT_sb"], f - 3)
                transposes([(B[4 + f % 4][:, P * m:P * m + P], (WR, WI)[m % 2][:, 2 * f + m // 2, :])
                            for m in range(4)]).then_inc(s["wT_ps"], 1)
            pe.wait_ge(s["bb_rep"], 2)
            for f in range(8):
                if f < 4:
                    pe.wait_ge(s["wT_sb"], 5 + f)
                else:
                    pe.wait_ge(s["kk_sb"], f - 3)
                for gg in (2 * f, 2 * f + 1):
                    o = B[4 + f % 4][:, 256 * (gg % 2):256 * (gg % 2) + 256]
                    for n, (bb, cc) in enumerate(((bbR, CR), (bbI, CI))):
                        last = pe.matmul(o, bb[:, gg].rearrange("p s h -> p (s h)"),
                                         cc[:, gg, :, 0:P], start=(n == 0), stop=(n == 1))
                last.then_inc(s["kk_ps"], 1)
            pe.wait_ge(s["u_turn"], 1)
            pe.wait_ge(s["kk_sb"], 6)
            for r in range(8):
                last = transposes([(B[4 + r // 4][:, P * (r % 4):P * (r % 4) + P], uc2[:, r].rearrange("p s h -> p (s h)"))])
                if r % 4 == 3:
                    last.then_inc(s["U_ps"], 1)
            pe.wait_ge(s["U_sb"], 2)
            pe.wait_ge(s["kk_sb"], 8)
            for i in range(GG):
                slot, q = i // 4, i % 4
                for g2 in range(2):
                    g = 2 * i + g2
                    o = B[6 + slot // 2][32 * q:32 * q + 32, 256 * (slot % 2):256 * (slot % 2) + 256]\
                        .rearrange("p (r n) -> p r n", r=2)[:, :, 64 * g2:64 * g2 + 64]
                    last = pe.matmul(o, U[:, g % 8, g // 8, :], WIN_M[:, i, :, 64 * g2:64 * g2 + 64],
                                     start=True, stop=True, tile_position=(0, 32 * q))
                if i % 8 == 7:
                    last.then_inc(s["st_ps"], 1)

            def gate_columns(i):
                piece_arrived(i)
                f = i - 8
                if f == 0:
                    pe.wait_ge(s["u_sb"], 2)
                elif f == 2:
                    pe.wait_ge(s["qk_tm"], 2)
                if f >= 4:
                    pe.wait_ge(s["gate_sb"], 2 * (f - 3))
                for c in range(2):
                    for k in range(KT):
                        last = pe.matmul(B[f % 4][:, TOK * c:TOK * c + TOK],
                                         stream[i % RING][:, k, P * c:P * c + P], xnT[:, k, :],
                                         start=(k == 0), stop=(k == KT - 1))
                last.then_inc(piece_used, 1)

            for i in (8, 9):
                gate_columns(i)
            pe.wait_ge(s["st_sb"], 2)
            for ri in range(2):
                transposes([(B[4 + ri][:, P * m:P * m + P], S_sb[:, m, ri, :]) for m in range(4)])\
                    .then_inc(s["sT_ps"], 1)
            for i in range(10, 14):
                gate_columns(i)
            pe.wait_ge(s["s_prev"], 1)
            pe.wait_ge(s["m_in"], 16 * L)
            for i in range(GG):
                slot, q = i // 4, i % 4
                o = B[6 + slot // 2][32 * q:32 * q + 32, 256 * (slot % 2):256 * (slot % 2) + 256]
                pe.matmul(o, Spr[:, i, :], CR[:, i, :, H:H + P], start=True, stop=False,
                          skip_group_check=True)
                pe.matmul(o, Spi[:, i, :], CI[:, i, :, H:H + P], start=False, stop=False,
                          skip_group_check=True)
                for g2 in range(2):
                    g = 2 * i + g2
                    last = pe.matmul(o[:, P * g2:P * g2 + P], U[:, g % 8, g // 8, :], MM[:, g, :],
                                     start=False, stop=(g2 == 1), skip_group_check=True)
                if i % 8 == 7:
                    last.then_inc(s["y_ps"], 1)
            for i in (14, 15):
                gate_columns(i)
            pe.wait_ge(s["y_sb"], 4)
            for t in range(L):
                last = transposes([(B[4 + t // 4][:, P * (t % 4):P * (t % 4) + P],
                                    Y_sb[:, t].rearrange("p a b h -> p (a b h)"))])
                if t % 4 == 3:
                    last.then_inc(s["yT_ps"], 1)
            pe.wait_ge(s["gate_sb"], 16)
            pe.wait_ge(s["qk_tm"], 4)
            for n, src in enumerate((q_tm, k_tm)):
                for t in range(TT):
                    transposes([(B[2 * n + t][:, P * h:P * h + P], src[:, t, P * h:P * h + P])
                                for h in range(HEADS)]).then_inc(s["qkT_ps"], 1)
            pe.wait_ge(s["qkT"], 4)

            units = [(h, t) for h in range(HEADS) for t in range(TT)]

            def scores(u):
                h, t = units[u]
                if u >= 2:
                    pe.wait_ge(s["prob"], 2 * (u - 1))
                for sub in range(2):
                    last = pe.matmul(B[u % 2][:, TOK * sub:TOK * sub + P * (t + 1)],
                                     qz[:, sub, h, P * t:P * t + P], kz[:, sub, h, 0:P * (t + 1)],
                                     start=True, stop=True)
                last.then_inc(s["score"], 1)

            def turn_w(u):
                h, t = units[u]
                pe.wait_ge(s["wt"], u + 1)
                if u >= 2:
                    pe.wait_ge(s["w_sb"], u - 1)
                transposes([(B[2 + u % 2][:, P * j:P * j + P], wmix[:, u % 2, P * j:P * j + P])
                            for j in range(t + 1)]).then_inc(s["w_ps"], 1)

            def values(u):
                h, t = units[u]
                pe.wait_ge(s["w_sb"], u + 1)
                if u == 0:
                    pe.wait_ge(s["yT"], 2)
                for j in range(t + 1):
                    last = pe.matmul(B[4 + h // 2][:, TOK * (h % 2) + P * t:TOK * (h % 2) + P * t + P],
                                     v_tm[:, j, P * h:P * h + P], wTs[:, u % 2, j, :],
                                     start=(j == 0), stop=(j == t))
                last.then_inc(s["oT_ps"], 1)

            def glu():
                pe.wait_ge(s["wg"], 1)
                pe.wait_ge(s["yT"], 2)
                for q2 in range(4):
                    for q in range(4):
                        last = pe.matmul(B[6 + q2 // 2][:, TOK * (q2 % 2):TOK * (q2 % 2) + TOK],
                                         wg[:, q, q2, :],
                                         yT[:, q, :], start=(q == 0), stop=(q == 3))
                    if q2 == 1:
                        last.then_inc(s["glu_ps"], 1)
                last.then_inc(piece_used, 1)

            scores(0)
            scores(1)
            for u in range(8):
                turn_w(u)
                if u + 2 < 8:
                    scores(u + 2)
                values(u)
                if u == 1:
                    glu()
            pe.wait_ge(s["o_sq"], 2)
            pe.wait_ge(s["glu_s"], 4)
            for m in range(2):
                pe.matmul(B[6 + m][:, :], ones, o2[:, 2 * m:2 * m + 2, :],
                          start=True, stop=True).then_inc(s["o_ms"], 1)
            pe.wait_ge(s["yg"], 1)
            for n in range(KT):
                if n % 4 == 0:
                    piece_arrived(17 + n // 4)
                if n == 0:
                    pe.wait_ge(s["w_sb"], 8)
                for q in range(4):
                    last = pe.matmul(B[n // 2][:, TOK * (n % 2):TOK * (n % 2) + TOK],
                                     pv(17 + n // 4)[:, q, P * (n % 4):P * (n % 4) + P], yT[:, q, :],
                                     start=(q == 0), stop=(q == 3))
                if n % 4 == 3:
                    last.then_inc(piece_used, 1)
                elif n % 2 == 1:
                    last.then_inc(s["ps_ssm"], 1)
            pe.wait_ge(s["oT"], 1)
            for n in range(KT):
                if n % 4 == 0:
                    piece_arrived(19 + n // 4)
                for q in range(4):
                    last = pe.matmul(B[4 + n // 2][:, TOK * (n % 2):TOK * (n % 2) + TOK],
                                     pv(19 + n // 4)[:, q, P * (n % 4):P * (n % 4) + P], oT[:, q, :],
                                     start=(q == 0), stop=(q == 3))
                if n % 4 == 3:
                    last.then_inc(piece_used, 1)
                elif n % 2 == 1:
                    last.then_inc(s["ps_att"], 1)
            pe.wait_ge(s["mixed"], 4)
            for i in range(21, 25):
                piece_arrived(i)
                c = i - 21
                for t in range(TT):
                    for k in range(KT):
                        last = pe.matmul(B[2 * t + c // 2][:, PIECE * (c % 2):PIECE * (c % 2) + PIECE],
                                         mixT[:, k, P * t:P * t + P], stream[i % RING][:, k, :],
                                         start=(k == 0), stop=(k == KT - 1))
                last.then_inc(piece_used, 1)
            pe.wait_ge(s["hn"], 2)
            for t in range(TT):
                for half in range(2):
                    transposes([(B[4 + 2 * t + half][:, P * k:P * k + P],
                                 hn[:, t, P * (4 * half + k):P * (4 * half + k) + P]) for k in range(4)])\
                        .then_inc(s["hT_ps"], 1)
            pe.wait_ge(s["hT"], 4)
            pe.wait_ge(s["wr_in"], 16)
            for k in range(KT):
                last = pe.matmul(B[0][0:E, 0:TOK], wr[:, k, :], hT[:, k, :], start=(k == 0), stop=(k == KT - 1))
            last.then_inc(s["lg_ps"], 1)
            pe.wait_ge(s["lg_sb"], 1)
            transposes([(B[1][:, E * t:E * t + E], lgT[0:E, P * t:P * t + P]) for t in range(TT)])\
                .then_inc(s["lgt_ps"], 1)
            pe.wait_ge(s["gw"], 1)
            o = B[0][:, 256:256 + 3 * E]
            pe.matmul(o[:, 0:E], ltri, routed[:, 0, :], start=True, stop=True)
            pe.matmul(o[:, E:2 * E], ones, routed[:, 0, :], start=True, stop=False)
            pe.matmul(o[:, E:2 * E], ltri, routed[:, 1, :], start=False, stop=True)
            pe.matmul(o[:, 2 * E:], ones, routed[:, 0, :], start=True, stop=False)
            pe.matmul(o[:, 2 * E:], ones, routed[:, 1, :], start=False, stop=True).then_inc(s["rk_ps"], 1)
            transposes([(B[1][0:E, 128 + P * t:128 + P * t + P], gw[:, t, :]) for t in range(TT)])\
                .then_inc(s["gT_ps"], 1)
            pe.wait_ge(s["gT"], 1)
            pe.wait_ge(s["bd_in"], 16)
            for t in range(TT):
                for n in range(2):
                    last = pe.matmul(B[4 + 2 * t + n][:, :], gwT[:, P * t:P * t + P],
                                     bdn[:, 512 * n:512 * n + 512], start=True, stop=False,
                                     skip_group_check=True)
            last.then_inc(s["bias_ps"], 1)

            def gather(nth, turned=None):
                pe.wait_ge(s["sel"], nth)
                for k in range(KT):
                    if k == 4 and turned is not None:
                        pe.wait_ge(s["swT"], turned)
                    for t in range(TT):
                        last = pe.matmul(B[2 + k // 4][:, P * (k % 4):P * (k % 4) + P],
                                         hn[:, t, P * k:P * k + P], selg[:, t, :],
                                         start=(t == 0), stop=(t == TT - 1))
                    if k % 4 == 3:
                        last.then_inc(s["xg_ps"], 1)

            def scatter():
                for t in range(TT):
                    for n, sw in enumerate((swT0, swT1)):
                        last = pe.matmul(B[4 + 2 * t + n][:, :], sw[:, t, :], y_s, start=False, stop=False,
                                         skip_group_check=True)
                last.then_inc(s["scat"], 1)

            pe.wait_ge(s["table_in"], 16)
            blocks = pe.value_load(table_row[0:1, 2:3], min_val=E, max_val=E + EXTRA)
            pe.wait_ge(s["loop_z"], 1)
            gather(1)
            with pe.Fori(0, blocks) as b:
                pe.wait_ge(bup_in, 16 * b + 16)
                pe.wait_ge(s["glu_sb"], b + 1)
                pe.wait_ge(s["xg"], 2 * b + 2)
                for n in range(2):
                    for h in range(2):
                        last = pe.matmul(B[n][64 * h:64 * h + 64, :], e0,
                                         bup[:, D * h + 512 * n:D * h + 512 * n + 512],
                                         start=True, stop=False, skip_group_check=True)
                last.then_inc(s["bup_used"], 1)
                for k in range(KT):
                    pe.wait_ge(up_in[k], 16 * b + 16)
                    for n in range(2):
                        for h in range(2):
                            last = pe.matmul(B[n][64 * h:64 * h + 64, :], xg[:, k, :],
                                             up_w[:, k, D * h + 512 * n:D * h + 512 * n + 512],
                                             start=False, stop=(k == KT - 1), skip_group_check=True)
                    last.then_inc(s["up_used"], 1)
                pe.wait_ge(s["ysb"], b + 1)
                scatter()
                pe.wait_ge(s["dsel"], b + 1)
                transposes([(B[3][:, P * t:P * t + P], selw[:, t, :]) for t in range(TT)])\
                    .then_inc(s["swt_ps"], 1)
                gather(b + 2, b + 1)
                pe.wait_ge(s["act"], b + 1)
                pe.wait_ge(s["xg"], 2 * b + 3)
                transposes([(B[2][:, P * j:P * j + P], act_s[:, P * j:P * j + P]) for j in range(4)])\
                    .then_inc(s["aT2_ps"], 1)
                pe.wait_ge(s["aT2"], b + 1)
                pe.wait_ge(s["xg"], 2 * b + 4)
                for k in range(KT):
                    if k % 2 == 0:
                        pe.wait_ge(dn_in[k // 2], 16 * b + 16)
                    for n in range(2):
                        last = pe.matmul(B[3][64 * n:64 * n + 64, :], actT[:, k % 4, k // 4, :],
                                         dn_w[:, k, 512 * n:512 * n + 512],
                                         start=(k == 0), stop=(k == KT - 1), skip_group_check=True)
                    if k % 2 == 1:
                        last.then_inc(s["dn_used"], 1)
            pe.wait_ge(s["ysb"], blocks + 1)
            scatter()

        @block.scalar
        def _(act):
            act.wait_ge(s["a_in"], 48)
            act.activation(dts[0:GG], dts[0:GG], ACT.Exp).then_inc(s["dt"], 1)
            act.wait_ge(s["x_in"], 16)
            for t in range(TT):
                act.activation(xn[:, t, :], hx[:, t, :], ACT.Square, accum_out=xs[:, t:t + 1])\
                    .then_inc(s["x_sq"], 1)
            act.wait_ge(s["x_var"], 1)
            act.activation(xr, xs, ACT.Sqrt).then_inc(s["x_rs"], 1)
            act.wait_ge(s["trig"], 1)
            act.activation(mg[:, 0, :], pa[:, 2, :], ACT.Exp)
            act.activation(mg[:, 1, :], pa[:, 2, :], ACT.Exp, scale=float(L))
            act.activation(tr[:, 3, :], tr[:, 2, :], ACT.Sin)
            act.activation(tr[:, 4, :], tr[:, 1, :], ACT.Sin).then_inc(s["sincos"], 1)
            for t in range(TT):
                act.wait_ge(piece_used, 2)
                act.activation(u_tm[:, t, :], B[t][:, :], ACT.Copy).then_inc(s["u_sb"], 1)
            act.wait_ge(s["lam_e"], 1)
            act.activation(lamv[:, 0:2], lamv[:, 2:4], ACT.Exp).then_inc(s["lam_n"], 1)
            for n, dst in enumerate((q_tm, k_tm)):
                act.wait_ge(piece_used, 4 + 2 * n)
                for t in range(TT):
                    act.activation(dst[:, t, :], B[2 + 2 * n + t][:, :], ACT.Square)\
                        .then_inc(s["q_sq"], 1)
            act.wait_ge(piece_used, 8)
            for t in range(TT):
                act.activation(v_tm[:, t, :], B[6 + t][:, :], ACT.Copy).then_inc(s["v_sb"], 1)
            act.wait_ge(s["qk_var"], 1)
            act.activation(qv, qv, ACT.Sqrt).then_inc(s["qk_rs"], 1)
            for f in range(8):
                act.wait_ge(s["wT_ps"], f + 1)
                act.activation(WIN_M[:, 2 * f:2 * f + 2].rearrange("p a b c -> p (a b c)"),
                               B[4 + f % 4][:, :], ACT.Copy).then_inc(s["wT_sb"], 1)
            act.wait_ge(s["u_back"], 64)
            act.activation(uc2.rearrange("p r s h -> p s r h"), uc.rearrange("p s (r h) -> p s r h", h=H),
                           ACT.Copy).then_inc(s["u_turn"], 1)
            for f in range(8):
                act.wait_ge(s["kk_ps"], f + 1)
                act.activation(KK[:, 4 * f:4 * f + 4].rearrange("p a b -> p (a b)"),
                               B[4 + f % 4][:, :], ACT.Copy).then_inc(s["kk_sb"], 1)
            for m in range(2):
                act.wait_ge(s["U_ps"], m + 1)
                act.activation(U[:, 4 * m:4 * m + 4].rearrange("p a b c -> p (a b c)"),
                               B[4 + m][:, :], ACT.Copy).then_inc(s["U_sb"], 1)
            for m in range(2):
                act.wait_ge(s["st_ps"], m + 1)
                act.activation(S_sb[:, 2 * m:2 * m + 2].rearrange("p a b c -> p (a b c)"),
                               B[6 + m][:, :], ACT.Copy).then_inc(s["st_sb"], 1)
            act.wait_ge(s["vec_in"], 16 * 12)

            def gate(n):
                f = n // 2
                act.wait_ge(piece_used, 9 + f)
                act.activation(gates[:, n, :], B[f % 4][:, TOK * (n % 2):TOK * (n % 2) + TOK],
                               ACT.Sigmoid, bias=bgate[:, n:n + 1]).then_inc(s["gate_sb"], 1)

            for n in range(12):
                gate(n)
            for m in range(2):
                act.wait_ge(s["y_ps"], m + 1)
                for i in range(2):
                    act.activation(Y_sb[:, :, 2 * m + i].rearrange("p t g h -> p g t h"),
                                   B[6 + m][:, 256 * i:256 * i + 256].rearrange("p (g t h) -> p g t h", g=2, h=H),
                                   ACT.Copy).then_inc(s["y_sb"], 1)
            for n in range(12, 16):
                gate(n)
            act.wait_ge(piece_used, 16)
            act.wait_ge(slot_in[16 % RING], 16 * sum(len(piece(j)) for j in range(16 % RING, 17, RING)))
            for q in range(4):
                last = act.activation(wg[:, q].rearrange("p c (t r) -> p c t r", t=4),
                                      pv(16)[:, q, :].rearrange("p (t c r) -> p c t r", t=4, c=4), ACT.Copy)
            last.then_inc(s["wg"], 1)
            for m in range(2):
                act.wait_ge(s["yT_ps"], m + 1)
                act.wait_ge(s["qkT_ps"], 4)
                act.activation(ge1[:, 4 * m:4 * m + 4].rearrange("p a b c -> p (a b c)"),
                               B[4 + m][:, :], ACT.Square).then_inc(s["gelu_sq"], 1)
            for m in range(2):
                act.wait_ge(s["gelu_w"], m + 1)
                act.activation(ge2[:, 4 * m:4 * m + 4].rearrange("p a b c -> p (a b c)"),
                               ge1[:, 4 * m:4 * m + 4].rearrange("p a b c -> p (a b c)"),
                               ACT.Sigmoid, scale=2 * math.sqrt(2 / math.pi)).then_inc(s["gelu_s"], 1)

            def softmax(u):
                t = u % 2
                act.wait_ge(s["smax"], u + 1)
                if u >= 2:
                    act.wait_ge(s["wt"], u - 1)
                for sub in range(2):
                    act.activation(probs(u, sub), B[u % 2][:, TOK * sub:TOK * sub + P * (t + 1)], ACT.Exp,
                                   bias=nmx[:, u % 2, sub:sub + 1], scale=SUB ** -0.5,
                                   accum_out=rsum[:, u % 2, sub:sub + 1]).then_inc(s["prob"], 1)

            def turned(u):
                t = u % 2
                act.wait_ge(s["w_ps"], u + 1)
                if u >= 2:
                    act.wait_ge(s["oT_ps"], u - 1)
                act.activation(wTs[:, u % 2, 0:t + 1, :].rearrange("p a b -> p (a b)"),
                               B[2 + u % 2][:, 0:P * (t + 1)], ACT.Copy).then_inc(s["w_sb"], 1)

            def glu_sigmoid():
                for q in range(4):
                    if q == 0:
                        act.wait_ge(s["glu_ps"], 1)
                    if q == 2:
                        act.wait_ge(piece_used, 17)
                    act.activation(ge1[:, 2 * q:2 * q + 2].rearrange("p a b c -> p (a b c)"),
                                   B[6 + q // 2][:, TOK * (q % 2):TOK * (q % 2) + TOK],
                                   ACT.Sigmoid, bias=bglu[:, q:q + 1]).then_inc(s["glu_s"], 1)

            softmax(0)
            softmax(1)
            for u in range(8):
                turned(u)
                if u + 2 < 8:
                    softmax(u + 2)
            glu_sigmoid()
            for m in range(2):
                act.wait_ge(s["oT_ps"], 4 * m + 4)
                act.activation(o2[:, 2 * m:2 * m + 2, :].rearrange("p a b -> p (a b)"), B[4 + m][:, :],
                               ACT.Square).then_inc(s["o_sq"], 1)
            act.wait_ge(s["o_var"], 1)
            act.activation(o_rs, o_rs, ACT.Sqrt).then_inc(s["o_rs"], 1)
            for t in range(TT):
                act.wait_ge(s["h"], 2 * t + 2)
                act.activation(hn[:, t, :], hx[:, t, :], ACT.Square, accum_out=xs[:, t:t + 1])\
                    .then_inc(s["h_sq"], 1)
            act.wait_ge(s["h_var"], 1)
            act.activation(xr, xs, ACT.Sqrt).then_inc(s["h_rs"], 1)
            for t in range(TT):
                for half in range(2):
                    act.wait_ge(s["hT_ps"], 2 * t + half + 1)
                    act.activation(hT[:, 4 * half:4 * half + 4, P * t:P * t + P],
                                   B[4 + 2 * t + half][:, :].rearrange("p (k n) -> p k n", k=4),
                                   ACT.Copy).then_inc(s["hT"], 1)
            act.wait_ge(s["top_e"], 1)
            for t in range(TT):
                act.activation(top_w[:, t, 0:TOPK], top_v[:, t, 0:TOPK], ACT.Exp,
                               bias=xs[:, t:t + 1], accum_out=xr[:, t:t + 1]).then_inc(s["top_x"], 1)

            def gathered(n):
                act.activation(xg[:, 4 * n:4 * n + 4, :],
                               B[2 + n][:, :].rearrange("p (k c) -> p k c", k=4)[:, :, 0:SLOTS],
                               ACT.Copy).then_inc(s["xg"], 1)

            act.wait_ge(s["table_in"], 16)
            blocks = act.value_load(table_row[0:1, 2:3], min_val=E, max_val=E + EXTRA)
            for n in range(2):
                act.wait_ge(s["xg_ps"], n + 1)
                gathered(n)
            with act.Fori(0, blocks) as b:
                act.wait_ge(s["glu_sb"], b + 2)
                act.activation(sig_t, glu_t, ACT.Sigmoid, scale=ALPHA).then_inc(s["sig"], 1)
                act.wait_ge(s["swt_ps"], b + 1)
                act.activation(swT0[0:64].rearrange("p a b -> p (a b)"), B[3][0:64, 0:2 * P], ACT.Copy)
                act.activation(swT1[64:P].rearrange("p a b -> p (a b)"), B[3][64:P, 0:2 * P], ACT.Copy)\
                    .then_inc(s["swT"], 1)
                for n in range(2):
                    act.wait_ge(s["xg_ps"], 2 * b + 3 + n)
                    gathered(n)
                act.wait_ge(s["aT2_ps"], b + 1)
                act.activation(actT.rearrange("p a b c -> p (a b c)"), B[2][:, :], ACT.Copy)\
                    .then_inc(s["aT2"], 1)
                act.wait_ge(s["dn_used"], 4 * b + 4)
                act.activation(y_s, B[3][:, :], ACT.Copy).then_inc(s["ysb"], 1)

        @block.vector
        def _(dve):
            steps = [0]

            def link(ins):
                steps[0] += 1
                ins.then_inc(s["dve_step"], 1)
                dve.wait_ge(s["dve_step"], steps[0])

            TTo, TS, STT = dve.tensor_tensor, dve.tensor_scalar, dve.scalar_tensor_tensor

            dve.wait_ge(s["dt"], 1)
            dtb = dts[0:GG].unsqueeze(2).to_broadcast([GG, 2, PS])
            for i in range(2):
                last = TTo(natA[0:GG, 2 + i, :].rearrange("p (t n) -> p t n", t=2),
                           natA[0:GG, i, :].rearrange("p (t n) -> p t n", t=2), dtb, ALU.mult)
            last.then_inc(s["aT_in"], 1)
            dve.wait_ge(s["x_sq"], 2)
            link(TS(xs, xs, 1.0 / D, EPS, ALU.mult, ALU.add))
            dve.reciprocal(xs, xs).then_inc(s["x_var"], 1)
            dve.wait_ge(s["x_rs"], 1)
            for t in range(TT):
                TS(xn[:, t, :], hx[:, t, :], xr[:, t:t + 1], None, ALU.mult).then_inc(s["xn"], 1)
            dve.wait_ge(s["vec_in"], 16 * 12)
            for t in range(TT):
                for half in range(2):
                    dve.wait_ge(s["xT_ps"], 2 * t + half + 1)
                    TTo(xnT[:, 4 * half:4 * half + 4, P * t:P * t + P],
                        B[2 * t + half][:, :].rearrange("p (k n) -> p k n", k=4),
                        g1[:, 4 * half:4 * half + 4].unsqueeze(2).to_broadcast([P, 4, P]), ALU.mult)\
                        .then_inc(s["xT"], 1)
            dve.wait_ge(s["aT_ps"], 1)
            link(dve.tensor_copy(pa.rearrange("p a b -> p (a b)"), B[4][:, 0:4 * GG]))
            kk, r, rc = tr[:, 0, :], tr[:, 1, :], tr[:, 2, :]
            sn, cs = tr[:, 4, :], tr[:, 3, :]
            link(TS(kk, pa[:, 3, :], 1 / (2 * math.pi), ROUND, ALU.mult, ALU.add))
            link(TS(kk, kk, ROUND, None, ALU.subtract))
            link(STT(r, kk, -TWO_PI_1, pa[:, 3, :], ALU.mult, ALU.add))
            link(STT(r, kk, -TWO_PI_2, r, ALU.mult, ALU.add))
            link(STT(r, kk, -TWO_PI_3, r, ALU.mult, ALU.add))
            link(TS(r, r, 3.1415925, -3.1415925, ALU.min, ALU.max))
            link(TS(rc, r, -1.0, None, ALU.mult))
            link(TTo(rc, rc, r, ALU.max))
            TS(rc, rc, -1.0, math.pi / 2, ALU.mult, ALU.add).then_inc(s["trig"], 1)
            for ri, dst in enumerate((cTr, cTi)):
                dve.wait_ge(s["cT_ps"], ri + 1)
                v = B[5 + ri][:, :].rearrange("p (g t h) -> p g t h", t=2, h=H)
                for t in range(2):
                    last = dve.tensor_copy(dst[64 * t:64 * t + 64], v[64 * t:64 * t + 64, :, t, :])
            link(last)

            def cmul(outr, outi, ar, ai, br, bi, shape):
                n = 1
                for d in shape:
                    n *= d
                t = []
                for v in (sc1, sc2, sc3, sc4):
                    v = v.rearrange("p a b -> p (a b)")[:, 0:n]
                    t.append(v if len(shape) == 1 else v.rearrange("p (a b) -> p a b", a=shape[0]))
                TTo(t[0], ar, br, ALU.mult)
                TTo(t[1], ai, bi, ALU.mult)
                TTo(t[2], ar, bi, ALU.mult)
                link(TTo(t[3], ai, br, ALU.mult))
                TTo(outr, t[0], t[1], ALU.subtract)
                link(TTo(outi, t[2], t[3], ALU.add))

            def per_pair(v, n):
                return v.unsqueeze(2).to_broadcast([P, GG, n])

            dve.wait_ge(s["sincos"], 1)
            dve.memset(Pr[:, :, 0], 1.0)
            dve.memset(Pi[:, :, 0], 0.0)
            TTo(Pr[:, :, 1], mg[:, 0, :], cs, ALU.mult)
            link(TTo(Pi[:, :, 1], mg[:, 0, :], sn, ALU.mult))
            for n in (1, 2, 4):
                cmul(Pr[:, :, n + 1:2 * n + 1], Pi[:, :, n + 1:2 * n + 1], Pr[:, :, 1:n + 1], Pi[:, :, 1:n + 1],
                     per_pair(Pr[:, :, n], n), per_pair(Pi[:, :, n], n), (GG, n))
            for t in range(L):
                dve.tensor_copy(Vr[:, :, t], Pr[:, :, L - 1 - t])
                last = dve.tensor_copy(Vi[:, :, t], Pi[:, :, L - 1 - t])
            link(last)
            lr, li = pa[:, 0, :], pa[:, 1, :]
            t0, t1, t2, t3, t4, t5 = t16
            TTo(t0, lr, lr, ALU.mult)
            TTo(t1, li, li, ALU.mult)
            link(TS(t2, Pr[:, :, 1], 1.0, None, ALU.subtract))
            link(TTo(t0, t0, t1, ALU.add))
            TTo(t1, t2, lr, ALU.mult)
            TTo(t3, Pi[:, :, 1], li, ALU.mult)
            TTo(t4, Pi[:, :, 1], lr, ALU.mult)
            link(TTo(t5, t2, li, ALU.mult))
            dve.reciprocal(t0, t0)
            TTo(t1, t1, t3, ALU.add)
            link(TTo(t4, t4, t5, ALU.subtract))
            TTo(cfr, t1, t0, ALU.mult)
            link(TTo(cfi, t4, t0, ALU.mult))
            dve.wait_ge(s["b_in"], 32)
            cmul(bbr, bbi, br_raw, bi_raw, per_pair(cfr, H), per_pair(cfi, H), (GG, H))

            dve.wait_ge(s["cp_zero"], 1)

            def four(v, n, e):
                return v.unsqueeze(2).to_broadcast([P, GG, n, H]) if e else \
                    v.unsqueeze(3).to_broadcast([P, GG, n, H])

            CRv, CIv = [v.rearrange("p g t (e h) -> p g t e h", h=H) for v in (CR, CI)]
            TTo(tA, four(Pr, 9, 0), four(cTr, 9, 1), ALU.mult)
            link(TTo(tB, four(Pi, 9, 0), four(cTi, 9, 1), ALU.mult))
            for t in range(2):
                o = slice(64 * t, 64 * t + 64)
                last = TTo(CRv[o, :, t], tA[o], tB[o], ALU.subtract)
            link(last)
            TTo(tA, four(Pr, 9, 0), four(cTi, 9, 1), ALU.mult)
            link(TTo(tB, four(Pi, 9, 0), four(cTr, 9, 1), ALU.mult))
            for t in range(2):
                o = slice(64 * t, 64 * t + 64)
                last = STT(CIv[o, :, t], tA[o], -1.0, tB[o], ALU.mult, ALU.subtract)
            last.then_inc(s["cp_ready"], 1)
            dve.wait_ge(s["cp_ready"], 1)
            WRv, WIv = [v.rearrange("p g (e h) -> p g e h", h=H) for v in (WR, WI)]
            tAw, tBw = tA[:, :, 0:L], tB[:, :, 0:L]
            TTo(tAw, four(Vr, L, 0), four(bbr, L, 1), ALU.mult)
            link(TTo(tBw, four(Vi, L, 0), four(bbi, L, 1), ALU.mult))
            link(TTo(WRv, tAw, tBw, ALU.subtract))
            TTo(tAw, four(Vr, L, 0), four(bbi, L, 1), ALU.mult)
            link(TTo(tBw, four(Vi, L, 0), four(bbr, L, 1), ALU.mult))
            TTo(WIv, tAw, tBw, ALU.add).then_inc(s["win_t"], 1)
            dve.wait_ge(s["lam_in"], 64)
            for i in range(2):
                last = dve.tensor_tensor_reduce(lamrow[:, 2 * i, :], lamrow[:, 2 * i, :],
                                                lamrow[:, 2 * i + 1, :], 1.0, 0.0, ALU.mult, ALU.add,
                                                lamv[:, 2 + i:3 + i])
            last.then_inc(s["lam_e"], 1)
            dve.wait_ge(s["q_sq"], 4)
            for n, src in enumerate((q_tm, k_tm)):
                last = dve.tensor_reduce(qv[:, n].rearrange("p t g -> p (t g)"),
                                         src.rearrange("p t (g d) -> p (t g) d", d=SUB), AX, ALU.add)
            link(last)
            link(TS(qv, qv, 1.0 / SUB, EPS, ALU.mult, ALU.add))
            dve.reciprocal(qv, qv).then_inc(s["qk_var"], 1)
            dve.wait_ge(s["qk_rs"], 1)
            for n, dst in enumerate((q_tm, k_tm)):
                for t in range(TT):
                    TTo(dst[:, t, :].rearrange("p (g d) -> p g d", d=SUB),
                        B[2 + 2 * n + t][:, :].rearrange("p (g d) -> p g d", d=SUB),
                        qv[:, n, t, :].unsqueeze(2).to_broadcast([P, 8, SUB]), ALU.mult)\
                        .then_inc(s["qk_tm"], 1)
            dve.wait_ge(s["lam_n"], 1)
            link(TTo(lamv[:, 4:5], lamv[:, 1:2], lamv[:, 0:1], ALU.subtract))
            link(TS(lamv[:, 4:5], lamv[:, 4:5], LAMBDA_INIT, None, ALU.subtract))
            link(dve.tensor_copy(e8r, cs))
            link(dve.tensor_copy(e8i, sn))
            for _ in range(3):
                cmul(t16[0], t16[1], e8r, e8i, e8r, e8i, (GG,))
                dve.tensor_copy(e8r, t16[0])
                link(dve.tensor_copy(e8i, t16[1]))
            dve.memset(Rr[:, :, 0], 1.0)
            dve.memset(Ri[:, :, 0], 0.0)
            dve.tensor_copy(Rr[:, :, 1], e8r)
            link(dve.tensor_copy(Ri[:, :, 1], e8i))
            for n in (1, 2, 4, 8, 15):
                cmul(Rr[:, :, n + 1:2 * n + 1], Ri[:, :, n + 1:2 * n + 1], Rr[:, :, 1:n + 1], Ri[:, :, 1:n + 1],
                     per_pair(Rr[:, :, n], n), per_pair(Ri[:, :, n], n), (GG, n))
            cmul(Rr[:, :, 31:32], Ri[:, :, 31:32], Rr[:, :, 30:31], Ri[:, :, 30:31],
                 Rr[:, :, 1:2], Ri[:, :, 1:2], (GG, 1))
            dve.tensor_copy(magz, per_pair(mg[:, 1, :], NC))
            dve.wait_ge(s["ident"], 1)
            link(dve.tensor_reduce(hsel, ident.rearrange("p (k h) -> p h k", h=H), AX, ALU.add))
            link(dve.memset(magz[:, :, 0], 0.0))
            dve.wait_ge(s["d_in"], 16)
            link(TTo(dd, dB, hsel.unsqueeze(1).to_broadcast([P, G, H]), ALU.mult))
            dve.wait_ge(s["kk_sb"], 8)
            TTo(KK[:, :, 0:H], KK[:, :, 0:H], dd, ALU.add).then_inc(s["kk_d"], 1)
            dve.wait_ge(s["kk_d"], 1)
            dve.wait_ge(s["sT_ps"], 2)
            Ir, Ii = [B[4 + n][:, :].rearrange("p (g c) -> p g c", c=NC) for n in range(2)]
            i0, i1, i2, i3 = [It[:, n] for n in range(4)]
            TTo(i0, Ir, Rr, ALU.mult)
            TTo(i1, Ii, Ri, ALU.mult)
            TTo(i2, Ii, Rr, ALU.mult)
            link(TTo(i3, Ir, Ri, ALU.mult))
            TTo(i0, i0, i1, ALU.add)
            link(TTo(i2, i2, i3, ALU.subtract))
            flat = lambda v: v.rearrange("p g c -> p (g c)")
            dve.tensor_tensor_scan(flat(i1), flat(magz), flat(i0), 0.0, ALU.mult, ALU.add)
            link(dve.tensor_tensor_scan(flat(i3), flat(magz), flat(i2), 0.0, ALU.mult, ALU.add))
            dve.memset(Spr[:, :, 0], 0.0)
            dve.memset(Spi[:, :, 0], 0.0)
            w = slice(0, NC - 1)
            TTo(i0[:, :, w], i1[:, :, w], Rr[:, :, w], ALU.mult)
            link(TTo(i2[:, :, w], i3[:, :, w], Ri[:, :, w], ALU.mult))
            link(TTo(Spr[:, :, 1:], i0[:, :, w], i2[:, :, w], ALU.subtract))
            TTo(i0[:, :, w], i3[:, :, w], Rr[:, :, w], ALU.mult)
            link(TTo(i2[:, :, w], i1[:, :, w], Ri[:, :, w], ALU.mult))
            TTo(Spi[:, :, 1:], i0[:, :, w], i2[:, :, w], ALU.add).then_inc(s["s_prev"], 1)
            dve.wait_ge(s["kz_fill"], 2)
            for n, (dst, gain) in enumerate(((qz, qg), (kz, kg))):
                for t in range(TT):
                    dve.wait_ge(s["qkT_ps"], 2 * n + t + 1)
                    for sub in range(2):
                        o = slice(64 * sub, 64 * sub + 64)
                        last = TS(dst[o, sub, :, P * t:P * t + P],
                                  B[2 * n + t][o, :].rearrange("p (h q) -> p h q", h=HEADS),
                                  gain[o], None, ALU.mult)
                    last.then_inc(s["qkT"], 1)
            for m in range(2):
                dve.wait_ge(s["gelu_sq"], m + 1)
                o = slice(4 * m, 4 * m + 4)
                y = B[4 + m][:, :].rearrange("p (t q c) -> p t q c", t=4, q=4)
                link(TS(ge1[:, o], ge1[:, o], 0.044715, 1.0, ALU.mult, ALU.add))
                TTo(ge1[:, o], ge1[:, o], y, ALU.mult).then_inc(s["gelu_w"], 1)
            for m in range(2):
                dve.wait_ge(s["gelu_s"], m + 1)
                y = B[4 + m][:, :].rearrange("p (t q c) -> p t q c", t=4, q=4)
                for t in range(4):
                    last = TTo(yT.rearrange("p q (c t) -> p t q c", t=L)[:, 4 * m + t],
                               y[:, t], ge2[:, 4 * m + t], ALU.mult)
                last.then_inc(s["yT"], 1)

            def row_max(u):
                t = u % 2
                dve.wait_ge(s["score"], u + 1)
                if u >= 2:
                    dve.wait_ge(s["prob"], 2 * (u - 1))
                link(dve.tensor_reduce(smx[:, u % 2, :], B[u % 2][:, :].rearrange("p (s k) -> p s k", s=2)
                                       [:, :, 0:P * (t + 1)], AX, ALU.max))
                TS(nmx[:, u % 2, :], smx[:, u % 2, :], -SUB ** -0.5, None, ALU.mult).then_inc(s["smax"], 1)

            def difference(u):
                t = u % 2
                dve.wait_ge(s["prob"], 2 * u + 2)
                link(dve.reciprocal(rinv[:, u % 2, :], rsum[:, u % 2, :]))
                link(TTo(rinv[:, u % 2, 1:2], rinv[:, u % 2, 1:2], lamv[:, 4:5], ALU.mult))
                if u >= 2:
                    dve.wait_ge(s["w_ps"], u - 1)
                wu = wmix[:, u % 2, 0:P * (t + 1)]
                link(TS(wu, probs(u, 1), rinv[:, u % 2, 1:2], None, ALU.mult))
                STT(wu, probs(u, 0), rinv[:, u % 2, 0:1], wu, ALU.mult, ALU.add).then_inc(s["wt"], 1)

            row_max(0)
            row_max(1)
            for u in range(8):
                difference(u)
                if u + 2 < 8:
                    row_max(u + 2)
            dve.wait_ge(s["glu_s"], 4)
            TTo(yT.rearrange("p q n -> p (q n)"), yT.rearrange("p q n -> p (q n)"),
                ge1.rearrange("p a b c -> p (a b c)"), ALU.mult).then_inc(s["yg"], 1)
            for m in range(2):
                dve.wait_ge(s["o_ms"], m + 1)
                last = TS(o_rs[:, 2 * m:2 * m + 2, :].rearrange("p a b -> p (a b)"), B[6 + m][:, :],
                          1.0 / P, EPS, ALU.mult, ALU.add)
            link(last)
            dve.reciprocal(o_rs, o_rs).then_inc(s["o_var"], 1)
            link(TS(lamv[:, 5:6], subg, 1.0 - LAMBDA_INIT, None, ALU.mult))
            dve.wait_ge(s["o_rs"], 1)
            for m in range(2):
                last = STT(oT[:, 2 * m:2 * m + 2, :].rearrange("p a b -> p (a b)"), B[4 + m][:, :],
                           lamv[:, 5:6], o_rs[:, 2 * m:2 * m + 2, :].rearrange("p a b -> p (a b)"),
                           ALU.mult, ALU.mult)
            last.then_inc(s["oT"], 1)
            gf = gates.rearrange("p n t -> p (n t)")
            mf = mixT.rearrange("p n t -> p (n t)")
            for f in range(4):
                if f % 2 == 0:
                    dve.wait_ge(s["ps_ssm"], f // 2 + 1)
                else:
                    dve.wait_ge(piece_used, 18 + f // 2)
                last = TTo(mf[:, 512 * f:512 * f + 512], B[f][:, :], gf[:, 512 * f:512 * f + 512], ALU.mult)
            link(last)
            for f in range(4):
                if f % 2 == 0:
                    dve.wait_ge(s["ps_att"], f // 2 + 1)
                else:
                    dve.wait_ge(piece_used, 20 + f // 2)
                m = mtmp[:, f % 2, :]
                link(TTo(m, B[4 + f][:, :], gf[:, 2048 + 512 * f:2048 + 512 * f + 512], ALU.mult))
                TTo(mf[:, 512 * f:512 * f + 512], mf[:, 512 * f:512 * f + 512], m, ALU.add)\
                    .then_inc(s["mixed"], 1)
            dve.wait_ge(piece_used, 25)
            for t in range(TT):
                for n in range(2):
                    TTo(hx[:, t, 512 * n:512 * n + 512], hx[:, t, 512 * n:512 * n + 512],
                        B[2 * t + n][:, :], ALU.add).then_inc(s["h"], 1)
            dve.wait_ge(s["h_sq"], 2)
            link(TS(xs, xs, 1.0 / D, EPS, ALU.mult, ALU.add))
            dve.reciprocal(xs, xs).then_inc(s["h_var"], 1)
            dve.wait_ge(s["g2_in"], 16)
            dve.wait_ge(s["h_rs"], 1)
            for t in range(TT):
                STT(hn[:, t, :], hx[:, t, :], xr[:, t:t + 1], g2b, ALU.mult, ALU.mult).then_inc(s["hn"], 1)
            dve.wait_ge(s["lg_ps"], 1)
            TS(lgT[0:E], B[0][0:E, 0:TOK], br_col[0:E], None, ALU.add).then_inc(s["lg_sb"], 1)
            dve.wait_ge(s["lgt_ps"], 1)
            link(dve.tensor_copy(lg.rearrange("p t e -> p (t e)"), B[1][:, 0:TT * E]))
            for t in range(TT):
                last = dve.max(top_v[:, t, :], lg[:, t, :])
            link(last)
            TS(xs, top_v[:, :, 0], -1.0, None, ALU.mult).then_inc(s["top_e"], 1)
            for t in range(TT):
                last = dve.max_index(top_i[:, t, :], top_v[:, t, :], lg[:, t, :])
            link(last)
            link(dve.tensor_copy(top_f, top_i))
            dve.wait_ge(s["top_x"], 2)
            link(dve.reciprocal(xr, xr))
            for t in range(TT):
                last = TS(top_w[:, t, 0:TOPK], top_w[:, t, 0:TOPK], xr[:, t:t + 1], None, ALU.mult)
            link(last)
            pick = lgT.rearrange("p (t e k) -> p t e k", t=TT, k=TOPK)
            for t in range(TT):
                for k in range(TOPK):
                    last = TS(pick[:, t, :, k], iota[:, 0:E], top_f[:, t, k:k + 1], top_w[:, t, k:k + 1],
                              ALU.is_equal, ALU.mult)
            link(last)
            link(dve.tensor_reduce(gw, pick, AX, ALU.add))
            TS(routed, gw, 0.0, None, ALU.is_gt).then_inc(s["gw"], 1)
            dve.wait_ge(s["rk_ps"], 1)
            o = B[0][:, 256:256 + 3 * E]
            link(STT(rank.rearrange("p t e -> p (t e)"), o[:, 0:TT * E], 1.0,
                     routed.rearrange("p t e -> p (t e)"), ALU.add, ALU.mult))
            TS(rank, rank, 1.0, None, ALU.subtract)
            link(dve.tensor_copy(cnt, o[:, 2 * E:]))
            dve.wait_ge(s["loop_z"], 1)
            dve.wait_ge(s["gT_ps"], 1)
            dve.tensor_copy(gwT[0:E], B[1][0:E, 128:128 + TOK]).then_inc(s["gT"], 1)
            link(TS(ovf, cnt, float(SLOTS), None, ALU.is_gt))
            link(STT(ovf, cnt, 2.0 * SLOTS, ovf, ALU.is_gt, ALU.add))
            link(STT(ovf, cnt, 3.0 * SLOTS, ovf, ALU.is_gt, ALU.add))
            link(dve.tensor_tensor_scan(cum, ones[:, 0:E], ovf, 0.0, ALU.mult, ALU.add))
            link(TS(before, cum, iop, None, ALU.is_le))
            dve.tensor_reduce(tabf[:, 0:1], before, AX, ALU.add)
            link(TTo(ovt, before, ovf, ALU.mult))
            link(dve.tensor_reduce(tabf[:, 1:2], ovt, AX, ALU.add))
            link(TS(tabf[:, 3:4], iop, 0.0, None, ALU.is_lt))
            link(TS(tabf[:, 4:5], iop, float(E), tabf[:, 3:4], ALU.add, ALU.mult))
            link(TTo(tabf[:, 0:1], tabf[:, 0:1], tabf[:, 4:5], ALU.add))
            link(TS(tabf[:, 0:1], tabf[:, 0:1], float(E - 1), None, ALU.min))
            link(TTo(tabf[:, 1:2], iop, tabf[:, 1:2], ALU.subtract))
            link(TS(tabf[:, 1:2], tabf[:, 1:2], 1.0, float(SLOTS), ALU.add, ALU.mult))
            link(TS(tabf[:, 3:4], tabf[:, 3:4], -1.0, 1.0, ALU.mult, ALU.add))
            link(TTo(tabf[:, 1:2], tabf[:, 1:2], tabf[:, 3:4], ALU.mult))
            link(TS(tabf[:, 1:2], tabf[:, 1:2], 0.0, 3.0 * SLOTS, ALU.max, ALU.min))
            link(TS(tabf[:, 2:3], cum[:, E - 1:E], float(E), None, ALU.add))
            dve.tensor_copy(table_i[:, 0:3], tabf[:, 0:3]).then_inc(s["table"], 1)

            def one_hot(dst, e, first, weighted):
                for t in range(TT):
                    last = TS(dst[:, t, :].rearrange("p (d n) -> p d n", d=2),
                              iota[:, bass.ds(first, SLOTS)].unsqueeze(1).to_broadcast([P, 2, SLOTS]),
                              rank[:, t, bass.ds(e, 1)], gw[:, t, bass.ds(e, 1)] if weighted else None,
                              ALU.is_equal, *((ALU.mult,) if weighted else ()))
                return last

            dve.wait_ge(s["gT"], 1)
            dve.memset(glu_t[:, 0:1], 0.0).then_inc(s["glu_sb"], 1)
            one_hot(selg, 0, 0, False).then_inc(s["sel"], 1)
            dve.wait_ge(s["table_in"], 16)
            blocks = dve.value_load(table_row[0:1, 2:3], min_val=E, max_val=E + EXTRA)
            with dve.Fori(0, blocks) as b:
                e = dve.value_load(table_row[0:1, bass.ds(3 * b, 1)], min_val=0, max_val=E - 1)
                first = dve.value_load(table_row[0:1, bass.ds(3 * b + 1, 1)], min_val=0, max_val=3 * SLOTS)
                e_next = dve.value_load(table_row[0:1, bass.ds(3 * b + 3, 1)], min_val=0, max_val=E - 1)
                first_next = dve.value_load(table_row[0:1, bass.ds(3 * b + 4, 1)], min_val=0,
                                            max_val=3 * SLOTS)
                dve.wait_ge(s["xg_ps"], 2 * b + 2)
                one_hot(selw, e, first, True).then_inc(s["dsel"], 1)
                one_hot(selg, e_next, first_next, False).then_inc(s["sel"], 1)
                dve.wait_ge(s["up_used"], KT * b + KT)
                for n in range(2):
                    v = B[n][:, :].rearrange("p (j two) -> p two j", two=2)
                    TS(glu_t[:, 256 * n:256 * n + 256], v[:, 0, :], LIMIT, None, ALU.min)
                    last = TS(lin_t[:, 256 * n:256 * n + 256], v[:, 1, :], LIMIT, -LIMIT, ALU.min, ALU.max)
                last.then_inc(s["glu_sb"], 1)
                dve.wait_ge(s["glu_sb"], b + 2)
                STT(lin_t, lin_t, 1.0, glu_t, ALU.add, ALU.mult).then_inc(s["gated"], 1)
                dve.wait_ge(s["gated"], b + 1)
                dve.wait_ge(s["sig"], b + 1)
                TTo(act_s, lin_t, sig_t, ALU.mult).then_inc(s["act"], 1)
            dve.wait_ge(s["scat"], blocks + 1)
            for t in range(TT):
                for n in range(2):
                    TTo(hx[:, t, 512 * n:512 * n + 512], hx[:, t, 512 * n:512 * n + 512],
                        B[4 + 2 * t + n][:, :], ALU.add).then_inc(s["fin"], 1)


_INS = ["x", "norm1_g", "w_in", "b_gate", "ssm_a_re", "ssm_a_im", "ssm_log_dt", "ssm_b_re", "ssm_b_im",
        "ssm_c_re", "ssm_c_im", "ssm_d", "ssm_w_glu", "ssm_b_glu", "q_norm_g", "k_norm_g", "lambda_q1",
        "lambda_k1", "lambda_q2", "lambda_k2", "subln_g", "w_proj_ssm", "w_proj_att", "w_out", "norm2_g",
        "w_router", "b_router", "w_up", "b_up", "w_down", "b_down"]


def kernel(**inputs):
    import numpy as np
    import concourse.bacc as bacc
    from concourse.bass_utils import run_bass_kernel_spmd

    nc = bacc.Bacc("TRN2", target_bir_lowering=False, num_devices=1)
    arrays, aps = {}, {}
    for name in _INS:
        v = np.ascontiguousarray(inputs[name])
        arrays[f"in_{name}"] = v
        aps[name] = nc.dram_tensor(f"in_{name}", v.shape, mybir.dt.from_np(v.dtype), kind="ExternalInput").ap()
    out = nc.dram_tensor("out_y", (1, TOK, D), F32, kind="ExternalOutput").ap()
    mixer_and_experts(nc, aps, out)
    r = run_bass_kernel_spmd(nc, [arrays], core_ids=[0])
    return r.results[0]["out_y"]
```

```python
import math
from contextlib import ExitStack

import concourse.bass as bass
from concourse import mybir

ALU = mybir.AluOpType
ACT = mybir.ActivationFunctionType
F32 = mybir.dt.float32
I32 = mybir.dt.int32
U32 = mybir.dt.uint32
AX = mybir.AxisListType.X

P = 128
D = 1024
TOK = 256
TT = TOK // P
KT = D // P
G, PS, H = 32, 64, 16
GG = G // 2
S = G * H
L = P // H
NC = TOK // L
HEADS, SUB = 4, 64
AW = HEADS * 2 * SUB
WIN = S + 3 * AW + 2 * D
CHUNK = 64
E, TOPK = 32, 4
SLOTS = 64
EXTRA = TOK * TOPK // (SLOTS + 1)
TABLE = E + EXTRA + 1
ALPHA, LIMIT, EPS = 1.702, 7.0, 1e-6
LAMBDA_INIT = 0.8 - 0.6 * math.exp(0.0)
BIG = 1e30
ROUND = 1.5 * 2.0 ** 23
TWO_PI_1 = 6.28125
TWO_PI_2 = 0.0019350051879882812
TWO_PI_3 = 2 * math.pi - TWO_PI_1 - TWO_PI_2
PIECE = 256
PIECES = 25
LC = 3 * E
RING = 3

SEMS = """ident a_in c_in b_in vec_in d_in lam_in dve_step pool_step x_sq x_var x_rs xn xT_ps xT dt aT_in
 aT_ps cT_ps trig sincos win_t cp_ready u_sb u_out u_back q_sq v_sb qk_var qk_rs qk_tm wT_ps
 wT_sb kk_ps kk_sb kk_d m_zero m_in cp_zero U_ps U_sb st_ps st_sb sT_ps s_prev y_ps y_sb yT_ps
 gelu_sq gelu_w gelu_s yT glu_ps glu_s yg gate_sb qkT_ps qkT kz_fill score smax prob lam_e lam_n
 wt w_ps w_sb oT_ps o_sq o_ms o_var o_rs oT ps_ssm ps_att mixed h h_sq h_var h_rs hn hT_ps hT
 lg_ps top_e top_x gw rk_ps gT_ps gT bd_in bias_ps table_out table_in table bup_z sel xg_ps xg
 swt_ps swT glu_sb sig act aT2_ps aT2 ysb scat up_used dn_used bup_used dsel fin fin_out wr_in
 g2_in loop_z u_turn wg bb_rep gated cT g1_in gate_ps out_ps rank routed turns""".split()


def mixer_and_experts(nc, a, out):
    ctx = ExitStack()
    with ctx:
        KB = 256
        arena = ctx.enter_context(nc.sbuf_tensor("arena", [P, 207 * KB], F32))
        u_dram = nc.dram_tensor("u_scratch", (TOK, S), F32, kind="Internal").ap()
        table_dram = nc.dram_tensor("table_scratch", (P, 3), I32, kind="Internal").ap()

        def at(kb, *dims):
            n = 1
            for d in dims:
                n *= d
            o = int(kb * KB)
            v = arena[:, o:o + n]
            names = "abcd"[:len(dims)]
            if len(dims) > 1:
                v = v.rearrange(f"p ({' '.join(names)}) -> p {' '.join(names)}",
                                **{k: d for k, d in zip(names, dims)})
            return v

        up_w = at(0, KT, 2 * D)
        dn_w = at(64, KT, D)
        CW = 9 * H
        CR = at(0, GG, 2, CW)
        CI = at(18, GG, 2, CW)
        WR = at(36, GG, P)
        WI = at(44, GG, P)
        KK = at(36, G, P)
        WIN_M = at(52, GG, 2, P)
        MM = at(68, G, P)
        tA = at(68, GG, 9, H)
        tB = at(172, GG, 9, H)
        U = at(84, 8, 4, NC)
        uc = at(88, L, P)
        uc2 = at(92, 8, L, H)
        Y_sb = at(88, L, 4, 2, H)
        bbR, bbI = at(188, GG, L, H), at(172, GG, L, H)
        wg = at(112, 4, 4, P)
        u_tm = at(92, TT, S)
        S_sb = at(92, 4, 2, P)
        hx = at(96, TT, D)
        hn = at(104, TT, D)
        Rr, Ri = at(104, GG, NC), at(106, GG, NC)
        magz = at(108, GG, NC)
        bbr, bbi = at(110, GG, H), at(111, GG, H)
        oT = at(104, HEADS, TOK)
        o2 = at(108, HEADS, TOK)
        xnT = at(112, KT, TOK)
        stream = [at(120 + 8 * i, 8, PIECE) for i in range(RING)]
        last_piece = at(112, 8, PIECE)
        gates = at(144, 16, TOK)
        xn = at(144, TT, D)
        c_sb = at(152, 2, 4, 2, PS)
        br_raw, bi_raw = at(156, GG, H), at(157, GG, H)
        q_tm, k_tm = at(160, TT, AW), at(164, TT, AW)
        ge1, ge2 = at(160, L, 4, NC), at(164, L, 4, NC)
        o_rs = at(164, HEADS, TOK)
        v_tm = at(168, TT, AW)
        qz = at(172, 2, HEADS, TOK)
        kz = at(180, 2, HEADS, TOK)
        mixT = at(172, KT, TOK)
        mtmp = at(180, 2, 2 * TOK)
        prob = at(188, 2, 2 * TOK)
        wmix = at(192, 2, TOK)
        wTs = at(194, 2, 2, P)
        cTr, cTi = at(188, GG, H), at(189, GG, H)
        Pr, Pi = at(190, GG, 9), at(190.75, GG, 9)
        Vr, Vi = at(191.5, GG, L), at(192, GG, L)
        sc1, sc2, sc3, sc4 = [at(184 + i, GG, H) for i in range(4)]
        It = at(52, 4, GG, NC)
        Spr, Spi = at(196, GG, NC), at(198, GG, NC)
        dB, dd = at(196, G, H), at(198, G, H)
        yT = at(196, 4, TOK)
        ident = at(200, P)
        ones = at(200.5, P)
        ltri = at(201, P)
        iota = at(201.5, 5 * SLOTS)
        tq = at(202.75, TOK)
        tk = at(203.75, TOK)
        e0 = at(204.75, SLOTS)
        hsel = at(205, H)
        small = at(205.0625, 496)

        def sm(o, *dims):
            n = 1
            for d in dims:
                n *= d
            v = small[:, o:o + n]
            names = "abc"[:len(dims)]
            if len(dims) > 1:
                v = v.rearrange(f"p ({' '.join(names)}) -> p {' '.join(names)}",
                                **{k: d for k, d in zip(names, dims)})
            return v

        g1 = sm(0, KT)
        bgate = sm(8, 16)
        bglu = sm(24, 4)
        xs = sm(28, TT)
        xs2 = sm(290 + 160, TT, 2)
        xr = sm(30, TT)
        iop = sm(32, 1)
        lamv = sm(33, 8)
        subg = sm(41, 1)
        qg = sm(42, 1)
        kg = sm(43, 1)
        dts = sm(44, 2)
        pa = sm(48, 4, GG)
        tr = sm(112, 6, GG)
        mg = sm(208, 2, GG)
        qv = sm(240, 2, TT, 8)
        smx = sm(272, 2, 2)
        nmx = sm(276, 2, 2)
        rsum = sm(280, 2, 2)
        rinv = sm(284, 2, 2)
        warm = sm(288, 1)
        e8r, e8i = sm(290, GG), sm(306, GG)
        cfr, cfi = sm(322, GG), sm(338, GG)
        t16 = [sm(354 + 16 * i, GG) for i in range(6)]
        natA = at(158, 4, P)
        lamrow = at(198, 4, SUB)
        hT = at(180, KT, TOK)
        bup = at(120, 2 * D)
        bdn = at(128, D)
        xg = at(132, KT, SLOTS)
        act_s = at(134, 4 * P)
        glu_t = at(136, 4 * P)
        lin_t = at(138, 4 * P)
        sig_t = at(140, 4 * P)
        actT = at(142, 4, 2, SLOTS)
        y_s = at(144, 4 * P)
        selw = at(146, TT, P)
        swT0, swT1 = at(147, TT, P), at(148, TT, P)
        selg = at(149, TT, P)
        wr = at(188, KT, LC)
        brb = at(191, E)
        one_k = at(191.25, TT, E, TOPK)
        gw_k = at(192.25, TT, E, TOPK)
        R1 = at(193.25, LC)
        R2 = at(193.75, LC)
        lg = at(152, TT, E)
        top_v = at(152.25, TT, 8)
        top_f = at(152.375, TT, 8)
        top_w = at(152.5, TT, 8)
        gw = at(153, TT, E)
        rank = at(153.5, TT, E)
        cnt = at(153.75, E)
        ovf = at(153.875, E)
        ovt = at(154, E)
        cum = at(154.125, E)
        before = at(154.25, E)
        tabf = at(154.375, 16)
        gwT = at(155, TOK)
        g2b = at(156, D)
        table_row = at(150, 3 * P).bitcast(I32)      
        top_i = at(152.625, TT * 8).bitcast(U32).rearrange("p (t n) -> p t n", t=TT)
        table_i = at(152.75, 4).bitcast(I32)

        B = [ctx.enter_context(nc.psum_tensor(f"bank{i}", [P, 512], F32)) for i in range(8)]
        s = {n: ctx.enter_context(nc.semaphore(n)) for n in SEMS}
        x_in = [ctx.enter_context(nc.semaphore(f"x{t}_in")) for t in range(TT)]
        last_in = ctx.enter_context(nc.semaphore("last_piece_in"))
        slot_in = [ctx.enter_context(nc.semaphore(f"slot{i}_in")) for i in range(RING)]
        up_in = [ctx.enter_context(nc.semaphore(f"up{i}_in")) for i in range(KT)]
        dn_in = [ctx.enter_context(nc.semaphore(f"dn{i}_in")) for i in range(KT // 2)]
        piece_used = ctx.enter_context(nc.semaphore("piece_used"))
        bup_in = ctx.enter_context(nc.semaphore("bup_in"))

        def slot_of(i):
            return last_piece if i == PIECES - 1 else stream[i % RING]

        def piece(i):
            slot = slot_of(i)
            if i < 16:
                w = a["w_in"][0].rearrange("(k p) n -> p k n", p=P)
                return [(slot, w[:, :, i * PIECE:(i + 1) * PIECE])]
            if i == 16:
                v = slot.rearrange("p a b -> p (a b)").rearrange("p (q n) -> p q n", q=4)
                w = a["ssm_w_glu"][0]
                return [(v[32 * t:32 * t + 32], w[P * t:P * t + P].rearrange("(q r) n -> r q n", q=4))
                        for t in range(4)]
            if i < 19:
                v = slot.rearrange("p a b -> p (a b)").rearrange("p (q n) -> p q n", q=4)
                w = a["w_proj_ssm"][0][:, (i - 17) * 512:(i - 16) * 512]
                return [(v[32 * t:32 * t + 32], w[P * t:P * t + P].rearrange("(q r) n -> r q n", q=4))
                        for t in range(4)]
            if i < 21:
                v = slot.rearrange("p a b -> p (a b)").rearrange("p (q n) -> p q n", q=4)
                w = a["w_proj_att"][0].rearrange("(k p) n -> p k n", p=P)
                return [(v, w[:, :, (i - 19) * 512:(i - 18) * 512])]
            w = a["w_out"][0].rearrange("(k p) n -> p k n", p=P)
            return [(slot, w[:, :, (i - 21) * PIECE:(i - 20) * PIECE])]

        def pv(i):
            return stream[i % RING].rearrange("p a b -> p (a b)").rearrange("p (q n) -> p q n", q=4)

        w_up, w_dn, b_up = a["w_up"][0], a["w_down"][0], a["b_up"][0]
        pairs = [(gg, g2) for gg in range(GG) for g2 in range(2)]

        def probs(u, sub):
            return prob[:, u % 2, :].rearrange("p (s k) -> p s k", s=2)[:, sub, 0:P * (u % 2 + 1)]

        block = ctx.enter_context(nc.Block())


        @block.sync
        def _(sp):
            for t in range(TT):
                sp.dma_start(hx[:, t, :], a["x"][0, P * t:P * t + P, :]).then_inc(x_in[t], 16)
            sp.dma_start(g1, a["norm1_g"][0].rearrange("(k p) -> p k", p=P),
                         allow_slow_non_contiguous=True).then_inc(s["g1_in"], 16)
            for src, o in ((a["ssm_a_re"], 0), (a["ssm_a_im"], 1)):
                sp.dma_start(natA[0:GG, o, :], src[0].rearrange("(g t) p -> g (t p)", t=2))\
                  .then_inc(s["a_in"], 16)
            sp.dma_start(dts[0:GG], a["ssm_log_dt"][0].rearrange("(g t) -> g t", t=2))\
              .then_inc(s["a_in"], 16)
            for i in range(PIECES):
                if i == PIECES - 1:
                    sp.wait_ge(piece_used, 17)
                elif i >= RING:
                    sp.wait_ge(piece_used, i - RING + 1)
                arrived = last_in if i == PIECES - 1 else slot_in[i % RING]
                for dst, src in piece(i):
                    sp.dma_start(dst, src).then_inc(arrived, 16)
                if i == 0:
                    for n, half in enumerate((a["ssm_c_re"], a["ssm_c_im"])):
                        for dup in range(2):
                            sp.dma_start(c_sb[:, n, :, dup, :],
                                         half[0].rearrange("g h p -> (g h) p").rearrange("(i q) p -> q i p", q=P))\
                              .then_inc(s["c_in"], 16)
                if i == 2:
                    for dst, src in ((br_raw, a["ssm_b_re"]), (bi_raw, a["ssm_b_im"])):
                        sp.dma_start(dst, src[0].rearrange("(g t) p h -> (t p) g h", t=2))\
                          .then_inc(s["b_in"], 16)
                    for n, name in enumerate(("lambda_q1", "lambda_k1", "lambda_q2", "lambda_k2")):
                        sp.dma_start(lamrow[:, n, :], a[name][0:1, :].to_broadcast([P, SUB]))\
                          .then_inc(s["lam_in"], 16)
                    sp.dma_start(dB.rearrange("p g h -> p (g h)"), a["ssm_d"][0:1, :].to_broadcast([P, S]))\
                      .then_inc(s["d_in"], 16)
                    sp.dma_start(bgate, a["b_gate"][0].rearrange("(n p) -> p n", p=P),
                                 allow_slow_non_contiguous=True).then_inc(s["vec_in"], 16)
                    sp.dma_start(subg, a["subln_g"][0].rearrange("(p o) -> p o", o=1)).then_inc(s["vec_in"], 16)
                    for t in range(4):
                        sp.dma_start(bglu[32 * t:32 * t + 32],
                                     a["ssm_b_glu"][0][P * t:P * t + P].rearrange("(q r) -> r q", q=4),
                                     allow_slow_non_contiguous=True).then_inc(s["vec_in"], 16)
                    for t in range(2):
                        for dst, name in ((qg, "q_norm_g"), (kg, "k_norm_g")):
                            sp.dma_start(dst[64 * t:64 * t + 64], a[name][0].rearrange("(p o) -> p o", o=1))\
                              .then_inc(s["vec_in"], 16)
                if i == 16:
                    sp.wait_ge(s["y_ps"], 1)
                    sp.wait_ge(s["yT_ps"], 2)
                if i >= 16:
                    k = i - 16
                    if k < KT:
                        sp.dma_start(up_w[:, k, :], w_up[0, P * k:P * k + P, :]).then_inc(up_in[k], 16)
                    if k >= 5:
                        j = k - 5
                        sp.dma_start(dn_w[:, 2 * j:2 * j + 2, :],
                                     w_dn[0, 2 * P * j:2 * P * (j + 1), :].rearrange("(k p) n -> p k n", p=P))\
                          .then_inc(dn_in[j], 16)
            sp.wait_ge(s["bup_z"], 1)
            sp.dma_start(bup[0:1, :], b_up[0:1, :]).then_inc(bup_in, 16)

            def load_block(b, e):
                sp.wait_ge(s["bup_used"], b)
                sp.dma_start(bup[0:1, :], b_up[bass.ds(e, 1), :]).then_inc(bup_in, 16)
                for k in range(KT):
                    sp.wait_ge(s["up_used"], KT * b - KT + k + 1)
                    sp.dma_start(up_w[:, k, :],
                                 w_up[bass.ds(e, 1), P * k:P * k + P, :].rearrange("o p n -> p (o n)"))\
                      .then_inc(up_in[k], 16)
                for j in range(KT // 2):
                    sp.wait_ge(s["dn_used"], 4 * b - 4 + j + 1)
                    sp.dma_start(dn_w[:, 2 * j:2 * j + 2, :],
                                 w_dn[bass.ds(e, 1), 2 * P * j:2 * P * (j + 1), :]
                                 .rearrange("o (k p) n -> p (o k) n", p=P)).then_inc(dn_in[j], 16)

            load_block(1, 1)
            sp.wait_ge(s["table_in"], 16)
            blocks = sp.value_load(table_row[0:1, 2:3], min_val=E, max_val=E + EXTRA)
            with sp.Fori(2, blocks) as b:
                load_block(b, sp.value_load(table_row[0:1, bass.ds(3 * b, 1)], min_val=0, max_val=E - 1))
            for t in range(TT):
                for n in range(2):
                    sp.wait_ge(s["fin"], 2 * t + n + 1)
                    sp.dma_start(out[0, P * t:P * t + P, 512 * n:512 * n + 512],
                                 hx[:, t, 512 * n:512 * n + 512]).then_inc(s["fin_out"], 16)
            sp.wait_ge(s["fin_out"], 64)

        @block.gpsimd
        def _(pool):
            steps = [0]

            def link(ins):
                steps[0] += 1
                ins.then_inc(s["pool_step"], 1)
                pool.wait_ge(s["pool_step"], steps[0])

            link(pool.memset(ident, 0.0))
            pool.affine_select(out=ident, in_=ident, compare_op=ALU.not_equal, fill=1.0, base=0,
                               pattern=[[-1, P]], channel_multiplier=1).then_inc(s["ident"], 1)
            pool.memset(ltri, 1.0)
            pool.memset(tq, 0.0)
            pool.memset(tk, 0.0)
            pool.memset(e0, 0.0)
            link(pool.memset(ones, 1.0))
            link(pool.affine_select(out=ltri, in_=ltri, compare_op=ALU.is_gt, fill=0.0, base=0,
                                    pattern=[[1, P]], channel_multiplier=-1))
            for half in range(2):
                lo = 64 * half
                for row in range(2):
                    q0, k0 = P * row, P * row + CHUNK
                    pool.affine_select(out=tq[lo:lo + 64, q0:q0 + CHUNK], in_=tq[lo:lo + 64, q0:q0 + CHUNK],
                                       compare_op=ALU.not_equal, fill=1.0, base=-row,
                                       pattern=[[0, CHUNK]], channel_multiplier=1)
                    last = pool.affine_select(out=tk[lo:lo + 64, k0:k0 + CHUNK],
                                              in_=tk[lo:lo + 64, k0:k0 + CHUNK],
                                              compare_op=ALU.not_equal, fill=-BIG, base=-row,
                                              pattern=[[0, CHUNK]], channel_multiplier=1)
                link(last)
            link(pool.memset(e0[0:1, :], 1.0))
            pool.iota(iota, pattern=[[1, 5 * SLOTS]], base=0, channel_multiplier=0,
                      allow_small_or_imprecise_dtypes=True)
            link(pool.iota(iop, pattern=[[0, 1]], base=-E, channel_multiplier=1,
                           allow_small_or_imprecise_dtypes=True))
            pool.memset(CR[0:64, :, 1, :], 0.0)
            link(pool.memset(CI[0:64, :, 1, :], 0.0))
            pool.memset(CR[64:P, :, 0, :], 0.0)
            pool.memset(CI[64:P, :, 0, :], 0.0).then_inc(s["cp_zero"], 1)
            pool.wait_ge(s["u_sb"], 2)
            pool.dma_start(u_dram.rearrange("(t p) n -> p t n", p=P), u_tm).then_inc(s["u_out"], 16)
            pool.wait_ge(s["u_out"], 16)
            for j in range(4):
                pool.dma_start(uc[32 * j:32 * j + 32],
                               u_dram[:, P * j:P * j + P].rearrange("(c s) n -> c s n", s=L))\
                    .then_inc(s["u_back"], 16)
            pool.wait_ge(s["win_t"], 1)
            for dst, src in ((bbR, bbr), (bbI, bbi)):
                pool.tensor_copy(dst, src.unsqueeze(2).to_broadcast([P, GG, L, H])).then_inc(s["bb_rep"], 1)
            pool.memset(MM, 0.0).then_inc(s["m_zero"], 1)
            pool.wait_ge(s["m_zero"], 1)
            pool.wait_ge(s["kk_ps"], 8)
            pool.wait_ge(s["turns"], 1)
            for t, lo in ((0, 64), (1, 0)):
                pool.tensor_copy(qz[lo:lo + 64, t], tq[lo:lo + 64].unsqueeze(1).to_broadcast([64, HEADS, TOK]))
                pool.tensor_copy(kz[lo:lo + 64, t], tk[lo:lo + 64].unsqueeze(1).to_broadcast([64, HEADS, TOK]))\
                    .then_inc(s["kz_fill"], 1)
                pool.wait_ge(s["kz_fill"], t + 1)
            pool.wait_ge(s["kk_d"], 1)
            for t in range(L):
                pool.dma_start(MM[H * t:H * t + H, :, H * t:P], KK[H * t:H * t + H, :, 0:P - H * t])\
                    .then_inc(s["m_in"], 16)
            pool.wait_ge(s["mixed"], 4)
            link(pool.memset(wr, 0.0))
            pool.memset(R1, 0.0)
            link(pool.memset(R2, 0.0))
            pool.dma_start(wr[:, :, 0:E], a["w_router"][0].rearrange("(k p) n -> p k n", p=P))\
                .then_inc(s["wr_in"], 16)
            pool.dma_start(brb, a["b_router"][0:1, :].to_broadcast([P, E])).then_inc(s["wr_in"], 16)
            pool.dma_start(g2b, a["norm2_g"][0:1, :].to_broadcast([P, D])).then_inc(s["g2_in"], 16)
            pool.wait_ge(s["out_ps"], 4)
            pool.memset(bup, 0.0).then_inc(s["bup_z"], 1)
            pool.memset(bdn, 0.0)
            pool.memset(gwT, 0.0)
            pool.memset(swT0, 0.0)
            link(pool.memset(swT1, 0.0))
            pool.dma_start(bdn[0:E, :], a["b_down"][0]).then_inc(s["bd_in"], 16)
            pool.memset(iota[:, 4 * SLOTS:], 4.0 * TOK).then_inc(s["loop_z"], 1)
            pool.wait_ge(s["table"], 1)
            pool.dma_start(table_dram, table_i[:, 0:3]).then_inc(s["table_out"], 16)
            pool.wait_ge(s["table_out"], 16)
            pool.dma_start(table_row[0:1, :], table_dram.rearrange("(o q) c -> o (q c)", o=1))\
                .then_inc(s["table_in"], 16)

        @block.tensor
        def _(pe):
            def piece_arrived(i):
                if i == PIECES - 1:
                    pe.wait_ge(last_in, 16)
                    return
                pe.wait_ge(slot_in[i % RING], 16 * sum(len(piece(j)) for j in range(i % RING, i + 1, RING)))

            def transposes(jobs):
                for dst, src in jobs:
                    last = pe.transpose(dst, src, ident[0:src.shape[0], 0:src.shape[0]])
                return last

            pe.wait_ge(s["ident"], 1)
            pe.wait_ge(s["aT_in"], 1)
            transposes([(B[4][:, GG * i:GG * i + GG], natA[0:GG, i, :]) for i in range(4)])\
                .then_inc(s["aT_ps"], 1)
            pe.wait_ge(s["c_in"], 64)
            for ri in range(2):
                transposes([(B[5 + ri][:, P * i:P * i + P], c_sb[:, ri, i].rearrange("p d n -> p (d n)"))
                            for i in range(4)]).then_inc(s["cT_ps"], 1)
            pe.wait_ge(s["xn"], 2)
            for t in range(TT):
                for half in range(2):
                    transposes([(B[2 * t + half][:, P * k:P * k + P],
                                 xn[:, t, P * (4 * half + k):P * (4 * half + k) + P]) for k in range(4)])\
                        .then_inc(s["xT_ps"], 1)
            pe.wait_ge(s["xT"], 4)

            def z_columns(first, banks):
                for i in (first, first + 1):
                    piece_arrived(i)
                    w, c = stream[i % RING], PIECE * (i - first)
                    for t in range(TT):
                        for k in range(KT):
                            last = pe.matmul(B[banks[t]][:, c:c + PIECE], xnT[:, k, P * t:P * t + P],
                                             w[:, k, :], start=(k == 0), stop=(k == KT - 1))
                    last.then_inc(piece_used, 1)

            z_columns(0, (0, 1))
            z_columns(2, (2, 3))
            pe.wait_ge(s["cT"], 1)
            z_columns(4, (4, 5))
            z_columns(6, (6, 7))


            def gate_tile(n):
                i = 8 + n // 2
                piece_arrived(i)
                if n < 2:
                    pe.wait_ge(s["u_sb"], n + 1)
                else:
                    pe.wait_ge(s["gate_sb"], n - 1)
                for k in range(KT):
                    last = pe.matmul(B[n % 2][:, 0:TOK], slot_of(i)[:, k, P * (n % 2):P * (n % 2) + P],
                                     xnT[:, k, :], start=(k == 0), stop=(k == KT - 1))
                last.then_inc(s["gate_ps"] if n % 2 == 0 else piece_used, 1)

            for n in (0, 1):
                gate_tile(n)
            pe.wait_ge(s["win_t"], 1)
            pe.wait_ge(s["qk_tm"], 4)
            pe.wait_ge(s["v_sb"], 2)
            for f in range(8):
                if f >= 4:
                    pe.wait_ge(s["wT_sb"], f - 3)
                transposes([(B[4 + f % 4][:, P * m:P * m + P], (WR, WI)[m % 2][:, 2 * f + m // 2, :])
                            for m in range(4)]).then_inc(s["wT_ps"], 1)
            pe.wait_ge(s["bb_rep"], 2)
            for f in range(8):
                if f < 4:
                    pe.wait_ge(s["wT_sb"], 5 + f)
                else:
                    pe.wait_ge(s["kk_sb"], f - 3)
                for gg in (2 * f, 2 * f + 1):
                    o = B[4 + f % 4][:, 256 * (gg % 2):256 * (gg % 2) + 256]
                    for n, (bb, cc) in enumerate(((bbR, CR), (bbI, CI))):
                        last = pe.matmul(o, bb[:, gg].rearrange("p s h -> p (s h)"),
                                         cc[:, gg, :, 0:P], start=(n == 0), stop=(n == 1))
                last.then_inc(s["kk_ps"], 1)
            pe.wait_ge(s["u_turn"], 1)
            pe.wait_ge(s["kk_sb"], 6)
            for r in range(8):
                last = transposes([(B[4 + r // 4][:, P * (r % 4):P * (r % 4) + P], uc2[:, r].rearrange("p s h -> p (s h)"))])
                if r % 4 == 3:
                    last.then_inc(s["U_ps"], 1)
            pe.wait_ge(s["U_sb"], 2)
            pe.wait_ge(s["kk_sb"], 8)
            for i in range(GG):
                slot, q = i // 4, i % 4
                for g2 in range(2):
                    g = 2 * i + g2
                    o = B[6 + slot // 2][32 * q:32 * q + 32, 256 * (slot % 2):256 * (slot % 2) + 256]\
                        .rearrange("p (r n) -> p r n", r=2)[:, :, 64 * g2:64 * g2 + 64]
                    last = pe.matmul(o, U[:, g % 8, g // 8, :], WIN_M[:, i, :, 64 * g2:64 * g2 + 64],
                                     start=True, stop=True, tile_position=(0, 32 * q))
                if i % 8 == 7:
                    last.then_inc(s["st_ps"], 1)

            pe.wait_ge(s["qk_tm"], 4)
            for n, src in enumerate((q_tm, k_tm)):
                for t in range(TT):
                    if n == 1:
                        pe.wait_ge(s["qkT"], t + 1)
                    transposes([(B[2 + t][:, P * h:P * h + P], src[:, t, P * h:P * h + P])
                                for h in range(HEADS)]).then_inc(s["qkT_ps"], 1)
            pe.wait_ge(s["st_sb"], 2)
            for ri in range(2):
                transposes([(B[4 + ri][:, P * m:P * m + P], S_sb[:, m, ri, :]) for m in range(4)])\
                    .then_inc(s["sT_ps"], 1)
            for n in (2, 3):
                gate_tile(n)

            def chunk_outputs():
                pe.wait_ge(s["m_in"], 16 * L)
                for i in range(GG):
                    slot, q = i // 4, i % 4
                    o = B[6 + slot // 2][32 * q:32 * q + 32, 256 * (slot % 2):256 * (slot % 2) + 256]
                    pe.matmul(o, Spr[:, i, :], CR[:, i, :, H:H + P], start=True, stop=False,
                              skip_group_check=True)
                    pe.matmul(o, Spi[:, i, :], CI[:, i, :, H:H + P], start=False, stop=False,
                              skip_group_check=True)
                    for g2 in range(2):
                        g = 2 * i + g2
                        last = pe.matmul(o[:, P * g2:P * g2 + P], U[:, g % 8, g // 8, :], MM[:, g, :],
                                         start=False, stop=(g2 == 1), skip_group_check=True)
                    if i % 8 == 7:
                        last.then_inc(s["y_ps"], 1)

            def turn_y():
                pe.wait_ge(s["y_sb"], 4)
                for t in range(L):
                    last = transposes([(B[6 + t // 4][:, P * (t % 4):P * (t % 4) + P],
                                        Y_sb[:, t].rearrange("p a b h -> p (a b h)"))])
                    if t % 4 == 3:
                        last.then_inc(s["yT_ps"], 1)

            units = [(h, t) for h in range(HEADS) for t in range(TT)]

            def scores(u):
                h, t = units[u]
                if u < 2:
                    pe.wait_ge(s["qkT"], 4)
                else:
                    pe.wait_ge(s["w_sb"], u - 1)
                for sub in range(2):
                    last = pe.matmul(B[2 + u % 2][:, TOK * sub:TOK * sub + P * (t + 1)],
                                     qz[:, sub, h, P * t:P * t + P], kz[:, sub, h, 0:P * (t + 1)],
                                     start=True, stop=True)
                last.then_inc(s["score"], 1)

            def turn_w(u):
                h, t = units[u]
                pe.wait_ge(s["wt"], u + 1)
                transposes([(B[2 + u % 2][:, P * j:P * j + P], wmix[:, u % 2, P * j:P * j + P])
                            for j in range(t + 1)]).then_inc(s["w_ps"], 1)

            def values(u):
                h, t = units[u]
                pe.wait_ge(s["w_sb"], u + 1)
                if u == 0:
                    pe.wait_ge(s["s_prev"], 1)
                for j in range(t + 1):
                    last = pe.matmul(B[4 + h // 2][:, TOK * (h % 2) + P * t:TOK * (h % 2) + P * t + P],
                                     v_tm[:, j, P * h:P * h + P], wTs[:, u % 2, j, :],
                                     start=(j == 0), stop=(j == t))
                last.then_inc(s["oT_ps"], 1)

            def glu():
                pe.wait_ge(s["wg"], 1)
                pe.wait_ge(s["yT"], 2)
                for q2 in range(4):
                    for q in range(4):
                        last = pe.matmul(B[q2 // 2][:, TOK * (q2 % 2):TOK * (q2 % 2) + TOK],
                                         wg[:, q, q2, :],
                                         yT[:, q, :], start=(q == 0), stop=(q == 3))
                    if q2 == 1:
                        last.then_inc(s["glu_ps"], 1)
                last.then_inc(piece_used, 1)

            for h in range(HEADS):
                scores(2 * h)
                scores(2 * h + 1)
                gate_tile(3 * h + 4)
                gate_tile(3 * h + 5)
                turn_w(2 * h)
                turn_w(2 * h + 1)
                gate_tile(3 * h + 6)
                values(2 * h)
                values(2 * h + 1)
                if h == 1:
                    chunk_outputs()
                elif h == 2:
                    turn_y()
            pe.wait_ge(s["o_sq"], 2)
            pe.wait_ge(s["w_sb"], 8)
            for m in range(2):
                pe.matmul(B[2 + m][:, :], ones, o2[:, 2 * m:2 * m + 2, :],
                          start=True, stop=True).then_inc(s["o_ms"], 1)
            pe.wait_ge(s["gate_sb"], 16)
            glu()
            pe.wait_ge(s["yg"], 1)
            for n in range(KT):
                if n % 4 == 0:
                    piece_arrived(17 + n // 4)
                if n == 0:
                    pe.wait_ge(s["glu_s"], 4)
                    pe.wait_ge(s["o_var"], 1)
                for q in range(4):
                    last = pe.matmul(B[n // 2][:, TOK * (n % 2):TOK * (n % 2) + TOK],
                                     pv(17 + n // 4)[:, q, P * (n % 4):P * (n % 4) + P], yT[:, q, :],
                                     start=(q == 0), stop=(q == 3))
                if n % 4 == 3:
                    last.then_inc(piece_used, 1)
                elif n % 2 == 1:
                    last.then_inc(s["ps_ssm"], 1)
            pe.wait_ge(s["oT"], 1)
            for n in range(KT):
                if n % 4 == 0:
                    piece_arrived(19 + n // 4)
                for q in range(4):
                    last = pe.matmul(B[4 + n // 2][:, TOK * (n % 2):TOK * (n % 2) + TOK],
                                     pv(19 + n // 4)[:, q, P * (n % 4):P * (n % 4) + P], oT[:, q, :],
                                     start=(q == 0), stop=(q == 3))
                if n % 4 == 3:
                    last.then_inc(piece_used, 1)
                elif n % 2 == 1:
                    last.then_inc(s["ps_att"], 1)
            pe.wait_ge(s["mixed"], 4)

            def turn_h(t):
                pe.wait_ge(s["hn"], t + 1)
                for half in range(2):
                    if t == 1:
                        pe.wait_ge(s["hT"], half + 1)
                    transposes([(B[4 + half][:, P * k:P * k + P],
                                 hn[:, t, P * (4 * half + k):P * (4 * half + k) + P]) for k in range(4)])\
                        .then_inc(s["hT_ps"], 1)

            def logits(t):
                pe.wait_ge(s["hT"], 2 * t + 2)
                pe.wait_ge(s["wr_in"], 32)
                for k in range(KT):
                    last = pe.matmul(B[6 + t][:, 0:LC], hT[:, k, P * t:P * t + P], wr[:, k, :],
                                     start=(k == 0), stop=(k == KT - 1))
                last.then_inc(s["lg_ps"], 1)

            for t in range(TT):
                for i in range(21, PIECES):
                    piece_arrived(i)
                    c = i - 21
                    for k in range(KT):
                        last = pe.matmul(B[2 * t + c // 2][:, PIECE * (c % 2):PIECE * (c % 2) + PIECE],
                                         mixT[:, k, P * t:P * t + P], slot_of(i)[:, k, :],
                                         start=(k == 0), stop=(k == KT - 1))
                    if c % 2 == 1:
                        last.then_inc(s["out_ps"], 1)
                    if t == 1 and c == 1:
                        turn_h(0)
                    if t == 1 and c == 2:
                        logits(0)
            turn_h(1)
            logits(1)
            pe.wait_ge(s["routed"], 1)
            o = B[0][:, 0:LC]
            pe.matmul(o, ltri, R1, start=True, stop=False)
            pe.matmul(o, ones, R2, start=False, stop=True).then_inc(s["rk_ps"], 1)
            def gather(nth, turned=None):
                pe.wait_ge(s["sel"], nth)
                for k in range(KT):
                    if k == 4 and turned is not None:
                        pe.wait_ge(s["swT"], turned)
                    for t in range(TT):
                        last = pe.matmul(B[2 + k // 4][:, P * (k % 4):P * (k % 4) + P],
                                         hn[:, t, P * k:P * k + P], selg[:, t, :],
                                         start=(t == 0), stop=(t == TT - 1))
                    if k % 4 == 3:
                        last.then_inc(s["xg_ps"], 1)

            def scatter():
                for t in range(TT):
                    for n, sw in enumerate((swT0, swT1)):
                        last = pe.matmul(B[4 + 2 * t + n][:, :], sw[:, t, :], y_s, start=False, stop=False,
                                         skip_group_check=True)
                last.then_inc(s["scat"], 1)

            def turn_weights():
                pe.wait_ge(s["gw"], 1)
                transposes([(B[3][0:E, P * t:P * t + P], gw[:, t, :]) for t in range(TT)]).then_inc(s["gT_ps"], 1)

            def weighted_biases():
                pe.wait_ge(s["gT"], 1)
                pe.wait_ge(s["bd_in"], 16)
                for t in range(TT):
                    for n in range(2):
                        last = pe.matmul(B[4 + 2 * t + n][:, :], gwT[:, P * t:P * t + P],
                                         bdn[:, 512 * n:512 * n + 512], start=True, stop=False,
                                         skip_group_check=True)
                last.then_inc(s["bias_ps"], 1)

            def expert_block(b, first=False):
                pe.wait_ge(bup_in, 16 * b + 16)
                if not first:
                    pe.wait_ge(s["glu_sb"], b)
                pe.wait_ge(s["xg"], 2 * b + 2)
                for n in range(2):
                    for h in range(2):
                        last = pe.matmul(B[n][64 * h:64 * h + 64, :], e0,
                                         bup[:, D * h + 512 * n:D * h + 512 * n + 512],
                                         start=True, stop=False, skip_group_check=True)
                last.then_inc(s["bup_used"], 1)
                if first:
                    turn_weights()
                for k in range(KT):
                    pe.wait_ge(up_in[k], 16 * b + 16)
                    for n in range(2):
                        for h in range(2):
                            last = pe.matmul(B[n][64 * h:64 * h + 64, :], xg[:, k, :],
                                             up_w[:, k, D * h + 512 * n:D * h + 512 * n + 512],
                                             start=False, stop=(k == KT - 1), skip_group_check=True)
                    last.then_inc(s["up_used"], 1)
                if first:
                    weighted_biases()
                else:
                    pe.wait_ge(s["ysb"], b)
                    scatter()
                pe.wait_ge(s["dsel"], b + 1)
                transposes([(B[3][:, P * t:P * t + P], selw[:, t, :]) for t in range(TT)])\
                    .then_inc(s["swt_ps"], 1)
                gather(b + 2, b + 1)
                pe.wait_ge(s["act"], b + 1)
                pe.wait_ge(s["xg"], 2 * b + 3)
                transposes([(B[2][:, P * j:P * j + P], act_s[:, P * j:P * j + P]) for j in range(4)])\
                    .then_inc(s["aT2_ps"], 1)
                pe.wait_ge(s["aT2"], b + 1)
                pe.wait_ge(s["xg"], 2 * b + 4)
                for k in range(KT):
                    if k % 2 == 0:
                        pe.wait_ge(dn_in[k // 2], 16 * b + 16)
                    for n in range(2):
                        last = pe.matmul(B[3][64 * n:64 * n + 64, :], actT[:, k % 4, k // 4, :],
                                         dn_w[:, k, 512 * n:512 * n + 512],
                                         start=(k == 0), stop=(k == KT - 1), skip_group_check=True)
                    if k % 2 == 1:
                        last.then_inc(s["dn_used"], 1)

            pe.wait_ge(s["rank"], 1)
            gather(1)
            expert_block(0, first=True)
            pe.wait_ge(s["table_in"], 16)
            blocks = pe.value_load(table_row[0:1, 2:3], min_val=E, max_val=E + EXTRA)
            with pe.Fori(1, blocks) as b:
                expert_block(b)
            pe.wait_ge(s["ysb"], blocks)
            scatter()

        @block.scalar
        def _(act):
            for t in range(TT):
                act.wait_ge(x_in[t], 16)
                act.activation(xn[:, t, :], hx[:, t, :], ACT.Square, accum_out=xs[:, t:t + 1])\
                    .then_inc(s["x_sq"], 1)
            act.wait_ge(s["x_var"], 1)
            act.activation(xr, xs, ACT.Sqrt).then_inc(s["x_rs"], 1)
            act.wait_ge(s["a_in"], 48)
            act.activation(dts[0:GG], dts[0:GG], ACT.Exp).then_inc(s["dt"], 1)
            act.wait_ge(s["trig"], 1)
            act.activation(mg[:, 0, :], pa[:, 2, :], ACT.Exp)
            act.activation(mg[:, 1, :], pa[:, 2, :], ACT.Exp, scale=float(L))
            act.activation(tr[:, 3, :], tr[:, 2, :], ACT.Sin)
            act.activation(tr[:, 4, :], tr[:, 1, :], ACT.Sin).then_inc(s["sincos"], 1)
            for t in range(TT):
                act.wait_ge(piece_used, 2)
                act.activation(u_tm[:, t, :], B[t][:, :], ACT.Copy).then_inc(s["u_sb"], 1)
            act.wait_ge(s["lam_e"], 1)
            act.activation(lamv[:, 0:2], lamv[:, 2:4], ACT.Exp).then_inc(s["lam_n"], 1)
            for n, dst in enumerate((q_tm, k_tm)):
                act.wait_ge(piece_used, 4 + 2 * n)
                for t in range(TT):
                    act.activation(dst[:, t, :], B[2 + 2 * n + t][:, :], ACT.Square)\
                        .then_inc(s["q_sq"], 1)
            act.wait_ge(piece_used, 8)
            for t in range(TT):
                act.activation(v_tm[:, t, :], B[6 + t][:, :], ACT.Copy).then_inc(s["v_sb"], 1)
            act.wait_ge(s["qk_var"], 1)
            act.activation(qv, qv, ACT.Sqrt).then_inc(s["qk_rs"], 1)
            act.wait_ge(s["vec_in"], 16 * 10)

            def gate(n):
                if n % 2 == 0:
                    act.wait_ge(s["gate_ps"], n // 2 + 1)
                else:
                    act.wait_ge(piece_used, 9 + n // 2)
                act.activation(gates[:, n, :], B[n % 2][:, 0:TOK],
                               ACT.Sigmoid, bias=bgate[:, n:n + 1]).then_inc(s["gate_sb"], 1)

            for n in range(2):
                gate(n)
            for f in range(8):
                act.wait_ge(s["wT_ps"], f + 1)
                act.activation(WIN_M[:, 2 * f:2 * f + 2].rearrange("p a b c -> p (a b c)"),
                               B[4 + f % 4][:, :], ACT.Copy).then_inc(s["wT_sb"], 1)
            act.wait_ge(s["u_back"], 64)
            act.activation(uc2.rearrange("p r s h -> p s r h"), uc.rearrange("p s (r h) -> p s r h", h=H),
                           ACT.Copy).then_inc(s["u_turn"], 1)
            for f in range(8):
                act.wait_ge(s["kk_ps"], f + 1)
                act.activation(KK[:, 4 * f:4 * f + 4].rearrange("p a b -> p (a b)"),
                               B[4 + f % 4][:, :], ACT.Copy).then_inc(s["kk_sb"], 1)
            for m in range(2):
                act.wait_ge(s["U_ps"], m + 1)
                act.activation(U[:, 4 * m:4 * m + 4].rearrange("p a b c -> p (a b c)"),
                               B[4 + m][:, :], ACT.Copy).then_inc(s["U_sb"], 1)
            for m in range(2):
                act.wait_ge(s["st_ps"], m + 1)
                act.activation(S_sb[:, 2 * m:2 * m + 2].rearrange("p a b c -> p (a b c)"),
                               B[6 + m][:, :], ACT.Copy).then_inc(s["st_sb"], 1)
            for n in (2, 3):
                gate(n)

            def chunk_outputs():
                for m in range(2):
                    act.wait_ge(s["y_ps"], m + 1)
                    for i in range(2):
                        act.activation(Y_sb[:, :, 2 * m + i].rearrange("p t g h -> p g t h"),
                                       B[6 + m][:, 256 * i:256 * i + 256]
                                       .rearrange("p (g t h) -> p g t h", g=2, h=H),
                                       ACT.Copy).then_inc(s["y_sb"], 1)

            def gelu_squares():
                for m in range(2):
                    act.wait_ge(s["yT_ps"], m + 1)
                    act.wait_ge(s["qkT_ps"], 4)
                    act.activation(ge1[:, 4 * m:4 * m + 4].rearrange("p a b c -> p (a b c)"),
                                   B[6 + m][:, :], ACT.Square).then_inc(s["gelu_sq"], 1)

            def softmax(u):
                t = u % 2
                act.wait_ge(s["smax"], u + 1)
                if u < 2:
                    act.wait_ge(s["kk_ps"], 8)
                else:
                    act.wait_ge(s["wt"], u - 1)
                for sub in range(2):
                    act.activation(probs(u, sub), B[2 + u % 2][:, TOK * sub:TOK * sub + P * (t + 1)], ACT.Exp,
                                   bias=nmx[:, u % 2, sub:sub + 1], scale=SUB ** -0.5,
                                   accum_out=rsum[:, u % 2, sub:sub + 1]).then_inc(s["prob"], 1)

            def turned(u):
                t = u % 2
                act.wait_ge(s["w_ps"], u + 1)
                if u >= 2:
                    act.wait_ge(s["oT_ps"], u - 1)
                act.activation(wTs[:, u % 2, 0:t + 1, :].rearrange("p a b -> p (a b)"),
                               B[2 + u % 2][:, 0:P * (t + 1)], ACT.Copy).then_inc(s["w_sb"], 1)

            def glu_sigmoid():
                for q in range(4):
                    if q == 0:
                        act.wait_ge(s["glu_ps"], 1)
                    if q == 2:
                        act.wait_ge(piece_used, 17)
                    act.activation(ge1[:, 2 * q:2 * q + 2].rearrange("p a b c -> p (a b c)"),
                                   B[q // 2][:, TOK * (q % 2):TOK * (q % 2) + TOK],
                                   ACT.Sigmoid, bias=bglu[:, q:q + 1]).then_inc(s["glu_s"], 1)

            for h in range(HEADS):
                softmax(2 * h)
                softmax(2 * h + 1)
                gate(3 * h + 4)
                gate(3 * h + 5)
                turned(2 * h)
                turned(2 * h + 1)
                gate(3 * h + 6)
                if h == 1:
                    chunk_outputs()
                elif h == 2:
                    gelu_squares()
            act.wait_ge(piece_used, 16)
            act.wait_ge(slot_in[16 % RING], 16 * sum(len(piece(j)) for j in range(16 % RING, 17, RING)))
            for q in range(4):
                last = act.activation(wg[:, q].rearrange("p c (t r) -> p c t r", t=4),
                                      pv(16)[:, q, :].rearrange("p (t c r) -> p c t r", t=4, c=4), ACT.Copy)
            last.then_inc(s["wg"], 1)
            for m in range(2):
                act.wait_ge(s["gelu_w"], m + 1)
                act.activation(ge2[:, 4 * m:4 * m + 4].rearrange("p a b c -> p (a b c)"),
                               ge1[:, 4 * m:4 * m + 4].rearrange("p a b c -> p (a b c)"),
                               ACT.Sigmoid, scale=2 * math.sqrt(2 / math.pi)).then_inc(s["gelu_s"], 1)
            for m in range(2):
                act.wait_ge(s["oT_ps"], 4 * m + 4)
                act.activation(o2[:, 2 * m:2 * m + 2, :].rearrange("p a b -> p (a b)"), B[4 + m][:, :],
                               ACT.Square).then_inc(s["o_sq"], 1)
            glu_sigmoid()
            act.wait_ge(s["o_var"], 1)
            act.activation(o_rs, o_rs, ACT.Sqrt).then_inc(s["o_rs"], 1)
            for t in range(TT):
                for half in range(2):
                    act.wait_ge(s["h"], 2 * t + half + 1)
                    act.activation(hn[:, t, 512 * half:512 * half + 512], hx[:, t, 512 * half:512 * half + 512],
                                   ACT.Square, accum_out=xs2[:, t, half:half + 1]).then_inc(s["h_sq"], 1)
                act.wait_ge(s["h_var"], t + 1)
                act.activation(xr[:, t:t + 1], xs[:, t:t + 1], ACT.Sqrt).then_inc(s["h_rs"], 1)
                for half in range(2):
                    act.wait_ge(s["hT_ps"], 2 * t + half + 1)
                    act.activation(hT[:, 4 * half:4 * half + 4, P * t:P * t + P],
                                   B[4 + half][:, :].rearrange("p (k n) -> p k n", k=4),
                                   ACT.Copy).then_inc(s["hT"], 1)
            act.wait_ge(s["top_e"], 1)
            for t in range(TT):
                act.activation(top_w[:, t, 0:TOPK], top_v[:, t, 0:TOPK], ACT.Exp,
                               bias=xs[:, t:t + 1], accum_out=xr[:, t:t + 1]).then_inc(s["top_x"], 1)

            def gathered(nth):
                for n in range(2):
                    act.wait_ge(s["xg_ps"], 2 * nth - 1 + n)
                    act.activation(xg[:, 4 * n:4 * n + 4, :],
                                   B[2 + n][:, :].rearrange("p (k c) -> p k c", k=4)[:, :, 0:SLOTS],
                                   ACT.Copy).then_inc(s["xg"], 1)

            def expert_block(b):
                act.wait_ge(s["glu_sb"], b + 1)
                act.activation(sig_t, glu_t, ACT.Sigmoid, scale=ALPHA).then_inc(s["sig"], 1)
                act.wait_ge(s["swt_ps"], b + 1)
                act.activation(swT0[0:64].rearrange("p a b -> p (a b)"), B[3][0:64, 0:2 * P], ACT.Copy)
                act.activation(swT1[64:P].rearrange("p a b -> p (a b)"), B[3][64:P, 0:2 * P], ACT.Copy)\
                    .then_inc(s["swT"], 1)
                gathered(b + 2)
                act.wait_ge(s["aT2_ps"], b + 1)
                act.activation(actT.rearrange("p a b c -> p (a b c)"), B[2][:, :], ACT.Copy)\
                    .then_inc(s["aT2"], 1)
                act.wait_ge(s["dn_used"], 4 * b + 4)
                act.activation(y_s, B[3][:, :], ACT.Copy).then_inc(s["ysb"], 1)

            act.wait_ge(s["loop_z"], 1)
            gathered(1)
            expert_block(0)
            act.wait_ge(s["table_in"], 16)
            blocks = act.value_load(table_row[0:1, 2:3], min_val=E, max_val=E + EXTRA)
            with act.Fori(1, blocks) as b:
                expert_block(b)

        @block.vector
        def _(dve):
            steps = [0]

            def link(ins):
                steps[0] += 1
                ins.then_inc(s["dve_step"], 1)
                dve.wait_ge(s["dve_step"], steps[0])

            TTo, TS, STT = dve.tensor_tensor, dve.tensor_scalar, dve.scalar_tensor_tensor

            dve.wait_ge(s["x_sq"], 2)
            link(TS(xs, xs, 1.0 / D, EPS, ALU.mult, ALU.add))
            dve.reciprocal(xs, xs).then_inc(s["x_var"], 1)
            dve.wait_ge(s["x_rs"], 1)
            for t in range(TT):
                TS(xn[:, t, :], hx[:, t, :], xr[:, t:t + 1], None, ALU.mult).then_inc(s["xn"], 1)
            dve.wait_ge(s["dt"], 1)
            dtb = dts[0:GG].unsqueeze(2).to_broadcast([GG, 2, PS])
            for i in range(2):
                last = TTo(natA[0:GG, 2 + i, :].rearrange("p (t n) -> p t n", t=2),
                           natA[0:GG, i, :].rearrange("p (t n) -> p t n", t=2), dtb, ALU.mult)
            last.then_inc(s["aT_in"], 1)
            dve.wait_ge(s["g1_in"], 16)
            for t in range(TT):
                for half in range(2):
                    dve.wait_ge(s["xT_ps"], 2 * t + half + 1)
                    TTo(xnT[:, 4 * half:4 * half + 4, P * t:P * t + P],
                        B[2 * t + half][:, :].rearrange("p (k n) -> p k n", k=4),
                        g1[:, 4 * half:4 * half + 4].unsqueeze(2).to_broadcast([P, 4, P]), ALU.mult)\
                        .then_inc(s["xT"], 1)
            dve.wait_ge(s["aT_ps"], 1)
            link(dve.tensor_copy(pa.rearrange("p a b -> p (a b)"), B[4][:, 0:4 * GG]))
            kk, r, rc = tr[:, 0, :], tr[:, 1, :], tr[:, 2, :]
            sn, cs = tr[:, 4, :], tr[:, 3, :]
            link(TS(kk, pa[:, 3, :], 1 / (2 * math.pi), ROUND, ALU.mult, ALU.add))
            link(TS(kk, kk, ROUND, None, ALU.subtract))
            link(STT(r, kk, -TWO_PI_1, pa[:, 3, :], ALU.mult, ALU.add))
            link(STT(r, kk, -TWO_PI_2, r, ALU.mult, ALU.add))
            link(STT(r, kk, -TWO_PI_3, r, ALU.mult, ALU.add))
            link(TS(r, r, 3.1415925, -3.1415925, ALU.min, ALU.max))
            link(TS(rc, r, -1.0, None, ALU.mult))
            link(TTo(rc, rc, r, ALU.max))
            TS(rc, rc, -1.0, math.pi / 2, ALU.mult, ALU.add).then_inc(s["trig"], 1)
            for ri, dst in enumerate((cTr, cTi)):
                dve.wait_ge(s["cT_ps"], ri + 1)
                v = B[5 + ri][:, :].rearrange("p (g t h) -> p g t h", t=2, h=H)
                for t in range(2):
                    last = dve.tensor_copy(dst[64 * t:64 * t + 64], v[64 * t:64 * t + 64, :, t, :])
            last.then_inc(s["cT"], 1)
            dve.wait_ge(s["cT"], 1)

            def cmul(outr, outi, ar, ai, br, bi, shape):
                n = 1
                for d in shape:
                    n *= d
                t = []
                for v in (sc1, sc2, sc3, sc4):
                    v = v.rearrange("p a b -> p (a b)")[:, 0:n]
                    t.append(v if len(shape) == 1 else v.rearrange("p (a b) -> p a b", a=shape[0]))
                TTo(t[0], ar, br, ALU.mult)
                TTo(t[1], ai, bi, ALU.mult)
                TTo(t[2], ar, bi, ALU.mult)
                link(TTo(t[3], ai, br, ALU.mult))
                TTo(outr, t[0], t[1], ALU.subtract)
                link(TTo(outi, t[2], t[3], ALU.add))

            def per_pair(v, n):
                return v.unsqueeze(2).to_broadcast([P, GG, n])

            dve.wait_ge(s["sincos"], 1)
            dve.memset(Pr[:, :, 0], 1.0)
            dve.memset(Pi[:, :, 0], 0.0)
            TTo(Pr[:, :, 1], mg[:, 0, :], cs, ALU.mult)
            link(TTo(Pi[:, :, 1], mg[:, 0, :], sn, ALU.mult))
            for n in (1, 2, 4):
                cmul(Pr[:, :, n + 1:2 * n + 1], Pi[:, :, n + 1:2 * n + 1], Pr[:, :, 1:n + 1], Pi[:, :, 1:n + 1],
                     per_pair(Pr[:, :, n], n), per_pair(Pi[:, :, n], n), (GG, n))
            for t in range(L):
                dve.tensor_copy(Vr[:, :, t], Pr[:, :, L - 1 - t])
                last = dve.tensor_copy(Vi[:, :, t], Pi[:, :, L - 1 - t])
            link(last)
            lr, li = pa[:, 0, :], pa[:, 1, :]
            t0, t1, t2, t3, t4, t5 = t16
            TTo(t0, lr, lr, ALU.mult)
            TTo(t1, li, li, ALU.mult)
            link(TS(t2, Pr[:, :, 1], 1.0, None, ALU.subtract))
            link(TTo(t0, t0, t1, ALU.add))
            TTo(t1, t2, lr, ALU.mult)
            TTo(t3, Pi[:, :, 1], li, ALU.mult)
            TTo(t4, Pi[:, :, 1], lr, ALU.mult)
            link(TTo(t5, t2, li, ALU.mult))
            dve.reciprocal(t0, t0)
            TTo(t1, t1, t3, ALU.add)
            link(TTo(t4, t4, t5, ALU.subtract))
            TTo(cfr, t1, t0, ALU.mult)
            link(TTo(cfi, t4, t0, ALU.mult))
            dve.wait_ge(s["b_in"], 32)
            cmul(bbr, bbi, br_raw, bi_raw, per_pair(cfr, H), per_pair(cfi, H), (GG, H))

            dve.wait_ge(s["cp_zero"], 1)

            def four(v, n, e):
                return v.unsqueeze(2).to_broadcast([P, GG, n, H]) if e else \
                    v.unsqueeze(3).to_broadcast([P, GG, n, H])

            CRv, CIv = [v.rearrange("p g t (e h) -> p g t e h", h=H) for v in (CR, CI)]
            TTo(tA, four(Pr, 9, 0), four(cTr, 9, 1), ALU.mult)
            link(TTo(tB, four(Pi, 9, 0), four(cTi, 9, 1), ALU.mult))
            for t in range(2):
                o = slice(64 * t, 64 * t + 64)
                last = TTo(CRv[o, :, t], tA[o], tB[o], ALU.subtract)
            link(last)
            TTo(tA, four(Pr, 9, 0), four(cTi, 9, 1), ALU.mult)
            link(TTo(tB, four(Pi, 9, 0), four(cTr, 9, 1), ALU.mult))
            for t in range(2):
                o = slice(64 * t, 64 * t + 64)
                last = STT(CIv[o, :, t], tA[o], -1.0, tB[o], ALU.mult, ALU.subtract)
            last.then_inc(s["cp_ready"], 1)
            dve.wait_ge(s["cp_ready"], 1)
            WRv, WIv = [v.rearrange("p g (e h) -> p g e h", h=H) for v in (WR, WI)]
            tAw, tBw = tA[:, :, 0:L], tB[:, :, 0:L]
            TTo(tAw, four(Vr, L, 0), four(bbr, L, 1), ALU.mult)
            link(TTo(tBw, four(Vi, L, 0), four(bbi, L, 1), ALU.mult))
            link(TTo(WRv, tAw, tBw, ALU.subtract))
            TTo(tAw, four(Vr, L, 0), four(bbi, L, 1), ALU.mult)
            link(TTo(tBw, four(Vi, L, 0), four(bbr, L, 1), ALU.mult))
            TTo(WIv, tAw, tBw, ALU.add).then_inc(s["win_t"], 1)
            dve.wait_ge(s["lam_in"], 64)
            for i in range(2):
                last = dve.tensor_tensor_reduce(lamrow[:, 2 * i, :], lamrow[:, 2 * i, :],
                                                lamrow[:, 2 * i + 1, :], 1.0, 0.0, ALU.mult, ALU.add,
                                                lamv[:, 2 + i:3 + i])
            last.then_inc(s["lam_e"], 1)
            dve.wait_ge(s["q_sq"], 4)
            for n, src in enumerate((q_tm, k_tm)):
                last = dve.tensor_reduce(qv[:, n].rearrange("p t g -> p (t g)"),
                                         src.rearrange("p t (g d) -> p (t g) d", d=SUB), AX, ALU.add)
            link(last)
            link(TS(qv, qv, 1.0 / SUB, EPS, ALU.mult, ALU.add))
            dve.reciprocal(qv, qv).then_inc(s["qk_var"], 1)
            dve.wait_ge(s["qk_rs"], 1)
            for n, dst in enumerate((q_tm, k_tm)):
                for t in range(TT):
                    TTo(dst[:, t, :].rearrange("p (g d) -> p g d", d=SUB),
                        B[2 + 2 * n + t][:, :].rearrange("p (g d) -> p g d", d=SUB),
                        qv[:, n, t, :].unsqueeze(2).to_broadcast([P, 8, SUB]), ALU.mult)\
                        .then_inc(s["qk_tm"], 1)
            dve.wait_ge(s["lam_n"], 1)
            link(TTo(lamv[:, 4:5], lamv[:, 1:2], lamv[:, 0:1], ALU.subtract))
            link(TS(lamv[:, 4:5], lamv[:, 4:5], LAMBDA_INIT, None, ALU.subtract))
            link(dve.tensor_copy(e8r, cs))
            link(dve.tensor_copy(e8i, sn))
            for _ in range(3):
                cmul(t16[0], t16[1], e8r, e8i, e8r, e8i, (GG,))
                dve.tensor_copy(e8r, t16[0])
                link(dve.tensor_copy(e8i, t16[1]))
            dve.memset(Rr[:, :, 0], 1.0)
            dve.memset(Ri[:, :, 0], 0.0)
            dve.tensor_copy(Rr[:, :, 1], e8r)
            link(dve.tensor_copy(Ri[:, :, 1], e8i))
            for n in (1, 2, 4, 8, 15):
                cmul(Rr[:, :, n + 1:2 * n + 1], Ri[:, :, n + 1:2 * n + 1], Rr[:, :, 1:n + 1], Ri[:, :, 1:n + 1],
                     per_pair(Rr[:, :, n], n), per_pair(Ri[:, :, n], n), (GG, n))
            cmul(Rr[:, :, 31:32], Ri[:, :, 31:32], Rr[:, :, 30:31], Ri[:, :, 30:31],
                 Rr[:, :, 1:2], Ri[:, :, 1:2], (GG, 1))
            dve.tensor_copy(magz, per_pair(mg[:, 1, :], NC)).then_inc(s["turns"], 1)
            dve.wait_ge(s["ident"], 1)
            link(dve.tensor_reduce(hsel, ident.rearrange("p (k h) -> p h k", h=H), AX, ALU.add))
            link(dve.memset(magz[:, :, 0], 0.0))
            dve.wait_ge(s["d_in"], 16)
            link(TTo(dd, dB, hsel.unsqueeze(1).to_broadcast([P, G, H]), ALU.mult))
            dve.wait_ge(s["kk_sb"], 8)
            TTo(KK[:, :, 0:H], KK[:, :, 0:H], dd, ALU.add).then_inc(s["kk_d"], 1)
            dve.wait_ge(s["kz_fill"], 2)
            dve.wait_ge(s["vec_in"], 16 * 10)
            for n, (dst, gain) in enumerate(((qz, qg), (kz, kg))):
                for t in range(TT):
                    dve.wait_ge(s["qkT_ps"], 2 * n + t + 1)
                    for sub in range(2):
                        o = slice(64 * sub, 64 * sub + 64)
                        last = TS(dst[o, sub, :, P * t:P * t + P],
                                  B[2 + t][o, :].rearrange("p (h q) -> p h q", h=HEADS),
                                  gain[o], None, ALU.mult)
                    last.then_inc(s["qkT"], 1)
            dve.wait_ge(s["kk_d"], 1)
            dve.wait_ge(s["sT_ps"], 2)
            Ir, Ii = [B[4 + n][:, :].rearrange("p (g c) -> p g c", c=NC) for n in range(2)]
            i0, i1, i2, i3 = [It[:, n] for n in range(4)]
            TTo(i0, Ir, Rr, ALU.mult)
            TTo(i1, Ii, Ri, ALU.mult)
            TTo(i2, Ii, Rr, ALU.mult)
            link(TTo(i3, Ir, Ri, ALU.mult))
            TTo(i0, i0, i1, ALU.add)
            link(TTo(i2, i2, i3, ALU.subtract))
            flat = lambda v: v.rearrange("p g c -> p (g c)")
            dve.tensor_tensor_scan(flat(i1), flat(magz), flat(i0), 0.0, ALU.mult, ALU.add)
            link(dve.tensor_tensor_scan(flat(i3), flat(magz), flat(i2), 0.0, ALU.mult, ALU.add))
            dve.memset(Spr[:, :, 0], 0.0)
            dve.memset(Spi[:, :, 0], 0.0)
            w = slice(0, NC - 1)
            TTo(i0[:, :, w], i1[:, :, w], Rr[:, :, w], ALU.mult)
            link(TTo(i2[:, :, w], i3[:, :, w], Ri[:, :, w], ALU.mult))
            link(TTo(Spr[:, :, 1:], i0[:, :, w], i2[:, :, w], ALU.subtract))
            TTo(i0[:, :, w], i3[:, :, w], Rr[:, :, w], ALU.mult)
            link(TTo(i2[:, :, w], i1[:, :, w], Ri[:, :, w], ALU.mult))
            TTo(Spi[:, :, 1:], i0[:, :, w], i2[:, :, w], ALU.add).then_inc(s["s_prev"], 1)
            def row_max(u):
                t = u % 2
                dve.wait_ge(s["score"], u + 1)
                if u >= 2:
                    dve.wait_ge(s["prob"], 2 * (u - 1))
                link(dve.tensor_reduce(smx[:, u % 2, :], B[2 + u % 2][:, :].rearrange("p (s k) -> p s k", s=2)
                                       [:, :, 0:P * (t + 1)], AX, ALU.max))
                TS(nmx[:, u % 2, :], smx[:, u % 2, :], -SUB ** -0.5, None, ALU.mult).then_inc(s["smax"], 1)

            def difference(u):
                t = u % 2
                dve.wait_ge(s["prob"], 2 * u + 2)
                link(dve.reciprocal(rinv[:, u % 2, :], rsum[:, u % 2, :]))
                link(TTo(rinv[:, u % 2, 1:2], rinv[:, u % 2, 1:2], lamv[:, 4:5], ALU.mult))
                if u >= 2:
                    dve.wait_ge(s["w_ps"], u - 1)
                wu = wmix[:, u % 2, 0:P * (t + 1)]
                link(TS(wu, probs(u, 1), rinv[:, u % 2, 1:2], None, ALU.mult))
                STT(wu, probs(u, 0), rinv[:, u % 2, 0:1], wu, ALU.mult, ALU.add).then_inc(s["wt"], 1)

            for h in range(HEADS):
                row_max(2 * h)
                row_max(2 * h + 1)
                difference(2 * h)
                difference(2 * h + 1)
            for m in range(2):
                dve.wait_ge(s["gelu_sq"], m + 1)
                o = slice(4 * m, 4 * m + 4)
                y = B[6 + m][:, :].rearrange("p (t q c) -> p t q c", t=4, q=4)
                link(TS(ge1[:, o], ge1[:, o], 0.044715, 1.0, ALU.mult, ALU.add))
                TTo(ge1[:, o], ge1[:, o], y, ALU.mult).then_inc(s["gelu_w"], 1)
            for m in range(2):
                dve.wait_ge(s["gelu_s"], m + 1)
                y = B[6 + m][:, :].rearrange("p (t q c) -> p t q c", t=4, q=4)
                for t in range(4):
                    last = TTo(yT.rearrange("p q (c t) -> p t q c", t=L)[:, 4 * m + t],
                               y[:, t], ge2[:, 4 * m + t], ALU.mult)
                last.then_inc(s["yT"], 1)

            dve.wait_ge(s["yT"], 2)
            for m in range(2):
                dve.wait_ge(s["o_ms"], m + 1)
                last = TS(o_rs[:, 2 * m:2 * m + 2, :].rearrange("p a b -> p (a b)"), B[2 + m][:, :],
                          1.0 / P, EPS, ALU.mult, ALU.add)
            link(last)
            dve.reciprocal(o_rs, o_rs).then_inc(s["o_var"], 1)
            dve.wait_ge(s["glu_s"], 4)
            TTo(yT.rearrange("p q n -> p (q n)"), yT.rearrange("p q n -> p (q n)"),
                ge1.rearrange("p a b c -> p (a b c)"), ALU.mult).then_inc(s["yg"], 1)
            link(TS(lamv[:, 5:6], subg, 1.0 - LAMBDA_INIT, None, ALU.mult))
            dve.wait_ge(s["o_rs"], 1)
            for m in range(2):
                last = STT(oT[:, 2 * m:2 * m + 2, :].rearrange("p a b -> p (a b)"), B[4 + m][:, :],
                           lamv[:, 5:6], o_rs[:, 2 * m:2 * m + 2, :].rearrange("p a b -> p (a b)"),
                           ALU.mult, ALU.mult)
            last.then_inc(s["oT"], 1)
            gf = gates.rearrange("p n t -> p (n t)")
            mf = mixT.rearrange("p n t -> p (n t)")
            for f in range(4):
                if f % 2 == 0:
                    dve.wait_ge(s["ps_ssm"], f // 2 + 1)
                else:
                    dve.wait_ge(piece_used, 18 + f // 2)
                last = TTo(mf[:, 512 * f:512 * f + 512], B[f][:, :], gf[:, 512 * f:512 * f + 512], ALU.mult)
            link(last)
            for f in range(4):
                if f % 2 == 0:
                    dve.wait_ge(s["ps_att"], f // 2 + 1)
                else:
                    dve.wait_ge(piece_used, 20 + f // 2)
                m = mtmp[:, f % 2, :]
                link(TTo(m, B[4 + f][:, :], gf[:, 2048 + 512 * f:2048 + 512 * f + 512], ALU.mult))
                TTo(mf[:, 512 * f:512 * f + 512], mf[:, 512 * f:512 * f + 512], m, ALU.add)\
                    .then_inc(s["mixed"], 1)
            dve.wait_ge(s["g2_in"], 16)
            dve.wait_ge(s["wr_in"], 32)

            def h_of(t):
                for n in range(2):
                    dve.wait_ge(s["out_ps"], 2 * t + n + 1)
                    TTo(hx[:, t, 512 * n:512 * n + 512], hx[:, t, 512 * n:512 * n + 512],
                        B[2 * t + n][:, :], ALU.add).then_inc(s["h"], 1)
                dve.wait_ge(s["h_sq"], 2 * t + 2)
                link(TTo(xs[:, t:t + 1], xs2[:, t, 0:1], xs2[:, t, 1:2], ALU.add))
                link(TS(xs[:, t:t + 1], xs[:, t:t + 1], 1.0 / D, EPS, ALU.mult, ALU.add))
                dve.reciprocal(xs[:, t:t + 1], xs[:, t:t + 1]).then_inc(s["h_var"], 1)
                dve.wait_ge(s["h_rs"], t + 1)
                STT(hn[:, t, :], hx[:, t, :], xr[:, t:t + 1], g2b, ALU.mult, ALU.mult).then_inc(s["hn"], 1)

            def best_of(t):
                dve.wait_ge(s["lg_ps"], t + 1)
                link(TTo(lg[:, t, :], B[6 + t][:, 0:E], brb, ALU.add))
                link(dve.max(top_v[:, t, :], lg[:, t, :]))
                link(dve.max_index(top_i[:, t, :], top_v[:, t, :], lg[:, t, :]))
                link(dve.tensor_copy(top_f[:, t, :], top_i[:, t, :]))
                link(TTo(one_k[:, t], iota[:, 0:E].unsqueeze(2).to_broadcast([P, E, TOPK]),
                         top_f[:, t, 0:TOPK].unsqueeze(1).to_broadcast([P, E, TOPK]), ALU.is_equal))
                link(dve.tensor_reduce(R1[:, E * t:E * t + E], one_k[:, t], AX, ALU.add))

            h_of(0)
            best_of(0)
            link(dve.tensor_copy(R2[:, E:2 * E], R1[:, 0:E]))
            h_of(1)
            best_of(1)
            TTo(R2[:, 2 * E:], R1[:, 0:E], R1[:, E:2 * E], ALU.add).then_inc(s["routed"], 1)
            TS(xs, top_v[:, :, 0], -1.0, None, ALU.mult).then_inc(s["top_e"], 1)
            dve.wait_ge(s["rk_ps"], 1)
            o = B[0][:, 0:LC]
            link(STT(rank.rearrange("p t e -> p (t e)"), o[:, 0:TT * E], 1.0, R1[:, 0:TT * E],
                     ALU.add, ALU.mult))
            link(dve.tensor_copy(cnt, o[:, 2 * E:]))
            TS(rank, rank, 1.0, None, ALU.subtract).then_inc(s["rank"], 1)
            dve.wait_ge(s["rank"], 1)

            def one_hot(dst, e, first, weighted):
                for t in range(TT):
                    last = TS(dst[:, t, :].rearrange("p (d n) -> p d n", d=2),
                              iota[:, bass.ds(first, SLOTS)].unsqueeze(1).to_broadcast([P, 2, SLOTS]),
                              rank[:, t, bass.ds(e, 1)], gw[:, t, bass.ds(e, 1)] if weighted else None,
                              ALU.is_equal, *((ALU.mult,) if weighted else ()))
                return last

            def expert_block(b, e, first, e_next, first_next, peeled=False):
                dve.wait_ge(s["xg_ps"], 2 * b + 2)
                if not peeled:
                    one_hot(selw, e, first, True).then_inc(s["dsel"], 1)
                one_hot(selg, e_next, first_next, False).then_inc(s["sel"], 1)
                dve.wait_ge(s["up_used"], KT * b + KT)
                for n in range(2):
                    v = B[n][:, :].rearrange("p (j two) -> p two j", two=2)
                    TS(glu_t[:, 256 * n:256 * n + 256], v[:, 0, :], LIMIT, None, ALU.min)
                    last = TS(lin_t[:, 256 * n:256 * n + 256], v[:, 1, :], LIMIT, -LIMIT, ALU.min, ALU.max)
                last.then_inc(s["glu_sb"], 1)
                dve.wait_ge(s["glu_sb"], b + 1)
                STT(lin_t, lin_t, 1.0, glu_t, ALU.add, ALU.mult).then_inc(s["gated"], 1)
                dve.wait_ge(s["gated"], b + 1)
                dve.wait_ge(s["sig"], b + 1)
                TTo(act_s, lin_t, sig_t, ALU.mult).then_inc(s["act"], 1)

            one_hot(selg, 0, 0, False).then_inc(s["sel"], 1)
            dve.wait_ge(s["top_x"], 2)
            link(dve.reciprocal(xr, xr))
            for t in range(TT):
                last = TS(top_w[:, t, 0:TOPK], top_w[:, t, 0:TOPK], xr[:, t:t + 1], None, ALU.mult)
            link(last)
            for t in range(TT):
                last = TTo(gw_k[:, t], one_k[:, t], top_w[:, t, 0:TOPK].unsqueeze(1).to_broadcast([P, E, TOPK]),
                           ALU.mult)
            link(last)
            dve.tensor_reduce(gw, gw_k, AX, ALU.add).then_inc(s["gw"], 1)
            dve.wait_ge(s["gw"], 1)
            one_hot(selw, 0, 0, True).then_inc(s["dsel"], 1)
            link(TS(ovf, cnt, float(SLOTS), None, ALU.is_gt))
            link(STT(ovf, cnt, 2.0 * SLOTS, ovf, ALU.is_gt, ALU.add))
            link(STT(ovf, cnt, 3.0 * SLOTS, ovf, ALU.is_gt, ALU.add))
            link(dve.tensor_tensor_scan(cum, ones[:, 0:E], ovf, 0.0, ALU.mult, ALU.add))
            link(TS(before, cum, iop, None, ALU.is_le))
            dve.tensor_reduce(tabf[:, 0:1], before, AX, ALU.add)
            link(TTo(ovt, before, ovf, ALU.mult))
            link(dve.tensor_reduce(tabf[:, 1:2], ovt, AX, ALU.add))
            link(TS(tabf[:, 3:4], iop, 0.0, None, ALU.is_lt))
            link(TS(tabf[:, 4:5], iop, float(E), tabf[:, 3:4], ALU.add, ALU.mult))
            link(TTo(tabf[:, 0:1], tabf[:, 0:1], tabf[:, 4:5], ALU.add))
            link(TS(tabf[:, 0:1], tabf[:, 0:1], float(E - 1), None, ALU.min))
            link(TTo(tabf[:, 1:2], iop, tabf[:, 1:2], ALU.subtract))
            link(TS(tabf[:, 1:2], tabf[:, 1:2], 1.0, float(SLOTS), ALU.add, ALU.mult))
            link(TS(tabf[:, 3:4], tabf[:, 3:4], -1.0, 1.0, ALU.mult, ALU.add))
            link(TTo(tabf[:, 1:2], tabf[:, 1:2], tabf[:, 3:4], ALU.mult))
            link(TS(tabf[:, 1:2], tabf[:, 1:2], 0.0, 3.0 * SLOTS, ALU.max, ALU.min))
            link(TS(tabf[:, 2:3], cum[:, E - 1:E], float(E), None, ALU.add))
            dve.tensor_copy(table_i[:, 0:3], tabf[:, 0:3]).then_inc(s["table"], 1)
            dve.wait_ge(s["loop_z"], 1)
            dve.wait_ge(s["gT_ps"], 1)
            dve.tensor_copy(gwT[0:E], B[3][0:E, 0:TOK]).then_inc(s["gT"], 1)
            expert_block(0, 0, 0, 1, 0, peeled=True)
            dve.wait_ge(s["table_in"], 16)
            blocks = dve.value_load(table_row[0:1, 2:3], min_val=E, max_val=E + EXTRA)
            with dve.Fori(1, blocks) as b:
                entry = [dve.value_load(table_row[0:1, bass.ds(3 * b + n, 1)], min_val=0, max_val=m)
                         for n, m in ((0, E - 1), (1, 3 * SLOTS), (3, E - 1), (4, 3 * SLOTS))]
                expert_block(b, *entry)
            dve.wait_ge(s["scat"], blocks)
            for t in range(TT):
                for n in range(2):
                    TTo(hx[:, t, 512 * n:512 * n + 512], hx[:, t, 512 * n:512 * n + 512],
                        B[4 + 2 * t + n][:, :], ALU.add).then_inc(s["fin"], 1)



_INS = ["x", "norm1_g", "w_in", "b_gate", "ssm_a_re", "ssm_a_im", "ssm_log_dt", "ssm_b_re", "ssm_b_im",
        "ssm_c_re", "ssm_c_im", "ssm_d", "ssm_w_glu", "ssm_b_glu", "q_norm_g", "k_norm_g", "lambda_q1",
        "lambda_k1", "lambda_q2", "lambda_k2", "subln_g", "w_proj_ssm", "w_proj_att", "w_out", "norm2_g",
        "w_router", "b_router", "w_up", "b_up", "w_down", "b_down"]


def kernel(**inputs):
    import numpy as np
    import concourse.bacc as bacc
    from concourse.bass_utils import run_bass_kernel_spmd

    nc = bacc.Bacc("TRN2", target_bir_lowering=False, num_devices=1)
    arrays, aps = {}, {}
    for name in _INS:
        v = np.ascontiguousarray(inputs[name])
        arrays[f"in_{name}"] = v
        aps[name] = nc.dram_tensor(f"in_{name}", v.shape, mybir.dt.from_np(v.dtype), kind="ExternalInput").ap()
    out = nc.dram_tensor("out_y", (1, TOK, D), F32, kind="ExternalOutput").ap()
    mixer_and_experts(nc, aps, out)
    r = run_bass_kernel_spmd(nc, [arrays], core_ids=[0])
    return r.results[0]["out_y"]
```

```python
import math
from contextlib import ExitStack

import concourse.bass as bass
from concourse import mybir

ALU = mybir.AluOpType
ACT = mybir.ActivationFunctionType
F32 = mybir.dt.float32
I32 = mybir.dt.int32
U32 = mybir.dt.uint32
AX = mybir.AxisListType.X

P = 128
D = 1024
TOK = 256
TT = TOK // P
KT = D // P
G, PS, H = 32, 64, 16
GG = G // 2
S = G * H
L = P // H
NC = TOK // L
HEADS, SUB = 4, 64
AW = HEADS * 2 * SUB
WIN = S + 3 * AW + 2 * D
CHUNK = 64
E, TOPK = 32, 4
SLOTS = 64
EXTRA = TOK * TOPK // (SLOTS + 1)
TURN = E // 2
ALPHA, LIMIT, EPS = 1.702, 7.0, 1e-6
LAMBDA_INIT = 0.8 - 0.6 * math.exp(0.0)
BIG = 1e30
ROUND = 1.5 * 2.0 ** 23
TWO_PI_1 = 6.28125
TWO_PI_2 = 0.0019350051879882812
TWO_PI_3 = 2 * math.pi - TWO_PI_1 - TWO_PI_2
PIECE = 256
PIECES = 25
LC = 3 * E
RING = 3

SEMS = """ident a_in c_in b_in vec_in d_in lam_in dve_step pool_step x_sq x_var x_rs xn xT_ps xT dt aT_in
 aT_ps cT_ps trig sincos win_t cp_ready u_sb u_out u_back q_sq v_sb qk_var qk_rs qk_tm wT_ps wT_sb
 kk_ps kk_sb kk_d m_zero m_in cp_zero U_ps U_sb st_ps st_sb sT_ps s_prev y_ps y_sb yT_ps gelu_sq
 gelu_w gelu_s yT glu_ps glu_s yg gate_sb qkT_ps qkT kz_fill score smax prob lam_e lam_n wt w_ps
 w_sb oT_ps o_sq o_ms o_var o_rs oT ps_ssm ps_att mixed h h_sq h_var h_rs hn hT_ps hT lg_ps top_e
 top_x gw rk_ps gT_ps gT bd_in bias_ps table_out table_in table bup_z sel xg_ps xg swt_ps swT glu_sb
 sig act aT2_ps aT2 ysb summed up_used dn_used bup_used dsel fin fin_out wr_in g2_in loop_z u_turn
 wg bb_rep gated cT g1_in gate_ps out_ps rank routed turns o_read warm""".split()


def mixer_and_experts(nc, a, out):
    ctx = ExitStack()
    with ctx:
        KB = 256
        arena = ctx.enter_context(nc.sbuf_tensor("arena", [P, 207 * KB], F32))
        u_dram = nc.dram_tensor("u_scratch", (TOK, S), F32, kind="Internal").ap()
        table_dram = nc.dram_tensor("table_scratch", (P, 3), I32, kind="Internal").ap()

        def at(kb, *dims):
            n = 1
            for d in dims:
                n *= d
            o = int(kb * KB)
            v = arena[:, o:o + n]
            names = "abcd"[:len(dims)]
            if len(dims) > 1:
                v = v.rearrange(f"p ({' '.join(names)}) -> p {' '.join(names)}",
                                **{k: d for k, d in zip(names, dims)})
            return v

        SHARED = KT - 2
        ORDER = (*range(SHARED, KT), *range(SHARED))
        ORDER_0 = tuple(range(KT))
        up_w = [[[at(8 * k + 4 * h, D) for h in range(2)] for k in range(KT)] for _ in range(2)]
        up_w[1][SHARED] = [at(168, D), at(196, D)]
        up_w[1][SHARED + 1] = [at(188, D), at(192, D)]
        dn_w = [[at(64 + 8 * j, 2, D) for j in range(4)], [at(kb, 2, D) for kb in (160, 172, 112, 180)]]
        CW = 9 * H
        CR = at(0, GG, 2, CW)
        CI = at(18, GG, 2, CW)
        WR = at(36, GG, P)
        WI = at(44, GG, P)
        KK = at(36, G, P)
        WIN_M = at(52, GG, 2, P)
        MM = at(68, G, P)
        tA = at(68, GG, 9, H)
        tB = at(172, GG, 9, H)
        U = at(84, 8, 4, NC)
        uc = at(88, L, P)
        uc2 = at(92, 8, L, H)
        Y_sb = at(88, L, 4, 2, H)
        bbR, bbI = at(188, GG, L, H), at(172, GG, L, H)
        wg = at(68, 4, 4, P)
        u_tm = at(92, TT, S)
        S_sb = at(92, 4, 2, P)
        hx = at(96, TT, D)
        hn = at(104, TT, D)
        Rr, Ri = at(104, GG, NC), at(106, GG, NC)
        magz = at(108, GG, NC)
        bbr, bbi = at(110, GG, H), at(111, GG, H)
        oT = at(104, HEADS, TOK)
        o2 = at(108, HEADS, TOK)
        xnT = at(112, KT, TOK)
        stream = [at(120 + 8 * i, 8, PIECE) for i in range(RING)]
        last_piece = at(112, 8, PIECE)
        gates = at(144, 16, TOK)
        xn = at(144, TT, D)
        c_sb = at(152, 2, 4, 2, PS)
        br_raw, bi_raw = at(156, GG, H), at(157, GG, H)
        q_tm, k_tm = at(160, TT, AW), at(164, TT, AW)
        yg = at(160, 4, TOK)
        ge1, ge2 = at(160, L, 4, NC), at(164, L, 4, NC)
        o_rs = at(164, HEADS, TOK)
        v_tm = at(168, TT, AW)
        qz = at(172, 2, HEADS, TOK)
        kz = at(180, 2, HEADS, TOK)
        mixT = at(172, KT, TOK)
        mtmp = at(180, 2, 2 * TOK)
        prob = at(188, 2, 2 * TOK)
        wmix = at(192, 2, TOK)
        wTs = at(194, 2, 2, P)
        cTr, cTi = at(188, GG, H), at(189, GG, H)
        Pr, Pi = at(190, GG, 9), at(190.75, GG, 9)
        Vr, Vi = at(191.5, GG, L), at(192, GG, L)
        sc1, sc2, sc3, sc4 = [at(184 + i, GG, H) for i in range(4)]
        It = at(52, 4, GG, NC)
        Spr, Spi = at(196, GG, NC), at(198, GG, NC)
        dB, dd = at(196, G, H), at(198, G, H)
        yT = at(196, 4, TOK)
        ident = at(200, P)
        ones = at(200.5, P)
        ltri = at(201, P)
        iota = at(201.5, 5 * SLOTS)
        tq = at(202.75, TOK)
        tk = at(203.75, TOK)
        e0 = at(204.75, SLOTS)
        hsel = at(205, H)
        small = at(205.0625, 496)

        def sm(o, *dims):
            n = 1
            for d in dims:
                n *= d
            v = small[:, o:o + n]
            names = "abc"[:len(dims)]
            if len(dims) > 1:
                v = v.rearrange(f"p ({' '.join(names)}) -> p {' '.join(names)}",
                                **{k: d for k, d in zip(names, dims)})
            return v

        g1 = sm(0, KT)
        bgate = sm(8, 16)
        bglu = sm(24, 4)
        xs = sm(28, TT)
        xs2 = sm(290 + 160, TT, 2)
        xr = sm(30, TT)
        iop = sm(32, 1)
        lamv = sm(33, 8)
        subg = sm(41, 1)
        qg = sm(42, 1)
        kg = sm(43, 1)
        dts = sm(44, 2)
        pa = sm(48, 4, GG)
        tr = sm(112, 6, GG)
        mg = sm(208, 2, GG)
        qv = sm(240, 2, TT, 8)
        smx = sm(272, 2, 2)
        nmx = sm(276, 2, 2)
        rsum = sm(280, 2, 2)
        rinv = sm(284, 2, 2)
        warm = sm(288, 1)
        e8r, e8i = sm(290, GG), sm(306, GG)
        cfr, cfi = sm(322, GG), sm(338, GG)
        t16 = [sm(354 + 16 * i, GG) for i in range(6)]
        natA = at(158, 4, P)
        lamrow = at(198, 4, SUB)
        hT = at(180, KT, TOK)
        bup = at(120, 2 * D)
        bdn = at(128, D)
        xg = at(132, KT, SLOTS)
        act_s = at(134, 4 * P)
        glu_t = at(136, 4 * P)
        lin_t = at(138, 4 * P)
        sig_t = at(140, 4 * P)
        actT = at(142, 4, 2, SLOTS)
        y_s = at(144, 4 * P)
        selw = at(146, TT, P)
        swT0, swT1 = at(147, TT, P), at(148, TT, P)
        selg = at(149, TT, P)
        wr = at(188, KT, LC)
        brb = at(191, E)
        one_k = at(191.25, TT, E, TOPK)
        gw_k = at(192.25, TT, E, TOPK)
        R1 = at(193.25, LC)
        R2 = at(193.75, LC)
        lg = at(152, TT, E)
        top_v = at(152.25, TT, 8)
        top_f = at(152.375, TT, 8)
        top_w = at(152.5, TT, 8)
        gw = at(153, TT, E)
        rank = at(153.5, TT, E)
        cnt = at(153.75, E)
        ovf = at(153.875, E)
        ovt = at(154, E)
        cum = at(154.125, E)
        before = at(154.25, E)
        tabf = at(154.375, 16)
        gwT = at(155, TOK)
        g2b = at(156, D)
        table_row = at(150, 3 * P).bitcast(I32)
        top_i = at(152.625, TT * 8).bitcast(U32).rearrange("p (t n) -> p t n", t=TT)
        table_i = at(152.75, 4).bitcast(I32)

        B = [ctx.enter_context(nc.psum_tensor(f"bank{i}", [P, 512], F32)) for i in range(8)]
        s = {n: ctx.enter_context(nc.semaphore(n)) for n in SEMS}
        x_in = [ctx.enter_context(nc.semaphore(f"x{t}_in")) for t in range(TT)]
        last_in = ctx.enter_context(nc.semaphore("last_piece_in"))
        slot_in = [ctx.enter_context(nc.semaphore(f"slot{i}_in")) for i in range(RING)]
        up_in = [[ctx.enter_context(nc.semaphore(f"up{i}_in")) for i in range(KT)]] * 2
        up_in[1] = up_in[0][:SHARED] + [ctx.enter_context(nc.semaphore(f"up{i}_in_odd")) for i in range(SHARED, KT)]
        dn_in = [[ctx.enter_context(nc.semaphore(f"dn{i}_in_{parity}")) for i in range(KT // 2)]
                 for parity in ("even", "odd")]
        piece_used = ctx.enter_context(nc.semaphore("piece_used"))
        bup_in = ctx.enter_context(nc.semaphore("bup_in"))

        def slot_of(i):
            return last_piece if i == PIECES - 1 else stream[i % RING]

        def piece(i):
            slot = slot_of(i)
            if i < 16:
                w = a["w_in"][0].rearrange("(k p) n -> p k n", p=P)
                return [(slot, w[:, :, i * PIECE:(i + 1) * PIECE])]
            if i == 16:
                v = slot.rearrange("p a b -> p (a b)").rearrange("p (q n) -> p q n", q=4)
                w = a["ssm_w_glu"][0]
                return [(v[32 * t:32 * t + 32], w[P * t:P * t + P].rearrange("(q r) n -> r q n", q=4))
                        for t in range(4)]
            if i < 19:
                v = slot.rearrange("p a b -> p (a b)").rearrange("p (q n) -> p q n", q=4)
                w = a["w_proj_ssm"][0][:, (i - 17) * 512:(i - 16) * 512]
                return [(v[32 * t:32 * t + 32], w[P * t:P * t + P].rearrange("(q r) n -> r q n", q=4))
                        for t in range(4)]
            if i < 21:
                v = slot.rearrange("p a b -> p (a b)").rearrange("p (q n) -> p q n", q=4)
                w = a["w_proj_att"][0].rearrange("(k p) n -> p k n", p=P)
                return [(v, w[:, :, (i - 19) * 512:(i - 18) * 512])]
            w = a["w_out"][0].rearrange("(k p) n -> p k n", p=P)
            return [(slot, w[:, :, (i - 21) * PIECE:(i - 20) * PIECE])]

        def pv(i):
            return stream[i % RING].rearrange("p a b -> p (a b)").rearrange("p (q n) -> p q n", q=4)

        w_up, w_dn, b_up = a["w_up"][0], a["w_down"][0], a["b_up"][0]
        pairs = [(gg, g2) for gg in range(GG) for g2 in range(2)]

        def probs(u, sub):
            return prob[:, u % 2, :].rearrange("p (s k) -> p s k", s=2)[:, sub, 0:P * (u % 2 + 1)]

        block = ctx.enter_context(nc.Block())


        @block.sync
        def _(sp):
            def load_up_tile(b, e, parity, k):
                if k < SHARED:
                    sp.dma_start(at(8 * k, 2 * D), w_up[bass.ds(e, 1), P * k:P * k + P, :]
                                 .rearrange("o p n -> p (o n)")).then_inc(up_in[parity][k], 16)
                    return
                for h in range(2):
                    sp.dma_start(up_w[parity][k][h],
                                 w_up[bass.ds(e, 1), P * k:P * k + P, D * h:D * h + D]
                                 .rearrange("o p n -> p (o n)")).then_inc(up_in[parity][k], 16)

            def load_dn(b, e, parity, j):
                sp.dma_start(dn_w[parity][j],
                             w_dn[bass.ds(e, 1), 2 * P * j:2 * P * (j + 1), :]
                             .rearrange("o (k p) n -> p (o k) n", p=P)).then_inc(dn_in[parity][j], 16)

            for t in range(TT):
                sp.dma_start(hx[:, t, :], a["x"][0, P * t:P * t + P, :]).then_inc(x_in[t], 16)
            sp.dma_start(g1, a["norm1_g"][0].rearrange("(k p) -> p k", p=P),
                         allow_slow_non_contiguous=True).then_inc(s["g1_in"], 16)
            for src, o in ((a["ssm_a_re"], 0), (a["ssm_a_im"], 1)):
                sp.dma_start(natA[0:GG, o, :], src[0].rearrange("(g t) p -> g (t p)", t=2))\
                  .then_inc(s["a_in"], 16)
            sp.dma_start(dts[0:GG], a["ssm_log_dt"][0].rearrange("(g t) -> g t", t=2))\
              .then_inc(s["a_in"], 16)
            for i in (*range(17), PIECES - 1, *range(17, PIECES - 1)):
                if i == 12:
                    sp.wait_ge(s["m_zero"], 1)
                    sp.wait_ge(s["kk_d"], 1)
                    for t in range(L):
                        sp.dma_start(MM[H * t:H * t + H, :, H * t:P], KK[H * t:H * t + H, :, 0:P - H * t])\
                            .then_inc(s["m_in"], 16)
                if i == PIECES - 1:
                    sp.wait_ge(piece_used, 16)
                elif i >= RING:
                    sp.wait_ge(piece_used, i - RING + 1)
                arrived = last_in if i == PIECES - 1 else slot_in[i % RING]
                for dst, src in piece(i):
                    sp.dma_start(dst, src).then_inc(arrived, 16)
                if i == 0:
                    for n, half in enumerate((a["ssm_c_re"], a["ssm_c_im"])):
                        for dup in range(2):
                            sp.dma_start(c_sb[:, n, :, dup, :],
                                         half[0].rearrange("g h p -> (g h) p").rearrange("(i q) p -> q i p", q=P))\
                              .then_inc(s["c_in"], 16)
                if i == 2:
                    for dst, src in ((br_raw, a["ssm_b_re"]), (bi_raw, a["ssm_b_im"])):
                        sp.dma_start(dst, src[0].rearrange("(g t) p h -> (t p) g h", t=2))\
                          .then_inc(s["b_in"], 16)
                    for n, name in enumerate(("lambda_q1", "lambda_k1", "lambda_q2", "lambda_k2")):
                        sp.dma_start(lamrow[:, n, :], a[name][0:1, :].to_broadcast([P, SUB]))\
                          .then_inc(s["lam_in"], 16)
                    sp.dma_start(dB.rearrange("p g h -> p (g h)"), a["ssm_d"][0:1, :].to_broadcast([P, S]))\
                      .then_inc(s["d_in"], 16)
                    sp.dma_start(bgate, a["b_gate"][0].rearrange("(n p) -> p n", p=P),
                                 allow_slow_non_contiguous=True).then_inc(s["vec_in"], 16)
                    sp.dma_start(subg, a["subln_g"][0].rearrange("(p o) -> p o", o=1)).then_inc(s["vec_in"], 16)
                    for t in range(4):
                        sp.dma_start(bglu[32 * t:32 * t + 32],
                                     a["ssm_b_glu"][0][P * t:P * t + P].rearrange("(q r) -> r q", q=4),
                                     allow_slow_non_contiguous=True).then_inc(s["vec_in"], 16)
                    for t in range(2):
                        for dst, name in ((qg, "q_norm_g"), (kg, "k_norm_g")):
                            sp.dma_start(dst[64 * t:64 * t + 64], a[name][0].rearrange("(p o) -> p o", o=1))\
                              .then_inc(s["vec_in"], 16)
                if i == 16:
                    sp.wait_ge(s["y_ps"], 1)
                    sp.wait_ge(s["yT_ps"], 2)
                if 16 <= i < PIECES - 1:
                    k = i - 16
                    if k < KT:
                        load_up_tile(0, 0, 0, k)
                    for j in {5: (0,), 6: (1,), 7: (2, 3)}.get(k, ()):
                        load_dn(0, 0, 0, j)
            sp.wait_ge(s["bup_z"], 1)
            sp.dma_start(bup[0:1, :], b_up[0:1, :]).then_inc(bup_in, 16)
            for j in range(KT // 2):
                if j == 0:
                    sp.wait_ge(piece_used, 19)
                    sp.wait_ge(s["oT"], 1)
                    load_up_tile(1, 1, 1, SHARED)
                elif j < 3:
                    sp.wait_ge(s["out_ps"], 4)
                else:
                    sp.wait_ge(s["lg_ps"], 2)
                load_dn(1, 1, 1, j)
            sp.wait_ge(s["gw"], 1)
            load_up_tile(1, 1, 1, SHARED + 1)

            def load_up(b, e, parity, order=ORDER):
                sp.wait_ge(s["bup_used"], b)
                sp.dma_start(bup[0:1, :], b_up[bass.ds(e, 1), :]).then_inc(bup_in, 16)
                for k in range(SHARED):
                    sp.wait_ge(s["up_used"], KT * b - KT + order.index(k) + 1)
                    load_up_tile(b, e, parity, k)

            def load_ahead(b, e, parity):
                for k in range(SHARED, KT):
                    load_up_tile(b, e, parity, k)

            def load_downs(b, e, parity):
                for j in range(KT // 2):
                    sp.wait_ge(s["dn_used"], 4 * b - 8 + j + 1)
                    load_dn(b, e, parity, j)

            def expert_of(b):
                return sp.value_load(table_row[0:1, bass.ds(3 * b, 1)], min_val=0, max_val=E - 1)

            load_up(1, 1, 1, ORDER_0)
            sp.wait_ge(s["up_used"], KT)
            load_ahead(2, 2, 0)
            load_downs(2, 2, 0)
            sp.wait_ge(s["table_in"], 16)
            fourth_last = sp.value_load(table_row[0:1, 2:3], min_val=E - 4, max_val=E + EXTRA - 3)
            last_b = fourth_last + 3
            with sp.Fori(2, TURN, 2) as b:
                this, after, later = expert_of(b), expert_of(b + 1), expert_of(b + 2)
                after_up = expert_of(b + 1)
                load_up(b, this, 0)
                load_ahead(b + 1, after, 1)
                load_downs(b + 1, after, 1)
                load_up(b + 1, after_up, 1)
                load_ahead(b + 2, later, 0)
                load_downs(b + 2, later, 0)
            load_up(TURN, expert_of(TURN), 0)
            load_ahead(TURN + 1, expert_of(TURN + 1), 1)
            with sp.Fori(TURN + 1, last_b, 2) as b:
                this, after, later = expert_of(b), expert_of(b + 1), expert_of(b + 2)
                after_up = expert_of(b + 1)
                load_up(b, this, 1)
                load_downs(b, this, 1)
                load_ahead(b + 1, after, 0)
                load_up(b + 1, after_up, 0)
                load_downs(b + 1, after, 0)
                load_ahead(b + 2, later, 1)
            last = expert_of(last_b)
            load_up(last_b, last, 1)
            load_downs(last_b, last, 1)
            for t in range(TT):
                for n in range(2):
                    sp.wait_ge(s["fin"], 2 * t + n + 1)
                    sp.dma_start(out[0, P * t:P * t + P, 512 * n:512 * n + 512],
                                 hx[:, t, 512 * n:512 * n + 512]).then_inc(s["fin_out"], 16)
            sp.wait_ge(s["fin_out"], 64)

        @block.gpsimd
        def _(pool):
            steps = [0]

            def link(ins):
                steps[0] += 1
                ins.then_inc(s["pool_step"], 1)
                pool.wait_ge(s["pool_step"], steps[0])

            pool.memset(warm, 0.0).then_inc(s["warm"], 1)
            pool.wait_ge(s["warm"], 1)
            link(pool.memset(ident, 0.0))
            pool.affine_select(out=ident, in_=ident, compare_op=ALU.not_equal, fill=1.0, base=0,
                               pattern=[[-1, P]], channel_multiplier=1).then_inc(s["ident"], 1)
            pool.memset(ltri, 1.0)
            pool.memset(tq, 0.0)
            pool.memset(tk, 0.0)
            pool.memset(e0, 0.0)
            link(pool.memset(ones, 1.0))
            link(pool.affine_select(out=ltri, in_=ltri, compare_op=ALU.is_gt, fill=0.0, base=0,
                                    pattern=[[1, P]], channel_multiplier=-1))
            for half in range(2):
                lo = 64 * half
                for row in range(2):
                    q0, k0 = P * row, P * row + CHUNK
                    pool.affine_select(out=tq[lo:lo + 64, q0:q0 + CHUNK], in_=tq[lo:lo + 64, q0:q0 + CHUNK],
                                       compare_op=ALU.not_equal, fill=1.0, base=-row,
                                       pattern=[[0, CHUNK]], channel_multiplier=1)
                    last = pool.affine_select(out=tk[lo:lo + 64, k0:k0 + CHUNK],
                                              in_=tk[lo:lo + 64, k0:k0 + CHUNK],
                                              compare_op=ALU.not_equal, fill=-BIG, base=-row,
                                              pattern=[[0, CHUNK]], channel_multiplier=1)
                link(last)
            link(pool.memset(e0[0:1, :], 1.0))
            pool.iota(iota, pattern=[[1, 5 * SLOTS]], base=0, channel_multiplier=0,
                      allow_small_or_imprecise_dtypes=True)
            link(pool.iota(iop, pattern=[[0, 1]], base=-E, channel_multiplier=1,
                           allow_small_or_imprecise_dtypes=True))
            pool.memset(CR[0:64, :, 1, :], 0.0)
            link(pool.memset(CI[0:64, :, 1, :], 0.0))
            pool.memset(CR[64:P, :, 0, :], 0.0)
            pool.memset(CI[64:P, :, 0, :], 0.0).then_inc(s["cp_zero"], 1)
            pool.wait_ge(s["u_sb"], 2)
            pool.dma_start(u_dram.rearrange("(t p) n -> p t n", p=P), u_tm).then_inc(s["u_out"], 16)
            pool.wait_ge(s["u_out"], 16)
            for j in range(4):
                pool.dma_start(uc[32 * j:32 * j + 32],
                               u_dram[:, P * j:P * j + P].rearrange("(c s) n -> c s n", s=L))\
                    .then_inc(s["u_back"], 16)
            pool.wait_ge(s["win_t"], 1)
            for dst, src in ((bbR, bbr), (bbI, bbi)):
                pool.tensor_copy(dst, src.unsqueeze(2).to_broadcast([P, GG, L, H])).then_inc(s["bb_rep"], 1)
            pool.memset(MM, 0.0).then_inc(s["m_zero"], 1)
            pool.wait_ge(s["m_zero"], 1)
            pool.wait_ge(s["kk_ps"], 8)
            pool.wait_ge(s["turns"], 1)
            for t, lo in ((0, 64), (1, 0)):
                pool.tensor_copy(qz[lo:lo + 64, t], tq[lo:lo + 64].unsqueeze(1).to_broadcast([64, HEADS, TOK]))
                pool.tensor_copy(kz[lo:lo + 64, t], tk[lo:lo + 64].unsqueeze(1).to_broadcast([64, HEADS, TOK]))\
                    .then_inc(s["kz_fill"], 1)
                pool.wait_ge(s["kz_fill"], t + 1)
            pool.wait_ge(s["mixed"], 4)
            link(pool.memset(wr, 0.0))
            pool.memset(R1, 0.0)
            link(pool.memset(R2, 0.0))
            pool.dma_start(wr[:, :, 0:E], a["w_router"][0].rearrange("(k p) n -> p k n", p=P))\
                .then_inc(s["wr_in"], 16)
            pool.dma_start(brb, a["b_router"][0:1, :].to_broadcast([P, E])).then_inc(s["wr_in"], 16)
            pool.dma_start(g2b, a["norm2_g"][0:1, :].to_broadcast([P, D])).then_inc(s["g2_in"], 16)
            pool.wait_ge(s["out_ps"], 3)
            pool.memset(bup, 0.0).then_inc(s["bup_z"], 1)
            pool.memset(bdn, 0.0)
            pool.memset(gwT, 0.0)
            pool.memset(swT0, 0.0)
            link(pool.memset(swT1, 0.0))
            pool.dma_start(bdn[0:E, :], a["b_down"][0]).then_inc(s["bd_in"], 16)
            pool.memset(iota[:, 4 * SLOTS:], 4.0 * TOK).then_inc(s["loop_z"], 1)
            pool.wait_ge(s["table"], 1)
            pool.dma_start(table_dram, table_i[:, 0:3]).then_inc(s["table_out"], 16)
            pool.wait_ge(s["table_out"], 16)
            pool.dma_start(table_row[0:1, :], table_dram.rearrange("(o q) c -> o (q c)", o=1))\
                .then_inc(s["table_in"], 16)

        @block.tensor
        def _(pe):
            def piece_arrived(i):
                if i == PIECES - 1:
                    pe.wait_ge(last_in, 16)
                    return
                pe.wait_ge(slot_in[i % RING], 16 * sum(len(piece(j)) for j in range(i % RING, i + 1, RING)))

            def transposes(jobs):
                for dst, src in jobs:
                    last = pe.transpose(dst, src, ident[0:src.shape[0], 0:src.shape[0]])
                return last

            pe.wait_ge(s["ident"], 1)
            for t in range(TT):
                pe.wait_ge(s["xn"], t + 1)
                for half in range(2):
                    transposes([(B[2 * t + half][:, P * k:P * k + P],
                                 xn[:, t, P * (4 * half + k):P * (4 * half + k) + P]) for k in range(4)])\
                        .then_inc(s["xT_ps"], 1)
            pe.wait_ge(s["aT_in"], 1)
            transposes([(B[4][:, GG * i:GG * i + GG], natA[0:GG, i, :]) for i in range(4)])\
                .then_inc(s["aT_ps"], 1)
            pe.wait_ge(s["c_in"], 64)
            for ri in range(2):
                transposes([(B[5 + ri][:, P * i:P * i + P], c_sb[:, ri, i].rearrange("p d n -> p (d n)"))
                            for i in range(4)]).then_inc(s["cT_ps"], 1)
            pe.wait_ge(s["xT"], 4)

            def z_columns(first, banks):
                for i in (first, first + 1):
                    piece_arrived(i)
                    w, c = stream[i % RING], PIECE * (i - first)
                    for t in range(TT):
                        for k in range(KT):
                            last = pe.matmul(B[banks[t]][:, c:c + PIECE], xnT[:, k, P * t:P * t + P],
                                             w[:, k, :], start=(k == 0), stop=(k == KT - 1))
                    last.then_inc(piece_used, 1)

            z_columns(0, (0, 1))
            z_columns(2, (2, 3))
            pe.wait_ge(s["cT"], 1)
            z_columns(4, (4, 5))
            z_columns(6, (6, 7))


            def gate_tile(n):
                i = 8 + n // 2
                piece_arrived(i)
                if n < 2:
                    pe.wait_ge(s["u_sb"], n + 1)
                else:
                    pe.wait_ge(s["gate_sb"], n - 1)
                for k in range(KT):
                    last = pe.matmul(B[n % 2][:, 0:TOK], slot_of(i)[:, k, P * (n % 2):P * (n % 2) + P],
                                     xnT[:, k, :], start=(k == 0), stop=(k == KT - 1))
                last.then_inc(s["gate_ps"] if n % 2 == 0 else piece_used, 1)

            for n in (0, 1):
                gate_tile(n)
            pe.wait_ge(s["win_t"], 1)
            pe.wait_ge(s["qk_tm"], 4)
            pe.wait_ge(s["v_sb"], 2)
            for f in range(8):
                if f >= 4:
                    pe.wait_ge(s["wT_sb"], f - 3)
                transposes([(B[4 + f % 4][:, P * m:P * m + P], (WR, WI)[m % 2][:, 2 * f + m // 2, :])
                            for m in range(4)]).then_inc(s["wT_ps"], 1)
            pe.wait_ge(s["bb_rep"], 2)
            for f in range(8):
                if f < 4:
                    pe.wait_ge(s["wT_sb"], 5 + f)
                else:
                    pe.wait_ge(s["kk_sb"], f - 3)
                for gg in (2 * f, 2 * f + 1):
                    o = B[4 + f % 4][:, 256 * (gg % 2):256 * (gg % 2) + 256]
                    for n, (bb, cc) in enumerate(((bbR, CR), (bbI, CI))):
                        last = pe.matmul(o, bb[:, gg].rearrange("p s h -> p (s h)"),
                                         cc[:, gg, :, 0:P], start=(n == 0), stop=(n == 1))
                last.then_inc(s["kk_ps"], 1)
            pe.wait_ge(s["u_turn"], 1)
            pe.wait_ge(s["kk_sb"], 6)
            for r in range(8):
                last = transposes([(B[4 + r // 4][:, P * (r % 4):P * (r % 4) + P], uc2[:, r].rearrange("p s h -> p (s h)"))])
                if r % 4 == 3:
                    last.then_inc(s["U_ps"], 1)
            pe.wait_ge(s["U_sb"], 2)
            pe.wait_ge(s["kk_sb"], 8)
            for i in range(GG):
                slot, q = i // 4, i % 4
                for g2 in range(2):
                    g = 2 * i + g2
                    o = B[6 + slot // 2][32 * q:32 * q + 32, 256 * (slot % 2):256 * (slot % 2) + 256]\
                        .rearrange("p (r n) -> p r n", r=2)[:, :, 64 * g2:64 * g2 + 64]
                    last = pe.matmul(o, U[:, g % 8, g // 8, :], WIN_M[:, i, :, 64 * g2:64 * g2 + 64],
                                     start=True, stop=True, tile_position=(0, 32 * q))
                if i % 8 == 7:
                    last.then_inc(s["st_ps"], 1)

            pe.wait_ge(s["st_sb"], 2)
            for ri in range(2):
                transposes([(B[4 + ri][:, P * m:P * m + P], S_sb[:, m, ri, :]) for m in range(4)])\
                    .then_inc(s["sT_ps"], 1)
            for n in (2, 3, 4):
                gate_tile(n)
            pe.wait_ge(s["qk_tm"], 4)
            for n, src in enumerate((q_tm, k_tm)):
                for t in range(TT):
                    if n == 1:
                        pe.wait_ge(s["qkT"], t + 1)
                    transposes([(B[2 + t][:, P * h:P * h + P], src[:, t, P * h:P * h + P])
                                for h in range(HEADS)]).then_inc(s["qkT_ps"], 1)

            def chunk_outputs():
                pe.wait_ge(s["m_in"], 16 * L)
                for i in range(GG):
                    slot, q = i // 4, i % 4
                    o = B[6 + slot // 2][32 * q:32 * q + 32, 256 * (slot % 2):256 * (slot % 2) + 256]
                    pe.matmul(o, Spr[:, i, :], CR[:, i, :, H:H + P], start=True, stop=False,
                              skip_group_check=True)
                    pe.matmul(o, Spi[:, i, :], CI[:, i, :, H:H + P], start=False, stop=False,
                              skip_group_check=True)
                    for g2 in range(2):
                        g = 2 * i + g2
                        last = pe.matmul(o[:, P * g2:P * g2 + P], U[:, g % 8, g // 8, :], MM[:, g, :],
                                         start=False, stop=(g2 == 1), skip_group_check=True)
                    if i % 8 == 7:
                        last.then_inc(s["y_ps"], 1)

            def turn_y():
                pe.wait_ge(s["y_sb"], 4)
                for t in range(L):
                    last = transposes([(B[6 + t // 4][:, P * (t % 4):P * (t % 4) + P],
                                        Y_sb[:, t].rearrange("p a b h -> p (a b h)"))])
                    if t % 4 == 3:
                        last.then_inc(s["yT_ps"], 1)

            units = [(h, t) for h in range(HEADS) for t in range(TT)]

            def scores(u):
                h, t = units[u]
                if u < 2:
                    pe.wait_ge(s["qkT"], 4)
                else:
                    pe.wait_ge(s["w_sb"], u - 1)
                for sub in range(2):
                    last = pe.matmul(B[2 + u % 2][:, TOK * sub:TOK * sub + P * (t + 1)],
                                     qz[:, sub, h, P * t:P * t + P], kz[:, sub, h, 0:P * (t + 1)],
                                     start=True, stop=True)
                last.then_inc(s["score"], 1)

            def turn_w(u):
                h, t = units[u]
                pe.wait_ge(s["wt"], u + 1)
                transposes([(B[2 + u % 2][:, P * j:P * j + P], wmix[:, u % 2, P * j:P * j + P])
                            for j in range(t + 1)]).then_inc(s["w_ps"], 1)

            def values(u):
                h, t = units[u]
                pe.wait_ge(s["w_sb"], u + 1)
                if u == 0:
                    pe.wait_ge(s["s_prev"], 1)
                for j in range(t + 1):
                    last = pe.matmul(B[4 + h // 2][:, TOK * (h % 2) + P * t:TOK * (h % 2) + P * t + P],
                                     v_tm[:, j, P * h:P * h + P], wTs[:, u % 2, j, :],
                                     start=(j == 0), stop=(j == t))
                last.then_inc(s["oT_ps"], 1)

            def glu():
                pe.wait_ge(s["wg"], 1)
                pe.wait_ge(s["yT"], 2)
                for q2 in range(4):
                    for q in range(4):
                        last = pe.matmul(B[q2 // 2][:, TOK * (q2 % 2):TOK * (q2 % 2) + TOK],
                                         wg[:, q, q2, :],
                                         yT[:, q, :], start=(q == 0), stop=(q == 3))
                    if q2 == 1:
                        last.then_inc(s["glu_ps"], 1)
                last.then_inc(piece_used, 1)

            for h in range(HEADS):
                scores(2 * h)
                scores(2 * h + 1)
                gate_tile(3 * h + 5)
                gate_tile(3 * h + 6)
                turn_w(2 * h)
                turn_w(2 * h + 1)
                if h < HEADS - 1:
                    gate_tile(3 * h + 7)
                values(2 * h)
                values(2 * h + 1)
                if h == 1:
                    chunk_outputs()
                elif h == 2:
                    turn_y()
            pe.wait_ge(s["w_sb"], 8)
            for m in range(2):
                pe.wait_ge(s["o_sq"], m + 1)
                pe.matmul(B[2 + m][:, :], ones, o2[:, 2 * m:2 * m + 2, :],
                          start=True, stop=True).then_inc(s["o_ms"], 1)
            pe.wait_ge(s["gate_sb"], 16)
            glu()
            for n in range(KT):
                if n % 4 == 0:
                    piece_arrived(17 + n // 4)
                if n == 0:
                    pe.wait_ge(s["glu_s"], 4)
                if n == 4:
                    pe.wait_ge(s["o_read"], 2)
                for q in range(4):
                    if n == 0 and q % 2 == 0:
                        pe.wait_ge(s["yg"], q // 2 + 1)
                    last = pe.matmul(B[n // 2][:, TOK * (n % 2):TOK * (n % 2) + TOK],
                                     pv(17 + n // 4)[:, q, P * (n % 4):P * (n % 4) + P], yg[:, q, :],
                                     start=(q == 0), stop=(q == 3))
                if n % 4 == 3:
                    last.then_inc(piece_used, 1)
                elif n % 2 == 1:
                    last.then_inc(s["ps_ssm"], 1)
            pe.wait_ge(s["oT"], 1)
            for n in range(KT):
                if n % 4 == 0:
                    piece_arrived(19 + n // 4)
                for q in range(4):
                    last = pe.matmul(B[4 + n // 2][:, TOK * (n % 2):TOK * (n % 2) + TOK],
                                     pv(19 + n // 4)[:, q, P * (n % 4):P * (n % 4) + P], oT[:, q, :],
                                     start=(q == 0), stop=(q == 3))
                if n % 4 == 3:
                    last.then_inc(piece_used, 1)
                elif n % 2 == 1:
                    last.then_inc(s["ps_att"], 1)
            pe.wait_ge(s["mixed"], 4)

            def up_bias(b):
                pe.wait_ge(bup_in, 16 * b + 16)
                for n in range(2):
                    for h in range(2):
                        last = pe.matmul(B[n][64 * h:64 * h + 64, :], e0,
                                         bup[:, D * h + 512 * n:D * h + 512 * n + 512],
                                         start=True, stop=False, skip_group_check=True)
                last.then_inc(s["bup_used"], 1)

            def turn_h(t):
                for half in range(2):
                    pe.wait_ge(s["hn"], 2 * t + half + 1)
                    if t == 1:
                        pe.wait_ge(s["hT"], half + 1)
                    transposes([(B[4 + half][:, P * k:P * k + P],
                                 hn[:, t, P * (4 * half + k):P * (4 * half + k) + P]) for k in range(4)])\
                        .then_inc(s["hT_ps"], 1)

            def logits(t):
                pe.wait_ge(s["wr_in"], 32)
                for k in range(KT):
                    if k % 4 == 0:
                        pe.wait_ge(s["hT"], 2 * t + k // 4 + 1)
                    last = pe.matmul(B[6 + t][:, 0:LC], hT[:, k, P * t:P * t + P], wr[:, k, :],
                                     start=(k == 0), stop=(k == KT - 1))
                last.then_inc(s["lg_ps"], 1)

            for t in range(TT):
                for i in range(21, PIECES):
                    piece_arrived(i)
                    c = i - 21
                    for k in range(KT):
                        last = pe.matmul(B[2 * t + c // 2][:, PIECE * (c % 2):PIECE * (c % 2) + PIECE],
                                         mixT[:, k, P * t:P * t + P], slot_of(i)[:, k, :],
                                         start=(k == 0), stop=(k == KT - 1))
                    if c % 2 == 1:
                        last.then_inc(s["out_ps"], 1)
                    if t == 1 and c == 1:
                        turn_h(0)
                    if t == 1 and c == 2:
                        logits(0)
            turn_h(1)
            logits(1)
            pe.wait_ge(s["h"], 2)
            up_bias(0)
            pe.wait_ge(s["routed"], 1)
            o = B[6][:, 0:LC]
            pe.matmul(o, ltri, R1, start=True, stop=False)
            pe.matmul(o, ones, R2, start=False, stop=True).then_inc(s["rk_ps"], 1)

            def gather(nth, turned=None):
                pe.wait_ge(s["sel"], nth)
                for k in range(KT):
                    if k == 4 and turned is not None:
                        pe.wait_ge(s["swT"], turned)
                    for t in range(TT):
                        last = pe.matmul(B[2 + k // 4][:, P * (k % 4):P * (k % 4) + P],
                                         hn[:, t, P * k:P * k + P], selg[:, t, :],
                                         start=(t == 0), stop=(t == TT - 1))
                    if k % 4 == 3:
                        last.then_inc(s["xg_ps"], 1)

            def scatter(last=False):
                for t in range(TT):
                    for n, sw in enumerate((swT0, swT1)):
                        product = pe.matmul(B[4 + 2 * t + n][:, :], sw[:, t, :], y_s, start=False, stop=last,
                                            skip_group_check=True)
                        if last:
                            product.then_inc(s["summed"], 1)

            def turn_weights():
                pe.wait_ge(s["gw"], 1)
                transposes([(B[3][0:E, P * t:P * t + P], gw[:, t, :]) for t in range(TT)]).then_inc(s["gT_ps"], 1)

            def weighted_biases():
                pe.wait_ge(s["gT"], 1)
                pe.wait_ge(s["bd_in"], 16)
                for t in range(TT):
                    for n in range(2):
                        last = pe.matmul(B[4 + 2 * t + n][:, :], gwT[:, P * t:P * t + P],
                                         bdn[:, 512 * n:512 * n + 512], start=True, stop=False,
                                         skip_group_check=True)
                last.then_inc(s["bias_ps"], 1)

            def expert_block(b, parity, first=False, last_block=False):
                if not first:
                    pe.wait_ge(s["glu_sb"], b)
                    up_bias(b)
                pe.wait_ge(s["xg"], 2 * b + 2)
                if first:
                    turn_weights()
                order = ORDER_0 if first else ORDER
                for k in order:
                    if k < SHARED:
                        pe.wait_ge(up_in[parity][k], 16 * b + 16)
                    else:
                        pe.wait_ge(up_in[parity][k], 16 * b + (16 if parity else 32))
                    for n in range(2):
                        for h in range(2):
                            last = pe.matmul(B[n][64 * h:64 * h + 64, :], xg[:, k, :],
                                             up_w[parity][k][h][:, 512 * n:512 * n + 512],
                                             start=False, stop=(k == order[-1]), skip_group_check=True)
                    last.then_inc(s["up_used"], 1)
                if first:
                    weighted_biases()
                else:
                    pe.wait_ge(s["ysb"], b)
                    scatter()
                pe.wait_ge(s["dsel"], b + 1)
                transposes([(B[3][:, P * t:P * t + P], selw[:, t, :]) for t in range(TT)])\
                    .then_inc(s["swt_ps"], 1)
                if not last_block:
                    gather(b + 2, b + 1)
                pe.wait_ge(s["act"], b + 1)
                if not last_block:
                    pe.wait_ge(s["xg"], 2 * b + 3)
                transposes([(B[2][:, P * j:P * j + P], act_s[:, P * j:P * j + P]) for j in range(4)])\
                    .then_inc(s["aT2_ps"], 1)
                pe.wait_ge(s["aT2"], b + 1)
                if last_block:
                    pe.wait_ge(s["swT"], b + 1)
                else:
                    pe.wait_ge(s["xg"], 2 * b + 4)
                for k in range(KT):
                    if k % 2 == 0:
                        pe.wait_ge(dn_in[parity][k // 2], 8 * b + (8 if parity else 16))
                    for n in range(2):
                        last = pe.matmul(B[3][64 * n:64 * n + 64, :], actT[:, k % 4, k // 4, :],
                                         dn_w[parity][k // 2][:, k % 2, 512 * n:512 * n + 512],
                                         start=(k == 0), stop=(k == KT - 1), skip_group_check=True)
                    if k % 2 == 1:
                        last.then_inc(s["dn_used"], 1)

            pe.wait_ge(s["rank"], 1)
            gather(1)
            expert_block(0, 0, first=True)
            pe.wait_ge(s["table_in"], 16)
            fourth_last = pe.value_load(table_row[0:1, 2:3], min_val=E - 4, max_val=E + EXTRA - 3)
            last_b = fourth_last + 3
            with pe.Fori(1, last_b, 2) as b:
                expert_block(b, 1)
                expert_block(b + 1, 0)
            expert_block(last_b, 1, last_block=True)
            pe.wait_ge(s["ysb"], fourth_last + 4)
            scatter(last=True)

        @block.scalar
        def _(act):
            act.wait_ge(s["warm"], 1)
            act.activation(warm, warm, ACT.Sqrt)
            for t in range(TT):
                act.wait_ge(x_in[t], 16)
                act.activation(xn[:, t, :], hx[:, t, :], ACT.Square, accum_out=xs[:, t:t + 1])\
                    .then_inc(s["x_sq"], 1)
                act.wait_ge(s["x_var"], t + 1)
                act.activation(xr[:, t:t + 1], xs[:, t:t + 1], ACT.Sqrt).then_inc(s["x_rs"], 1)
            act.wait_ge(s["a_in"], 48)
            act.activation(dts[0:GG], dts[0:GG], ACT.Exp).then_inc(s["dt"], 1)
            act.wait_ge(s["trig"], 1)
            act.activation(mg[:, 0, :], pa[:, 2, :], ACT.Exp)
            act.activation(mg[:, 1, :], pa[:, 2, :], ACT.Exp, scale=float(L))
            act.activation(tr[:, 3, :], tr[:, 2, :], ACT.Sin)
            act.activation(tr[:, 4, :], tr[:, 1, :], ACT.Sin).then_inc(s["sincos"], 1)
            for t in range(TT):
                act.wait_ge(piece_used, 2)
                act.activation(u_tm[:, t, :], B[t][:, :], ACT.Copy).then_inc(s["u_sb"], 1)
            act.wait_ge(s["lam_e"], 1)
            act.activation(lamv[:, 0:2], lamv[:, 2:4], ACT.Exp).then_inc(s["lam_n"], 1)
            for n, dst in enumerate((q_tm, k_tm)):
                act.wait_ge(piece_used, 4 + 2 * n)
                for t in range(TT):
                    act.activation(dst[:, t, :], B[2 + 2 * n + t][:, :], ACT.Square)\
                        .then_inc(s["q_sq"], 1)
            act.wait_ge(piece_used, 8)
            for t in range(TT):
                act.activation(v_tm[:, t, :], B[6 + t][:, :], ACT.Copy).then_inc(s["v_sb"], 1)
            act.wait_ge(s["qk_var"], 1)
            act.activation(qv, qv, ACT.Sqrt).then_inc(s["qk_rs"], 1)
            act.wait_ge(s["vec_in"], 16 * 10)

            def gate(n):
                if n % 2 == 0:
                    act.wait_ge(s["gate_ps"], n // 2 + 1)
                else:
                    act.wait_ge(piece_used, 9 + n // 2)
                act.activation(gates[:, n, :], B[n % 2][:, 0:TOK],
                               ACT.Sigmoid, bias=bgate[:, n:n + 1]).then_inc(s["gate_sb"], 1)

            for n in range(2):
                gate(n)
            for f in range(8):
                act.wait_ge(s["wT_ps"], f + 1)
                act.activation(WIN_M[:, 2 * f:2 * f + 2].rearrange("p a b c -> p (a b c)"),
                               B[4 + f % 4][:, :], ACT.Copy).then_inc(s["wT_sb"], 1)
            act.wait_ge(s["u_back"], 64)
            act.activation(uc2.rearrange("p r s h -> p s r h"), uc.rearrange("p s (r h) -> p s r h", h=H),
                           ACT.Copy).then_inc(s["u_turn"], 1)
            for f in range(8):
                act.wait_ge(s["kk_ps"], f + 1)
                act.activation(KK[:, 4 * f:4 * f + 4].rearrange("p a b -> p (a b)"),
                               B[4 + f % 4][:, :], ACT.Copy).then_inc(s["kk_sb"], 1)
            for m in range(2):
                act.wait_ge(s["U_ps"], m + 1)
                act.activation(U[:, 4 * m:4 * m + 4].rearrange("p a b c -> p (a b c)"),
                               B[4 + m][:, :], ACT.Copy).then_inc(s["U_sb"], 1)
            for m in range(2):
                act.wait_ge(s["st_ps"], m + 1)
                act.activation(S_sb[:, 2 * m:2 * m + 2].rearrange("p a b c -> p (a b c)"),
                               B[6 + m][:, :], ACT.Copy).then_inc(s["st_sb"], 1)
            for n in (2, 3, 4):
                gate(n)

            def chunk_outputs():
                for m in range(2):
                    act.wait_ge(s["y_ps"], m + 1)
                    for i in range(2):
                        act.activation(Y_sb[:, :, 2 * m + i].rearrange("p t g h -> p g t h"),
                                       B[6 + m][:, 256 * i:256 * i + 256]
                                       .rearrange("p (g t h) -> p g t h", g=2, h=H),
                                       ACT.Copy).then_inc(s["y_sb"], 1)

            def gelu_squares():
                for m in range(2):
                    act.wait_ge(s["yT_ps"], m + 1)
                    act.wait_ge(s["qkT_ps"], 4)
                    act.activation(ge1[:, 4 * m:4 * m + 4].rearrange("p a b c -> p (a b c)"),
                                   B[6 + m][:, :], ACT.Square).then_inc(s["gelu_sq"], 1)

            def softmax(u):
                t = u % 2
                act.wait_ge(s["smax"], u + 1)
                if u < 2:
                    act.wait_ge(s["kk_ps"], 8)
                else:
                    act.wait_ge(s["wt"], u - 1)
                for sub in range(2):
                    act.activation(probs(u, sub), B[2 + u % 2][:, TOK * sub:TOK * sub + P * (t + 1)], ACT.Exp,
                                   bias=nmx[:, u % 2, sub:sub + 1], scale=SUB ** -0.5,
                                   accum_out=rsum[:, u % 2, sub:sub + 1]).then_inc(s["prob"], 1)

            def turned(u):
                t = u % 2
                act.wait_ge(s["w_ps"], u + 1)
                if u >= 2:
                    act.wait_ge(s["oT_ps"], u - 1)
                act.activation(wTs[:, u % 2, 0:t + 1, :].rearrange("p a b -> p (a b)"),
                               B[2 + u % 2][:, 0:P * (t + 1)], ACT.Copy).then_inc(s["w_sb"], 1)

            def turned_w_glu():
                act.wait_ge(s["y_ps"], 2)
                act.wait_ge(slot_in[16 % RING], 16 * sum(len(piece(j)) for j in range(16 % RING, 17, RING)))
                for q in range(4):
                    last = act.activation(wg[:, q].rearrange("p c (t r) -> p c t r", t=4),
                                          pv(16)[:, q, :].rearrange("p (t c r) -> p c t r", t=4, c=4), ACT.Copy)
                last.then_inc(s["wg"], 1)

            def gelu_sigmoid():
                for m in range(2):
                    act.wait_ge(s["gelu_w"], m + 1)
                    act.activation(ge2[:, 4 * m:4 * m + 4].rearrange("p a b c -> p (a b c)"),
                                   ge1[:, 4 * m:4 * m + 4].rearrange("p a b c -> p (a b c)"),
                                   ACT.Sigmoid, scale=2 * math.sqrt(2 / math.pi)).then_inc(s["gelu_s"], 1)

            def squares(m):
                act.wait_ge(s["oT_ps"], 4 * m + 4)
                act.wait_ge(s["s_prev"], 1)
                act.activation(o2[:, 2 * m:2 * m + 2, :].rearrange("p a b -> p (a b)"), B[4 + m][:, :],
                               ACT.Square).then_inc(s["o_sq"], 1)

            def glu_sigmoid():
                for q in range(4):
                    if q == 0:
                        act.wait_ge(s["glu_ps"], 1)
                    if q == 2:
                        act.wait_ge(piece_used, 17)
                    act.activation(yg[:, q, :], B[q // 2][:, TOK * (q % 2):TOK * (q % 2) + TOK],
                                   ACT.Sigmoid, bias=bglu[:, q:q + 1]).then_inc(s["glu_s"], 1)

            for h in range(HEADS):
                softmax(2 * h)
                softmax(2 * h + 1)
                if h == 2:
                    squares(0)
                elif h == 3:
                    turned_w_glu()
                gate(3 * h + 5)
                gate(3 * h + 6)
                turned(2 * h)
                turned(2 * h + 1)
                if h < HEADS - 1:
                    gate(3 * h + 7)
                if h == 1:
                    chunk_outputs()
                elif h == 2:
                    gelu_squares()
            gelu_sigmoid()
            squares(1)
            glu_sigmoid()
            act.wait_ge(s["o_var"], 1)
            act.activation(o_rs, o_rs, ACT.Sqrt).then_inc(s["o_rs"], 1)
            for t in range(TT):
                for half in range(2):
                    act.wait_ge(s["h"], 2 * t + half + 1)
                    act.activation(hn[:, t, 512 * half:512 * half + 512], hx[:, t, 512 * half:512 * half + 512],
                                   ACT.Square, accum_out=xs2[:, t, half:half + 1]).then_inc(s["h_sq"], 1)
                act.wait_ge(s["h_var"], t + 1)
                act.activation(xr[:, t:t + 1], xs[:, t:t + 1], ACT.Sqrt).then_inc(s["h_rs"], 1)
                for half in range(2):
                    act.wait_ge(s["hT_ps"], 2 * t + half + 1)
                    act.activation(hT[:, 4 * half:4 * half + 4, P * t:P * t + P],
                                   B[4 + half][:, :].rearrange("p (k n) -> p k n", k=4),
                                   ACT.Copy).then_inc(s["hT"], 1)
            act.wait_ge(s["top_e"], 1)
            for t in range(TT):
                act.activation(top_w[:, t, 0:TOPK], top_v[:, t, 0:TOPK], ACT.Exp,
                               bias=xs[:, t:t + 1], accum_out=xr[:, t:t + 1]).then_inc(s["top_x"], 1)

            def gathered(nth):
                for n in range(2):
                    act.wait_ge(s["xg_ps"], 2 * nth - 1 + n)
                    act.activation(xg[:, 4 * n:4 * n + 4, :],
                                   B[2 + n][:, :].rearrange("p (k c) -> p k c", k=4)[:, :, 0:SLOTS],
                                   ACT.Copy).then_inc(s["xg"], 1)

            def expert_block(b, last_block=False):
                act.wait_ge(s["glu_sb"], b + 1)
                act.activation(sig_t, glu_t, ACT.Sigmoid, scale=ALPHA).then_inc(s["sig"], 1)
                act.wait_ge(s["swt_ps"], b + 1)
                act.activation(swT0[0:64].rearrange("p a b -> p (a b)"), B[3][0:64, 0:2 * P], ACT.Copy)
                act.activation(swT1[64:P].rearrange("p a b -> p (a b)"), B[3][64:P, 0:2 * P], ACT.Copy)\
                    .then_inc(s["swT"], 1)
                if not last_block:
                    gathered(b + 2)
                act.wait_ge(s["aT2_ps"], b + 1)
                act.activation(actT.rearrange("p a b c -> p (a b c)"), B[2][:, :], ACT.Copy)\
                    .then_inc(s["aT2"], 1)
                act.wait_ge(s["dn_used"], 4 * b + 4)
                act.activation(y_s, B[3][:, :], ACT.Copy).then_inc(s["ysb"], 1)

            act.wait_ge(s["loop_z"], 1)
            gathered(1)
            expert_block(0)
            act.wait_ge(s["table_in"], 16)
            fourth_last = act.value_load(table_row[0:1, 2:3], min_val=E - 4, max_val=E + EXTRA - 3)
            last_b = fourth_last + 3
            with act.Fori(1, last_b) as b:
                expert_block(b)
            expert_block(last_b, last_block=True)

        @block.vector
        def _(dve):
            steps = [0]

            def link(ins):
                steps[0] += 1
                ins.then_inc(s["dve_step"], 1)
                dve.wait_ge(s["dve_step"], steps[0])

            TTo, TS, STT = dve.tensor_tensor, dve.tensor_scalar, dve.scalar_tensor_tensor

            for t in range(TT):
                x_rms = xs[:, t:t + 1]
                dve.wait_ge(s["x_sq"], t + 1)
                link(TS(x_rms, x_rms, 1.0 / D, EPS, ALU.mult, ALU.add))
                dve.reciprocal(x_rms, x_rms).then_inc(s["x_var"], 1)
                dve.wait_ge(s["x_rs"], t + 1)
                TS(xn[:, t, :], hx[:, t, :], xr[:, t:t + 1], None, ALU.mult).then_inc(s["xn"], 1)
            dve.wait_ge(s["g1_in"], 16)
            for t in range(TT):
                for half in range(2):
                    dve.wait_ge(s["xT_ps"], 2 * t + half + 1)
                    TTo(xnT[:, 4 * half:4 * half + 4, P * t:P * t + P],
                        B[2 * t + half][:, :].rearrange("p (k n) -> p k n", k=4),
                        g1[:, 4 * half:4 * half + 4].unsqueeze(2).to_broadcast([P, 4, P]), ALU.mult)\
                        .then_inc(s["xT"], 1)
            dve.wait_ge(s["dt"], 1)
            dtb = dts[0:GG].unsqueeze(2).to_broadcast([GG, 2, PS])
            for i in range(2):
                last = TTo(natA[0:GG, 2 + i, :].rearrange("p (t n) -> p t n", t=2),
                           natA[0:GG, i, :].rearrange("p (t n) -> p t n", t=2), dtb, ALU.mult)
            last.then_inc(s["aT_in"], 1)
            dve.wait_ge(s["aT_ps"], 1)
            link(dve.tensor_copy(pa.rearrange("p a b -> p (a b)"), B[4][:, 0:4 * GG]))
            kk, r, rc = tr[:, 0, :], tr[:, 1, :], tr[:, 2, :]
            sn, cs = tr[:, 4, :], tr[:, 3, :]
            link(TS(kk, pa[:, 3, :], 1 / (2 * math.pi), ROUND, ALU.mult, ALU.add))
            link(TS(kk, kk, ROUND, None, ALU.subtract))
            link(STT(r, kk, -TWO_PI_1, pa[:, 3, :], ALU.mult, ALU.add))
            link(STT(r, kk, -TWO_PI_2, r, ALU.mult, ALU.add))
            link(STT(r, kk, -TWO_PI_3, r, ALU.mult, ALU.add))
            link(TS(r, r, 3.1415925, -3.1415925, ALU.min, ALU.max))
            link(TS(rc, r, -1.0, None, ALU.mult))
            link(TTo(rc, rc, r, ALU.max))
            TS(rc, rc, -1.0, math.pi / 2, ALU.mult, ALU.add).then_inc(s["trig"], 1)
            for ri, dst in enumerate((cTr, cTi)):
                dve.wait_ge(s["cT_ps"], ri + 1)
                v = B[5 + ri][:, :].rearrange("p (g t h) -> p g t h", t=2, h=H)
                for t in range(2):
                    last = dve.tensor_copy(dst[64 * t:64 * t + 64], v[64 * t:64 * t + 64, :, t, :])
            last.then_inc(s["cT"], 1)
            dve.wait_ge(s["cT"], 1)

            def cmul(outr, outi, ar, ai, br, bi, shape):
                n = 1
                for d in shape:
                    n *= d
                t = []
                for v in (sc1, sc2, sc3, sc4):
                    v = v.rearrange("p a b -> p (a b)")[:, 0:n]
                    t.append(v if len(shape) == 1 else v.rearrange("p (a b) -> p a b", a=shape[0]))
                TTo(t[0], ar, br, ALU.mult)
                TTo(t[1], ai, bi, ALU.mult)
                TTo(t[2], ar, bi, ALU.mult)
                link(TTo(t[3], ai, br, ALU.mult))
                TTo(outr, t[0], t[1], ALU.subtract)
                link(TTo(outi, t[2], t[3], ALU.add))

            def per_pair(v, n):
                return v.unsqueeze(2).to_broadcast([P, GG, n])

            dve.wait_ge(s["sincos"], 1)
            dve.memset(Pr[:, :, 0], 1.0)
            dve.memset(Pi[:, :, 0], 0.0)
            TTo(Pr[:, :, 1], mg[:, 0, :], cs, ALU.mult)
            link(TTo(Pi[:, :, 1], mg[:, 0, :], sn, ALU.mult))
            for n in (1, 2, 4):
                cmul(Pr[:, :, n + 1:2 * n + 1], Pi[:, :, n + 1:2 * n + 1], Pr[:, :, 1:n + 1], Pi[:, :, 1:n + 1],
                     per_pair(Pr[:, :, n], n), per_pair(Pi[:, :, n], n), (GG, n))
            for t in range(L):
                dve.tensor_copy(Vr[:, :, t], Pr[:, :, L - 1 - t])
                last = dve.tensor_copy(Vi[:, :, t], Pi[:, :, L - 1 - t])
            link(last)
            lr, li = pa[:, 0, :], pa[:, 1, :]
            t0, t1, t2, t3, t4, t5 = t16
            TTo(t0, lr, lr, ALU.mult)
            TTo(t1, li, li, ALU.mult)
            link(TS(t2, Pr[:, :, 1], 1.0, None, ALU.subtract))
            link(TTo(t0, t0, t1, ALU.add))
            TTo(t1, t2, lr, ALU.mult)
            TTo(t3, Pi[:, :, 1], li, ALU.mult)
            TTo(t4, Pi[:, :, 1], lr, ALU.mult)
            link(TTo(t5, t2, li, ALU.mult))
            dve.reciprocal(t0, t0)
            TTo(t1, t1, t3, ALU.add)
            link(TTo(t4, t4, t5, ALU.subtract))
            TTo(cfr, t1, t0, ALU.mult)
            link(TTo(cfi, t4, t0, ALU.mult))
            dve.wait_ge(s["b_in"], 32)
            cmul(bbr, bbi, br_raw, bi_raw, per_pair(cfr, H), per_pair(cfi, H), (GG, H))

            dve.wait_ge(s["cp_zero"], 1)

            def four(v, n, e):
                return v.unsqueeze(2).to_broadcast([P, GG, n, H]) if e else \
                    v.unsqueeze(3).to_broadcast([P, GG, n, H])

            CRv, CIv = [v.rearrange("p g t (e h) -> p g t e h", h=H) for v in (CR, CI)]
            TTo(tA, four(Pr, 9, 0), four(cTr, 9, 1), ALU.mult)
            link(TTo(tB, four(Pi, 9, 0), four(cTi, 9, 1), ALU.mult))
            for t in range(2):
                o = slice(64 * t, 64 * t + 64)
                last = TTo(CRv[o, :, t], tA[o], tB[o], ALU.subtract)
            link(last)
            TTo(tA, four(Pr, 9, 0), four(cTi, 9, 1), ALU.mult)
            link(TTo(tB, four(Pi, 9, 0), four(cTr, 9, 1), ALU.mult))
            for t in range(2):
                o = slice(64 * t, 64 * t + 64)
                last = STT(CIv[o, :, t], tA[o], -1.0, tB[o], ALU.mult, ALU.subtract)
            last.then_inc(s["cp_ready"], 1)
            dve.wait_ge(s["cp_ready"], 1)
            WRv, WIv = [v.rearrange("p g (e h) -> p g e h", h=H) for v in (WR, WI)]
            tAw, tBw = tA[:, :, 0:L], tB[:, :, 0:L]
            TTo(tAw, four(Vr, L, 0), four(bbr, L, 1), ALU.mult)
            link(TTo(tBw, four(Vi, L, 0), four(bbi, L, 1), ALU.mult))
            link(TTo(WRv, tAw, tBw, ALU.subtract))
            TTo(tAw, four(Vr, L, 0), four(bbi, L, 1), ALU.mult)
            link(TTo(tBw, four(Vi, L, 0), four(bbr, L, 1), ALU.mult))
            TTo(WIv, tAw, tBw, ALU.add).then_inc(s["win_t"], 1)
            dve.wait_ge(s["lam_in"], 64)
            for i in range(2):
                last = dve.tensor_tensor_reduce(lamrow[:, 2 * i, :], lamrow[:, 2 * i, :],
                                                lamrow[:, 2 * i + 1, :], 1.0, 0.0, ALU.mult, ALU.add,
                                                lamv[:, 2 + i:3 + i])
            last.then_inc(s["lam_e"], 1)
            dve.wait_ge(s["q_sq"], 4)
            for n, src in enumerate((q_tm, k_tm)):
                last = dve.tensor_reduce(qv[:, n].rearrange("p t g -> p (t g)"),
                                         src.rearrange("p t (g d) -> p (t g) d", d=SUB), AX, ALU.add)
            link(last)
            link(TS(qv, qv, 1.0 / SUB, EPS, ALU.mult, ALU.add))
            dve.reciprocal(qv, qv).then_inc(s["qk_var"], 1)
            dve.wait_ge(s["qk_rs"], 1)
            for n, dst in enumerate((q_tm, k_tm)):
                for t in range(TT):
                    TTo(dst[:, t, :].rearrange("p (g d) -> p g d", d=SUB),
                        B[2 + 2 * n + t][:, :].rearrange("p (g d) -> p g d", d=SUB),
                        qv[:, n, t, :].unsqueeze(2).to_broadcast([P, 8, SUB]), ALU.mult)\
                        .then_inc(s["qk_tm"], 1)
            dve.wait_ge(s["lam_n"], 1)
            link(TTo(lamv[:, 4:5], lamv[:, 1:2], lamv[:, 0:1], ALU.subtract))
            link(TS(lamv[:, 4:5], lamv[:, 4:5], LAMBDA_INIT, None, ALU.subtract))
            link(dve.tensor_copy(e8r, cs))
            link(dve.tensor_copy(e8i, sn))
            for _ in range(3):
                cmul(t16[0], t16[1], e8r, e8i, e8r, e8i, (GG,))
                dve.tensor_copy(e8r, t16[0])
                link(dve.tensor_copy(e8i, t16[1]))
            dve.memset(Rr[:, :, 0], 1.0)
            dve.memset(Ri[:, :, 0], 0.0)
            dve.tensor_copy(Rr[:, :, 1], e8r)
            link(dve.tensor_copy(Ri[:, :, 1], e8i))
            for n in (1, 2, 4, 8, 15):
                cmul(Rr[:, :, n + 1:2 * n + 1], Ri[:, :, n + 1:2 * n + 1], Rr[:, :, 1:n + 1], Ri[:, :, 1:n + 1],
                     per_pair(Rr[:, :, n], n), per_pair(Ri[:, :, n], n), (GG, n))
            cmul(Rr[:, :, 31:32], Ri[:, :, 31:32], Rr[:, :, 30:31], Ri[:, :, 30:31],
                 Rr[:, :, 1:2], Ri[:, :, 1:2], (GG, 1))
            dve.tensor_copy(magz, per_pair(mg[:, 1, :], NC)).then_inc(s["turns"], 1)
            dve.wait_ge(s["ident"], 1)
            link(dve.tensor_reduce(hsel, ident.rearrange("p (k h) -> p h k", h=H), AX, ALU.add))
            link(dve.memset(magz[:, :, 0], 0.0))
            dve.wait_ge(s["d_in"], 16)
            link(TTo(dd, dB, hsel.unsqueeze(1).to_broadcast([P, G, H]), ALU.mult))
            dve.wait_ge(s["kk_sb"], 8)
            TTo(KK[:, :, 0:H], KK[:, :, 0:H], dd, ALU.add).then_inc(s["kk_d"], 1)
            dve.wait_ge(s["kk_d"], 1)
            dve.wait_ge(s["sT_ps"], 2)
            Ir, Ii = [B[4 + n][:, :].rearrange("p (g c) -> p g c", c=NC) for n in range(2)]
            i0, i1, i2, i3 = [It[:, n] for n in range(4)]
            TTo(i0, Ir, Rr, ALU.mult)
            TTo(i1, Ii, Ri, ALU.mult)
            TTo(i2, Ii, Rr, ALU.mult)
            link(TTo(i3, Ir, Ri, ALU.mult))
            TTo(i0, i0, i1, ALU.add)
            link(TTo(i2, i2, i3, ALU.subtract))
            flat = lambda v: v.rearrange("p g c -> p (g c)")
            dve.tensor_tensor_scan(flat(i1), flat(magz), flat(i0), 0.0, ALU.mult, ALU.add)
            link(dve.tensor_tensor_scan(flat(i3), flat(magz), flat(i2), 0.0, ALU.mult, ALU.add))
            dve.memset(Spr[:, :, 0], 0.0)
            dve.memset(Spi[:, :, 0], 0.0)
            w = slice(0, NC - 1)
            TTo(i0[:, :, w], i1[:, :, w], Rr[:, :, w], ALU.mult)
            link(TTo(i2[:, :, w], i3[:, :, w], Ri[:, :, w], ALU.mult))
            link(TTo(Spr[:, :, 1:], i0[:, :, w], i2[:, :, w], ALU.subtract))
            TTo(i0[:, :, w], i3[:, :, w], Rr[:, :, w], ALU.mult)
            link(TTo(i2[:, :, w], i1[:, :, w], Ri[:, :, w], ALU.mult))
            TTo(Spi[:, :, 1:], i0[:, :, w], i2[:, :, w], ALU.add).then_inc(s["s_prev"], 1)
            dve.wait_ge(s["kz_fill"], 2)
            dve.wait_ge(s["vec_in"], 16 * 10)
            for n, (dst, gain) in enumerate(((qz, qg), (kz, kg))):
                for t in range(TT):
                    dve.wait_ge(s["qkT_ps"], 2 * n + t + 1)
                    for sub in range(2):
                        o = slice(64 * sub, 64 * sub + 64)
                        last = TS(dst[o, sub, :, P * t:P * t + P],
                                  B[2 + t][o, :].rearrange("p (h q) -> p h q", h=HEADS),
                                  gain[o], None, ALU.mult)
                    last.then_inc(s["qkT"], 1)

            def row_max(u):
                t = u % 2
                dve.wait_ge(s["score"], u + 1)
                if u >= 2:
                    dve.wait_ge(s["prob"], 2 * (u - 1))
                link(dve.tensor_reduce(smx[:, u % 2, :], B[2 + u % 2][:, :].rearrange("p (s k) -> p s k", s=2)
                                       [:, :, 0:P * (t + 1)], AX, ALU.max))
                TS(nmx[:, u % 2, :], smx[:, u % 2, :], -SUB ** -0.5, None, ALU.mult).then_inc(s["smax"], 1)

            def difference(u):
                t = u % 2
                dve.wait_ge(s["prob"], 2 * u + 2)
                link(dve.reciprocal(rinv[:, u % 2, :], rsum[:, u % 2, :]))
                link(TTo(rinv[:, u % 2, 1:2], rinv[:, u % 2, 1:2], lamv[:, 4:5], ALU.mult))
                if u >= 2:
                    dve.wait_ge(s["w_ps"], u - 1)
                wu = wmix[:, u % 2, 0:P * (t + 1)]
                link(TS(wu, probs(u, 1), rinv[:, u % 2, 1:2], None, ALU.mult))
                STT(wu, probs(u, 0), rinv[:, u % 2, 0:1], wu, ALU.mult, ALU.add).then_inc(s["wt"], 1)

            for h in range(HEADS):
                row_max(2 * h)
                row_max(2 * h + 1)
                difference(2 * h)
                difference(2 * h + 1)
            for m in range(2):
                dve.wait_ge(s["gelu_sq"], m + 1)
                o = slice(4 * m, 4 * m + 4)
                y = B[6 + m][:, :].rearrange("p (t q c) -> p t q c", t=4, q=4)
                link(TS(ge1[:, o], ge1[:, o], 0.044715, 1.0, ALU.mult, ALU.add))
                TTo(ge1[:, o], ge1[:, o], y, ALU.mult).then_inc(s["gelu_w"], 1)
            for m in range(2):
                dve.wait_ge(s["gelu_s"], m + 1)
                y = B[6 + m][:, :].rearrange("p (t q c) -> p t q c", t=4, q=4)
                for t in range(4):
                    last = TTo(yT.rearrange("p q (c t) -> p t q c", t=L)[:, 4 * m + t],
                               y[:, t], ge2[:, 4 * m + t], ALU.mult)
                last.then_inc(s["yT"], 1)

            dve.wait_ge(s["yT"], 2)
            for m in range(2):
                dve.wait_ge(s["glu_s"], 2 * m + 2)
                TTo(yg[:, 2 * m:2 * m + 2], yT[:, 2 * m:2 * m + 2], yg[:, 2 * m:2 * m + 2], ALU.mult)\
                    .then_inc(s["yg"], 1)
            for m in range(2):
                dve.wait_ge(s["o_ms"], m + 1)
                TS(o_rs[:, 2 * m:2 * m + 2, :].rearrange("p a b -> p (a b)"), B[2 + m][:, :],
                   1.0 / P, EPS, ALU.mult, ALU.add).then_inc(s["o_read"], 1)
            dve.wait_ge(s["o_read"], 2)
            dve.reciprocal(o_rs, o_rs).then_inc(s["o_var"], 1)
            link(TS(lamv[:, 5:6], subg, 1.0 - LAMBDA_INIT, None, ALU.mult))
            dve.wait_ge(s["o_rs"], 1)
            for m in range(2):
                last = STT(oT[:, 2 * m:2 * m + 2, :].rearrange("p a b -> p (a b)"), B[4 + m][:, :],
                           lamv[:, 5:6], o_rs[:, 2 * m:2 * m + 2, :].rearrange("p a b -> p (a b)"),
                           ALU.mult, ALU.mult)
            last.then_inc(s["oT"], 1)
            gf = gates.rearrange("p n t -> p (n t)")
            mf = mixT.rearrange("p n t -> p (n t)")
            for f in range(4):
                if f % 2 == 0:
                    dve.wait_ge(s["ps_ssm"], f // 2 + 1)
                else:
                    dve.wait_ge(piece_used, 18 + f // 2)
                last = TTo(mf[:, 512 * f:512 * f + 512], B[f][:, :], gf[:, 512 * f:512 * f + 512], ALU.mult)
            link(last)
            for f in range(4):
                if f % 2 == 0:
                    dve.wait_ge(s["ps_att"], f // 2 + 1)
                else:
                    dve.wait_ge(piece_used, 20 + f // 2)
                m = mtmp[:, f % 2, :]
                link(TTo(m, B[4 + f][:, :], gf[:, 2048 + 512 * f:2048 + 512 * f + 512], ALU.mult))
                TTo(mf[:, 512 * f:512 * f + 512], mf[:, 512 * f:512 * f + 512], m, ALU.add)\
                    .then_inc(s["mixed"], 1)
            dve.wait_ge(s["g2_in"], 16)
            dve.wait_ge(s["wr_in"], 32)

            def h_of(t):
                for n in range(2):
                    dve.wait_ge(s["out_ps"], 2 * t + n + 1)
                    TTo(hx[:, t, 512 * n:512 * n + 512], hx[:, t, 512 * n:512 * n + 512],
                        B[2 * t + n][:, :], ALU.add).then_inc(s["h"], 1)
                dve.wait_ge(s["h_sq"], 2 * t + 2)
                link(TTo(xs[:, t:t + 1], xs2[:, t, 0:1], xs2[:, t, 1:2], ALU.add))
                link(TS(xs[:, t:t + 1], xs[:, t:t + 1], 1.0 / D, EPS, ALU.mult, ALU.add))
                dve.reciprocal(xs[:, t:t + 1], xs[:, t:t + 1]).then_inc(s["h_var"], 1)
                dve.wait_ge(s["h_rs"], t + 1)
                for n in range(2):
                    o = slice(512 * n, 512 * n + 512)
                    STT(hn[:, t, o], hx[:, t, o], xr[:, t:t + 1], g2b[:, o], ALU.mult, ALU.mult)\
                        .then_inc(s["hn"], 1)

            def best_of(t):
                dve.wait_ge(s["lg_ps"], t + 1)
                link(TTo(lg[:, t, :], B[6 + t][:, 0:E], brb, ALU.add))
                link(dve.max(top_v[:, t, :], lg[:, t, :]))
                link(dve.max_index(top_i[:, t, :], top_v[:, t, :], lg[:, t, :]))
                link(dve.tensor_copy(top_f[:, t, :], top_i[:, t, :]))
                link(TTo(one_k[:, t], iota[:, 0:E].unsqueeze(2).to_broadcast([P, E, TOPK]),
                         top_f[:, t, 0:TOPK].unsqueeze(1).to_broadcast([P, E, TOPK]), ALU.is_equal))
                link(dve.tensor_reduce(R1[:, E * t:E * t + E], one_k[:, t], AX, ALU.add))

            h_of(0)
            best_of(0)
            link(dve.tensor_copy(R2[:, E:2 * E], R1[:, 0:E]))
            h_of(1)
            best_of(1)
            TTo(R2[:, 2 * E:], R1[:, 0:E], R1[:, E:2 * E], ALU.add).then_inc(s["routed"], 1)
            TS(xs, top_v[:, :, 0], -1.0, None, ALU.mult).then_inc(s["top_e"], 1)
            dve.wait_ge(s["rk_ps"], 1)
            o = B[6][:, 0:LC]
            link(STT(rank.rearrange("p t e -> p (t e)"), o[:, 0:TT * E], 1.0, R1[:, 0:TT * E],
                     ALU.add, ALU.mult))
            link(dve.tensor_copy(cnt, o[:, 2 * E:]))
            TS(rank, rank, 1.0, None, ALU.subtract).then_inc(s["rank"], 1)
            dve.wait_ge(s["rank"], 1)

            def one_hot(dst, e, first, weighted):
                for t in range(TT):
                    last = TS(dst[:, t, :].rearrange("p (d n) -> p d n", d=2),
                              iota[:, bass.ds(first, SLOTS)].unsqueeze(1).to_broadcast([P, 2, SLOTS]),
                              rank[:, t, bass.ds(e, 1)], gw[:, t, bass.ds(e, 1)] if weighted else None,
                              ALU.is_equal, *((ALU.mult,) if weighted else ()))
                return last

            def expert_block(b, this, after):
                dve.wait_ge(s["xg_ps"], 2 * b + 2)
                if this is not None:
                    one_hot(selw, *this, True).then_inc(s["dsel"], 1)
                if after is not None:
                    one_hot(selg, *after, False).then_inc(s["sel"], 1)
                dve.wait_ge(s["up_used"], KT * b + KT)
                for n in range(2):
                    v = B[n][:, :].rearrange("p (j two) -> p two j", two=2)
                    TS(glu_t[:, 256 * n:256 * n + 256], v[:, 0, :], LIMIT, None, ALU.min)
                    last = TS(lin_t[:, 256 * n:256 * n + 256], v[:, 1, :], LIMIT, -LIMIT, ALU.min, ALU.max)
                last.then_inc(s["glu_sb"], 1)
                dve.wait_ge(s["glu_sb"], b + 1)
                STT(lin_t, lin_t, 1.0, glu_t, ALU.add, ALU.mult).then_inc(s["gated"], 1)
                dve.wait_ge(s["gated"], b + 1)
                dve.wait_ge(s["sig"], b + 1)
                TTo(act_s, lin_t, sig_t, ALU.mult).then_inc(s["act"], 1)

            one_hot(selg, 0, 0, False).then_inc(s["sel"], 1)
            dve.wait_ge(s["top_x"], 2)
            link(dve.reciprocal(xr, xr))
            for t in range(TT):
                last = TS(top_w[:, t, 0:TOPK], top_w[:, t, 0:TOPK], xr[:, t:t + 1], None, ALU.mult)
            link(last)
            for t in range(TT):
                last = TTo(gw_k[:, t], one_k[:, t], top_w[:, t, 0:TOPK].unsqueeze(1).to_broadcast([P, E, TOPK]),
                           ALU.mult)
            link(last)
            dve.tensor_reduce(gw, gw_k, AX, ALU.add).then_inc(s["gw"], 1)
            dve.wait_ge(s["gw"], 1)
            one_hot(selw, 0, 0, True).then_inc(s["dsel"], 1)
            link(TS(ovf, cnt, float(SLOTS), None, ALU.is_gt))
            link(STT(ovf, cnt, 2.0 * SLOTS, ovf, ALU.is_gt, ALU.add))
            link(STT(ovf, cnt, 3.0 * SLOTS, ovf, ALU.is_gt, ALU.add))
            link(dve.tensor_tensor_scan(cum, ones[:, 0:E], ovf, 0.0, ALU.mult, ALU.add))
            link(TS(before, cum, iop, None, ALU.is_le))
            dve.tensor_reduce(tabf[:, 0:1], before, AX, ALU.add)
            link(TTo(ovt, before, ovf, ALU.mult))
            link(dve.tensor_reduce(tabf[:, 1:2], ovt, AX, ALU.add))
            link(TS(tabf[:, 3:4], iop, 0.0, None, ALU.is_lt))
            link(TS(tabf[:, 4:5], iop, float(E), tabf[:, 3:4], ALU.add, ALU.mult))
            link(TTo(tabf[:, 0:1], tabf[:, 0:1], tabf[:, 4:5], ALU.add))
            link(TS(tabf[:, 5:6], tabf[:, 0:1], float(E), 4.0 * SLOTS, ALU.is_ge, ALU.mult))
            link(TS(tabf[:, 0:1], tabf[:, 0:1], float(E - 1), None, ALU.min))
            link(TTo(tabf[:, 1:2], iop, tabf[:, 1:2], ALU.subtract))
            link(TS(tabf[:, 1:2], tabf[:, 1:2], 1.0, float(SLOTS), ALU.add, ALU.mult))
            link(TS(tabf[:, 3:4], tabf[:, 3:4], -1.0, 1.0, ALU.mult, ALU.add))
            link(TTo(tabf[:, 1:2], tabf[:, 1:2], tabf[:, 3:4], ALU.mult))
            link(TS(tabf[:, 1:2], tabf[:, 1:2], 0.0, 3.0 * SLOTS, ALU.max, ALU.min))
            link(TTo(tabf[:, 1:2], tabf[:, 1:2], tabf[:, 5:6], ALU.max))
            link(TS(tabf[:, 2:3], cum[:, E - 1:E], 0.5, 0.5 * E + 0.25, ALU.mult, ALU.add))
            link(TS(tabf[:, 2:3], tabf[:, 2:3], ROUND, None, ALU.add))
            link(TS(tabf[:, 2:3], tabf[:, 2:3], ROUND, 2.0, ALU.subtract, ALU.mult))
            link(TS(tabf[:, 2:3], tabf[:, 2:3], 4.0, None, ALU.subtract))
            dve.tensor_copy(table_i[:, 0:3], tabf[:, 0:3]).then_inc(s["table"], 1)
            dve.wait_ge(s["loop_z"], 1)
            dve.wait_ge(s["gT_ps"], 1)
            dve.tensor_copy(gwT[0:E], B[3][0:E, 0:TOK]).then_inc(s["gT"], 1)
            expert_block(0, None, (1, 0))
            dve.wait_ge(s["table_in"], 16)
            fourth_last = dve.value_load(table_row[0:1, 2:3], min_val=E - 4, max_val=E + EXTRA - 3)
            last_b = fourth_last + 3

            def entry(b):
                return [dve.value_load(table_row[0:1, bass.ds(3 * b + n, 1)], min_val=0, max_val=m)
                        for n, m in ((0, E - 1), (1, 4 * SLOTS))]

            with dve.Fori(1, last_b) as b:
                expert_block(b, entry(b), entry(b + 1))
            expert_block(last_b, entry(last_b), None)
            for t in range(TT):
                for n in range(2):
                    dve.wait_ge(s["summed"], 2 * t + n + 1)
                    TTo(hx[:, t, 512 * n:512 * n + 512], hx[:, t, 512 * n:512 * n + 512],
                        B[4 + 2 * t + n][:, :], ALU.add).then_inc(s["fin"], 1)


_INS = ["x", "norm1_g", "w_in", "b_gate", "ssm_a_re", "ssm_a_im", "ssm_log_dt", "ssm_b_re", "ssm_b_im",
        "ssm_c_re", "ssm_c_im", "ssm_d", "ssm_w_glu", "ssm_b_glu", "q_norm_g", "k_norm_g", "lambda_q1",
        "lambda_k1", "lambda_q2", "lambda_k2", "subln_g", "w_proj_ssm", "w_proj_att", "w_out", "norm2_g",
        "w_router", "b_router", "w_up", "b_up", "w_down", "b_down"]


def kernel(**inputs):
    import numpy as np
    import concourse.bacc as bacc
    from concourse.bass_utils import run_bass_kernel_spmd

    nc = bacc.Bacc("TRN2", target_bir_lowering=False, num_devices=1)
    arrays, aps = {}, {}
    for name in _INS:
        v = np.ascontiguousarray(inputs[name])
        arrays[f"in_{name}"] = v
        aps[name] = nc.dram_tensor(f"in_{name}", v.shape, mybir.dt.from_np(v.dtype), kind="ExternalInput").ap()
    out = nc.dram_tensor("out_y", (1, TOK, D), F32, kind="ExternalOutput").ap()
    mixer_and_experts(nc, aps, out)
    r = run_bass_kernel_spmd(nc, [arrays], core_ids=[0])
    return r.results[0]["out_y"]
```
